# Optimizing a Trainium2 kernel written in Bass

```python
import jax, jax.numpy as jnp
from jax import lax
import numpy as np
import math

D_MODEL = 1024
BATCH = 1
SEQ = 256
DEPTH = 2

GRID_W = 64
ROPE_THETA = 10000.0
EPS = 1e-6
Q_BLOCK = 128

MLA_HEADS = 8
MLA_Q_LORA = 256
MLA_KV_LORA = 128
MLA_NOPE = 64
MLA_ROPE = 32
MLA_V = 64
MLA_QK = MLA_NOPE + MLA_ROPE

GQA_HEADS = 8
GQA_KV_HEADS = 2
GQA_HEAD_DIM = 64

POOL_WINDOWS = (2, 4, 8, 16)
POOL_GROUPS = 4
POOL_GROUP = 128
POOL_WIDTH = POOL_GROUPS * POOL_GROUP

N_BRANCH = 3
MLA_OUT = MLA_HEADS * MLA_V
GQA_OUT = GQA_HEADS * GQA_HEAD_DIM

D_FF = 2816
CONV_W = 3

IN_SIZES = (MLA_Q_LORA, MLA_KV_LORA, MLA_ROPE,
            GQA_HEADS * GQA_HEAD_DIM, GQA_KV_HEADS * GQA_HEAD_DIM, GQA_KV_HEADS * GQA_HEAD_DIM,
            POOL_WIDTH, N_BRANCH * D_MODEL)
IN_WIDTH = (MLA_Q_LORA + MLA_KV_LORA + MLA_ROPE
            + (GQA_HEADS + 2 * GQA_KV_HEADS) * GQA_HEAD_DIM
            + POOL_WIDTH + N_BRANCH * D_MODEL)


def rms_norm(x, g):
    xf = x.astype(jnp.float32)
    y = xf * lax.rsqrt(jnp.mean(xf * xf, axis=-1, keepdims=True) + EPS)
    return (y * g.astype(jnp.float32)).astype(x.dtype)

def split_columns(y, sizes):
    out, start = [], 0
    for n in sizes:
        out.append(y[..., start:start + n])
        start += n
    return out

def axial_rope_tables(seq_len, rot_dim):
    rows = seq_len // GRID_W
    row_idx = jnp.repeat(jnp.arange(rows, dtype=jnp.float32), GRID_W)
    col_idx = jnp.tile(jnp.arange(GRID_W, dtype=jnp.float32), rows)
    n_axis = rot_dim // 4
    inv_freq = ROPE_THETA ** (-jnp.arange(n_axis, dtype=jnp.float32) / n_axis)
    ang = jnp.concatenate([row_idx[:, None] * inv_freq, col_idx[:, None] * inv_freq], axis=-1)
    return jnp.cos(ang), jnp.sin(ang)

def apply_rope(x, cos, sin):
    half = x.shape[-1] // 2
    x1, x2 = x[..., :half], x[..., half:]
    c = cos[None, :, None, :].astype(x.dtype)
    s = sin[None, :, None, :].astype(x.dtype)
    return jnp.concatenate([x1 * c - x2 * s, x1 * s + x2 * c], axis=-1)

def block_attention(q, k, v):
    b, s, h, dk = q.shape
    g = k.shape[2]
    rep = h // g
    dv = v.shape[-1]
    scale = dk ** -0.5
    nb = s // Q_BLOCK
    qb = q.reshape(b, nb, Q_BLOCK, g, rep, dk).transpose(1, 0, 2, 3, 4, 5)

    def one_block(qi):
        sc = jnp.einsum('bqgrd,bkgd->bgrqk', qi, k, preferred_element_type=jnp.float32) * scale
        p = jax.nn.softmax(sc, axis=-1).astype(v.dtype)
        return jnp.einsum('bgrqk,bkgv->bqgrv', p, v)

    out = lax.map(one_block, qb)
    return out.transpose(1, 0, 2, 3, 4, 5).reshape(b, s, h, dv)

def mla_branch(c_q, c_kv, k_rope_raw, q_norm_g, w_uq, kv_norm_g, w_ukv, qh_g, kh_g, cos, sin):
    b, s, _ = c_q.shape
    q = (rms_norm(c_q, q_norm_g) @ w_uq).reshape(b, s, MLA_HEADS, MLA_QK)
    kv = (rms_norm(c_kv, kv_norm_g) @ w_ukv).reshape(b, s, MLA_HEADS, MLA_NOPE + MLA_V)
    k_nope, v = kv[..., :MLA_NOPE], kv[..., MLA_NOPE:]
    k_rope = jnp.broadcast_to(k_rope_raw[:, :, None, :], (b, s, MLA_HEADS, MLA_ROPE))
    k = jnp.concatenate([k_nope, k_rope], axis=-1)
    q = rms_norm(q, qh_g)
    k = rms_norm(k, kh_g)
    q = jnp.concatenate([q[..., :MLA_NOPE], apply_rope(q[..., MLA_NOPE:], cos, sin)], axis=-1)
    k = jnp.concatenate([k[..., :MLA_NOPE], apply_rope(k[..., MLA_NOPE:], cos, sin)], axis=-1)
    o = block_attention(q, k, v)
    return o.reshape(b, s, MLA_OUT)

def gqa_branch(q_raw, k_raw, v_raw, qn_g, kn_g, cos, sin):
    b, s, _ = q_raw.shape
    q = q_raw.reshape(b, s, GQA_HEADS, GQA_HEAD_DIM)
    k = k_raw.reshape(b, s, GQA_KV_HEADS, GQA_HEAD_DIM)
    v = v_raw.reshape(b, s, GQA_KV_HEADS, GQA_HEAD_DIM)
    q = apply_rope(rms_norm(q, qn_g), cos, sin)
    k = apply_rope(rms_norm(k, kn_g), cos, sin)
    o = block_attention(q, k, v)
    return o.reshape(b, s, GQA_OUT)

def pool_branch(p, w_pool, pool_scale):
    b, s, _ = p.shape
    pg = p.reshape(b, s, POOL_GROUPS, POOL_GROUP)
    pf = pg.astype(jnp.float32)
    csum = jnp.concatenate([jnp.zeros((b, 1, POOL_GROUPS, POOL_GROUP), jnp.float32),
                            jnp.cumsum(pf, axis=1)], axis=1)
    t = jnp.arange(s)
    means = []
    for gi, w in enumerate(POOL_WINDOWS):
        lo = jnp.clip(t - w // 2, 0, s)
        hi = jnp.clip(t + w - w // 2, 0, s)
        cg = csum[:, :, gi]
        total = jnp.take(cg, hi, axis=1) - jnp.take(cg, lo, axis=1)
        means.append(total / (hi - lo).astype(jnp.float32)[None, :, None])
    pooled = jnp.stack(means, axis=2)
    mixed = (pooled - pf).astype(p.dtype)
    y = jnp.einsum('bsgc,gcd->bsgd', mixed, w_pool).reshape(b, s, POOL_WIDTH)
    return y * pool_scale

def depthwise_conv(u, w, bias):
    c = u.shape[-1]
    y = lax.conv_general_dilated(u, w[:, None, :], window_strides=(1,),
                                 padding=[(CONV_W // 2, CONV_W // 2)],
                                 dimension_numbers=('NWC', 'WIO', 'NWC'),
                                 feature_group_count=c)
    return y + bias

def first_inputs(seed: int = 0) -> dict:
    key = jax.random.key(seed)
    ks = jax.random.split(key, 24)
    f32 = jnp.float32

    def dense(k, shape, fan_in):
        return jax.random.normal(k, shape, f32) * (fan_in ** -0.5)

    def gain(k, shape):
        return 1.0 + 0.1 * jax.random.normal(k, shape, f32)

    L = DEPTH
    conv_center = jnp.zeros((CONV_W, 1), f32).at[CONV_W // 2].set(1.0)
    return {
        'x': jax.random.normal(ks[0], (BATCH, SEQ, D_MODEL), f32),
        'attn_norm_g': gain(ks[1], (L, D_MODEL)),
        'w_in': dense(ks[2], (L, D_MODEL, IN_WIDTH), D_MODEL),
        'mla_q_norm_g': gain(ks[3], (L, MLA_Q_LORA)),
        'mla_w_uq': dense(ks[4], (L, MLA_Q_LORA, MLA_HEADS * MLA_QK), MLA_Q_LORA),
        'mla_kv_norm_g': gain(ks[5], (L, MLA_KV_LORA)),
        'mla_w_ukv': dense(ks[6], (L, MLA_KV_LORA, MLA_HEADS * (MLA_NOPE + MLA_V)), MLA_KV_LORA),
        'mla_q_head_g': gain(ks[7], (L, MLA_QK)),
        'mla_k_head_g': gain(ks[8], (L, MLA_QK)),
        'gqa_q_head_g': gain(ks[9], (L, GQA_HEAD_DIM)),
        'gqa_k_head_g': gain(ks[10], (L, GQA_HEAD_DIM)),
        'pool_w': dense(ks[11], (L, POOL_GROUPS, POOL_GROUP, POOL_GROUP), POOL_GROUP),
        'pool_scale': gain(ks[12], (L, POOL_WIDTH)),
        'w_branch_mla': dense(ks[13], (L, MLA_OUT, D_MODEL), MLA_OUT),
        'w_branch_gqa': dense(ks[14], (L, GQA_OUT, D_MODEL), GQA_OUT),
        'w_branch_pool': dense(ks[15], (L, POOL_WIDTH, D_MODEL), POOL_WIDTH),
        'w_out': dense(ks[16], (L, D_MODEL, D_MODEL), D_MODEL),
        'ffn_norm_g': gain(ks[17], (L, D_MODEL)),
        'ffn_w_up': dense(ks[18], (L, D_MODEL, 2 * D_FF), D_MODEL),
        'ffn_conv_w': conv_center[None] + 0.3 * jax.random.normal(ks[19], (L, CONV_W, 2 * D_FF), f32),
        'ffn_conv_b': 0.01 * jax.random.normal(ks[20], (L, 2 * D_FF), f32),
        'ffn_w_down': dense(ks[21], (L, D_FF, D_MODEL), D_FF),
    }

def first_block(x, attn_norm_g, w_in, mla_q_norm_g, mla_w_uq, mla_kv_norm_g, mla_w_ukv,
              mla_q_head_g, mla_k_head_g, gqa_q_head_g, gqa_k_head_g, pool_w, pool_scale,
              w_branch_mla, w_branch_gqa, w_branch_pool, w_out, ffn_norm_g, ffn_w_up,
              ffn_conv_w, ffn_conv_b, ffn_w_down):
    b, s, d = x.shape
    cos_m, sin_m = axial_rope_tables(s, MLA_ROPE)
    cos_g, sin_g = axial_rope_tables(s, GQA_HEAD_DIM)
    for l in range(DEPTH):
        h = rms_norm(x, attn_norm_g[l])
        proj = h @ w_in[l]
        c_q, c_kv, k_rope, gq, gk, gv, pool_in, gate_logits = split_columns(proj, IN_SIZES)
        o_mla = mla_branch(c_q, c_kv, k_rope, mla_q_norm_g[l], mla_w_uq[l], mla_kv_norm_g[l],
                           mla_w_ukv[l], mla_q_head_g[l], mla_k_head_g[l], cos_m, sin_m)
        o_gqa = gqa_branch(gq, gk, gv, gqa_q_head_g[l], gqa_k_head_g[l], cos_g, sin_g)
        o_pool = pool_branch(pool_in, pool_w[l], pool_scale[l])
        gates = jax.nn.sigmoid(gate_logits.astype(jnp.float32)).astype(x.dtype).reshape(b, s, N_BRANCH, d)
        merged = (gates[:, :, 0] * (o_mla @ w_branch_mla[l])
                  + gates[:, :, 1] * (o_gqa @ w_branch_gqa[l])
                  + gates[:, :, 2] * (o_pool @ w_branch_pool[l]))
        x = x + merged @ w_out[l]
        hf = rms_norm(x, ffn_norm_g[l])
        u = depthwise_conv(hf @ ffn_w_up[l], ffn_conv_w[l], ffn_conv_b[l])
        u_gate, u_val = u[..., :D_FF], u[..., D_FF:]
        x = x + (jax.nn.silu(u_gate) * u_val) @ ffn_w_down[l]
    return x


N_MIXERS = 4
HEAD_DIM = 64
N_HEADS = D_MODEL // HEAD_DIM
ROT_DIM = HEAD_DIM // 4
ROPE_THETA_2 = 500000.0
DIL_CONFIGS = ((128, 1), (512, 4), (2048, 16))
N_HEADS_DIL = 8
DIL_GROUP_WIDTH = N_HEADS_DIL * HEAD_DIM
DIL_IN_WIDTH = len(DIL_CONFIGS) * 3 * DIL_GROUP_WIDTH
IDX_HEADS = 8
IDX_DIM = 64
TOPK_TOKENS = 256
DSA_IN_WIDTH = 3 * D_MODEL + IDX_HEADS * IDX_DIM + IDX_DIM + IDX_HEADS
MOBA_BLOCK = 256
MOBA_TOPK = 3
MOBA_Q_CHUNK = 32
D_FF_2 = 4 * D_MODEL
PLE_DIM = 256


def _n_layers_of(mixer):
    return len(range(mixer, DEPTH, N_MIXERS))

def rms_norm_2(x, g):
    x32 = x.astype(jnp.float32)
    y = x32 * lax.rsqrt(jnp.mean(x32 * x32, axis=-1, keepdims=True) + EPS)
    return (y * g.astype(jnp.float32)).astype(x.dtype)

def rope_tables(positions):
    inv_freq = ROPE_THETA_2 ** (-jnp.arange(0, ROT_DIM, 2, dtype=jnp.float32) / ROT_DIM)
    ang = positions.astype(jnp.float32)[..., None] * inv_freq
    return jnp.cos(ang)[:, :, None, :], jnp.sin(ang)[:, :, None, :]

def apply_partial_rope(t, cos, sin):
    half = ROT_DIM // 2
    t1 = t[..., :half].astype(jnp.float32)
    t2 = t[..., half:ROT_DIM].astype(jnp.float32)
    rot = jnp.concatenate([t1 * cos - t2 * sin, t2 * cos + t1 * sin], axis=-1).astype(t.dtype)
    return jnp.concatenate([rot, t[..., ROT_DIM:]], axis=-1)

def stick_breaking_attention(x, w_in, w_out):
    B, S, _ = x.shape
    q, k, v = jnp.split(x @ w_in, 3, axis=-1)
    q = q.reshape(B, S, N_HEADS, HEAD_DIM)
    k = k.reshape(B, S, N_HEADS, HEAD_DIM)
    v = v.reshape(B, S, N_HEADS, HEAD_DIM)
    scale = HEAD_DIM ** -0.5
    outs = []
    for blk in range(S // Q_BLOCK):
        t0 = blk * Q_BLOCK
        L = t0 + Q_BLOCK
        z = jnp.einsum('bqhd,bkhd->bhqk', q[:, t0:L], k[:, :L]).astype(jnp.float32) * scale
        t_idx = t0 + jnp.arange(Q_BLOCK)[:, None]
        s_idx = jnp.arange(L)[None, :]
        past = s_idx < t_idx
        log_fail = jnp.where(past, jax.nn.log_sigmoid(-z), 0.0)
        later = lax.cumsum(log_fail, axis=3, reverse=True) - log_fail
        a = jnp.where(past, jnp.exp(jax.nn.log_sigmoid(z) + later), 0.0)
        outs.append(jnp.einsum('bhqk,bkhd->bqhd', a.astype(v.dtype), v[:, :L]))
    o = jnp.concatenate(outs, axis=1).reshape(B, S, N_HEADS * HEAD_DIM)
    return o @ w_out

def banded_attention(q, k, v, n_back):
    N, L, H, Dh = q.shape
    nb = L // Q_BLOCK
    qb = q.reshape(N, nb, Q_BLOCK, H, Dh)
    kb = k.reshape(N, nb, Q_BLOCK, H, Dh)
    vb = v.reshape(N, nb, Q_BLOCK, H, Dh)
    zero = jnp.zeros_like(kb[:, :1])
    k2 = jnp.concatenate([jnp.concatenate([zero, kb[:, :-1]], axis=1), kb], axis=2)
    v2 = jnp.concatenate([jnp.concatenate([zero, vb[:, :-1]], axis=1), vb], axis=2)
    s = jnp.einsum('nbqhd,nbkhd->nbhqk', qb, k2).astype(jnp.float32) * (Dh ** -0.5)
    dist = Q_BLOCK + jnp.arange(Q_BLOCK)[:, None] - jnp.arange(2 * Q_BLOCK)[None, :]
    band = (dist >= 0) & (dist <= n_back)
    first_pad = (jnp.arange(nb) == 0)[:, None, None] & (jnp.arange(2 * Q_BLOCK) < Q_BLOCK)[None, None, :]
    mask = band[None] & ~first_pad
    s = jnp.where(mask[None, :, None], s, -jnp.inf)
    lse = jax.nn.logsumexp(s, axis=-1)
    prob = jnp.exp(s - lse[..., None])
    o = jnp.einsum('nbhqk,nbkhd->nbqhd', prob.astype(v.dtype), v2)
    return o.reshape(N, L, H, Dh), lse.transpose(0, 1, 3, 2).reshape(N, L, H)

def dilated_attention(x, w_in, w_out, cos, sin):
    B, S, _ = x.shape
    H = N_HEADS_DIL
    G = len(DIL_CONFIGS)
    proj = (x @ w_in).reshape(B, S, G, 3, H, HEAD_DIM)
    outs, lses = [], []
    for g, (window, dil) in enumerate(DIL_CONFIGS):
        q = apply_partial_rope(proj[:, :, g, 0], cos, sin)
        k = apply_partial_rope(proj[:, :, g, 1], cos, sin)
        v = proj[:, :, g, 2]
        L = S // dil
        Lp = -(-L // Q_BLOCK) * Q_BLOCK

        def strided(t):
            t = t.reshape(B, L, dil, H, HEAD_DIM).transpose(0, 2, 1, 3, 4).reshape(B * dil, L, H, HEAD_DIM)
            return jnp.pad(t, ((0, 0), (0, Lp - L), (0, 0), (0, 0)))

        o, lse = banded_attention(strided(q), strided(k), strided(v), window // dil)
        o = o[:, :L].reshape(B, dil, L, H, HEAD_DIM).transpose(0, 2, 1, 3, 4).reshape(B, S, H, HEAD_DIM)
        lse = lse[:, :L].reshape(B, dil, L, H).transpose(0, 2, 1, 3).reshape(B, S, H)
        outs.append(o)
        lses.append(lse)
    alpha = jax.nn.softmax(jnp.stack(lses, axis=0), axis=0)
    o = jnp.einsum('gbsh,gbshd->bshd', alpha, jnp.stack(outs, axis=0).astype(jnp.float32)).astype(x.dtype)
    return o.reshape(B, S, H * HEAD_DIM) @ w_out

def dsa_attention(x, w_in, w_out, cos, sin):
    B, S, _ = x.shape
    D = N_HEADS * HEAD_DIM
    cuts = [D, 2 * D, 3 * D, 3 * D + IDX_HEADS * IDX_DIM, 3 * D + IDX_HEADS * IDX_DIM + IDX_DIM]
    q, k, v, qi, ki, wi = jnp.split(x @ w_in, cuts, axis=-1)
    q = apply_partial_rope(q.reshape(B, S, N_HEADS, HEAD_DIM), cos, sin)
    k = apply_partial_rope(k.reshape(B, S, N_HEADS, HEAD_DIM), cos, sin)
    v = v.reshape(B, S, N_HEADS, HEAD_DIM)
    qi = apply_partial_rope(qi.reshape(B, S, IDX_HEADS, IDX_DIM), cos, sin)
    ki = apply_partial_rope(ki.reshape(B, S, 1, IDX_DIM), cos, sin)[:, :, 0]
    wi = wi.astype(jnp.float32) * (IDX_HEADS ** -0.5)
    topk = min(TOPK_TOKENS, S // 4)
    scale = HEAD_DIM ** -0.5
    key_pos = jnp.arange(S)

    def block(bi):
        t0 = bi * Q_BLOCK
        t_pos = t0 + jnp.arange(Q_BLOCK)
        qb = lax.dynamic_slice_in_dim(q, t0, Q_BLOCK, axis=1)
        qib = lax.dynamic_slice_in_dim(qi, t0, Q_BLOCK, axis=1)
        wib = lax.dynamic_slice_in_dim(wi, t0, Q_BLOCK, axis=1)
        rel = jax.nn.relu(jnp.einsum('bqhd,bkd->bqhk', qib, ki).astype(jnp.float32))
        score = jnp.einsum('bqh,bqhk->bqk', wib, rel)
        causal = key_pos[None, :] <= t_pos[:, None]
        score = jnp.where(causal[None], score, -jnp.inf)
        _, idx = lax.top_k(score, topk)
        valid = idx <= t_pos[None, :, None]
        k_sel = jax.vmap(lambda kk, ii: kk[ii])(k, idx)
        v_sel = jax.vmap(lambda vv, ii: vv[ii])(v, idx)
        s = jnp.einsum('bqhd,bqkhd->bqhk', qb, k_sel).astype(jnp.float32) * scale
        s = jnp.where(valid[:, :, None, :], s, -jnp.inf)
        prob = jax.nn.softmax(s, axis=-1)
        return jnp.einsum('bqhk,bqkhd->bqhd', prob.astype(v.dtype), v_sel)

    o = lax.map(block, jnp.arange(S // Q_BLOCK))
    o = o.transpose(1, 0, 2, 3, 4).reshape(B, S, D)
    return o @ w_out

def moba_attention(x, w_in, w_out, cos, sin):
    B, S, _ = x.shape
    H = N_HEADS
    q, k, v = jnp.split(x @ w_in, 3, axis=-1)
    q = apply_partial_rope(q.reshape(B, S, H, HEAD_DIM), cos, sin)
    k = apply_partial_rope(k.reshape(B, S, H, HEAD_DIM), cos, sin)
    v = v.reshape(B, S, H, HEAD_DIM)
    nb = -(-S // MOBA_BLOCK)
    Sp = nb * MOBA_BLOCK
    pad = ((0, 0), (0, Sp - S), (0, 0), (0, 0))
    kb = jnp.pad(k, pad).reshape(B, nb, MOBA_BLOCK, H, HEAD_DIM).transpose(0, 3, 1, 2, 4)
    vb = jnp.pad(v, pad).reshape(B, nb, MOBA_BLOCK, H, HEAD_DIM).transpose(0, 3, 1, 2, 4)
    k_mean = jnp.mean(kb.astype(jnp.float32), axis=3)
    topk = min(MOBA_TOPK, nb - 1)
    scale = HEAD_DIM ** -0.5
    b_ix = jnp.arange(B)[:, None, None, None]
    h_ix = jnp.arange(H)[None, None, :, None]

    def chunk(ci):
        t0 = ci * MOBA_Q_CHUNK
        t_pos = t0 + jnp.arange(MOBA_Q_CHUNK)
        cur = t0 // MOBA_BLOCK
        qc = lax.dynamic_slice_in_dim(q, t0, MOBA_Q_CHUNK, axis=1)
        k_own = lax.dynamic_index_in_dim(kb, cur, axis=2, keepdims=False)
        v_own = lax.dynamic_index_in_dim(vb, cur, axis=2, keepdims=False)
        own_pos = cur * MOBA_BLOCK + jnp.arange(MOBA_BLOCK)
        s_own = jnp.einsum('bqhd,bhkd->bqhk', qc, k_own).astype(jnp.float32) * scale
        s_own = jnp.where((own_pos[None, :] <= t_pos[:, None])[None, :, None, :], s_own, -jnp.inf)
        if topk == 0:
            prob = jax.nn.softmax(s_own, axis=-1)
            return jnp.einsum('bqhk,bhkd->bqhd', prob.astype(v.dtype), v_own)
        gate = jnp.einsum('bqhd,bhnd->bqhn', qc.astype(jnp.float32), k_mean)
        gate = jnp.where(jnp.arange(nb) < cur, gate, -jnp.inf)
        _, sel = lax.top_k(gate, topk)
        valid = sel < cur
        k_sel = kb[b_ix, h_ix, sel]
        v_sel = vb[b_ix, h_ix, sel]
        s_sel = jnp.einsum('bqhd,bqhjkd->bqhjk', qc, k_sel).astype(jnp.float32) * scale
        s_sel = jnp.where(valid[..., None], s_sel, -jnp.inf).reshape(B, MOBA_Q_CHUNK, H, topk * MOBA_BLOCK)
        prob = jax.nn.softmax(jnp.concatenate([s_sel, s_own], axis=-1), axis=-1).astype(v.dtype)
        p_sel = prob[..., :topk * MOBA_BLOCK].reshape(B, MOBA_Q_CHUNK, H, topk, MOBA_BLOCK)
        p_own = prob[..., topk * MOBA_BLOCK:]
        return (jnp.einsum('bqhjk,bqhjkd->bqhd', p_sel, v_sel)
                + jnp.einsum('bqhk,bhkd->bqhd', p_own, v_own))

    o = lax.map(chunk, jnp.arange(S // MOBA_Q_CHUNK))
    o = o.transpose(1, 0, 2, 3, 4).reshape(B, S, H * HEAD_DIM)
    return o @ w_out

def second_inputs(seed: int = 0) -> dict:
    key = jax.random.key(seed)
    ks = iter(jax.random.split(key, 32))

    def dense(shape, fan_in):
        return jax.random.normal(next(ks), shape, jnp.float32) * (fan_in ** -0.5)

    def gain(shape):
        return 1.0 + 0.05 * jax.random.normal(next(ks), shape, jnp.float32)

    nA, nB, nC, nD = (_n_layers_of(m) for m in range(N_MIXERS))
    x = jax.random.normal(next(ks), (BATCH, SEQ, D_MODEL), jnp.float32)
    p = jax.random.normal(next(ks), (DEPTH, BATCH, SEQ, PLE_DIM), jnp.float32)
    offsets = jax.random.randint(next(ks), (BATCH, 1), 0, 4096, dtype=jnp.int32)
    positions = offsets + jnp.arange(SEQ, dtype=jnp.int32)[None, :]
    return {
        'x': x,
        'p': p,
        'positions': positions,
        'w_in_sb': dense((nA, D_MODEL, 3 * D_MODEL), D_MODEL),
        'w_out_sb': dense((nA, D_MODEL, D_MODEL), D_MODEL),
        'w_in_dil': dense((nB, D_MODEL, DIL_IN_WIDTH), D_MODEL),
        'w_out_dil': dense((nB, DIL_GROUP_WIDTH, D_MODEL), DIL_GROUP_WIDTH),
        'w_in_dsa': dense((nC, D_MODEL, DSA_IN_WIDTH), D_MODEL),
        'w_out_dsa': dense((nC, D_MODEL, D_MODEL), D_MODEL),
        'w_in_moba': dense((nD, D_MODEL, 3 * D_MODEL), D_MODEL),
        'w_out_moba': dense((nD, D_MODEL, D_MODEL), D_MODEL),
        'g_mix_pre': gain((DEPTH, D_MODEL)),
        'g_mix_post': gain((DEPTH, D_MODEL)),
        'g_ffn_pre': gain((DEPTH, D_MODEL)),
        'g_ffn_post': gain((DEPTH, D_MODEL)),
        'w_ff_in': dense((DEPTH, D_MODEL, D_FF_2), D_MODEL),
        'w_ff_out': dense((DEPTH, D_FF_2, D_MODEL), D_FF_2),
        'g_ple': gain((DEPTH, D_MODEL)),
        'w_ple_gate': dense((DEPTH, D_MODEL, D_MODEL), D_MODEL),
        'w_ple': dense((DEPTH, PLE_DIM, D_MODEL), PLE_DIM),
    }

def second_block(x, p, positions, w_in_sb, w_out_sb, w_in_dil, w_out_dil, w_in_dsa, w_out_dsa,
              w_in_moba, w_out_moba, g_mix_pre, g_mix_post, g_ffn_pre, g_ffn_post,
              w_ff_in, w_ff_out, g_ple, w_ple_gate, w_ple):
    cos, sin = rope_tables(positions)
    h = x
    for i in range(DEPTH):
        mixer, j = i % N_MIXERS, i // N_MIXERS
        u = rms_norm_2(h, g_mix_pre[i])
        if mixer == 0:
            y = stick_breaking_attention(u, w_in_sb[j], w_out_sb[j])
        elif mixer == 1:
            y = dilated_attention(u, w_in_dil[j], w_out_dil[j], cos, sin)
        elif mixer == 2:
            y = dsa_attention(u, w_in_dsa[j], w_out_dsa[j], cos, sin)
        else:
            y = moba_attention(u, w_in_moba[j], w_out_moba[j], cos, sin)
        h = h + rms_norm_2(y, g_mix_post[i])
        u = rms_norm_2(h, g_ffn_pre[i])
        f = jnp.square(jax.nn.relu(u @ w_ff_in[i])) @ w_ff_out[i]
        h = h + rms_norm_2(f, g_ffn_post[i])
        gate = jax.nn.sigmoid(rms_norm_2(h, g_ple[i]) @ w_ple_gate[i])
        h = h + (p[i] @ w_ple[i]) * gate
    return h


def setup_inputs(seed=0):
    out = dict(first_inputs(seed))
    for name, value in second_inputs(seed + 1).items():
        if name != "x":
            out[name + "_2"] = value
    return out


def reference(
    x, attn_norm_g, w_in, mla_q_norm_g, mla_w_uq, mla_kv_norm_g, mla_w_ukv, mla_q_head_g,
    mla_k_head_g, gqa_q_head_g, gqa_k_head_g, pool_w, pool_scale, w_branch_mla, w_branch_gqa,
    w_branch_pool, w_out, ffn_norm_g, ffn_w_up, ffn_conv_w, ffn_conv_b, ffn_w_down, p_2,
    positions_2, w_in_sb_2, w_out_sb_2, w_in_dil_2, w_out_dil_2, w_in_dsa_2, w_out_dsa_2,
    w_in_moba_2, w_out_moba_2, g_mix_pre_2, g_mix_post_2, g_ffn_pre_2, g_ffn_post_2, w_ff_in_2,
    w_ff_out_2, g_ple_2, w_ple_gate_2, w_ple_2,
):
    x = first_block(
        x, attn_norm_g, w_in, mla_q_norm_g, mla_w_uq, mla_kv_norm_g, mla_w_ukv, mla_q_head_g,
        mla_k_head_g, gqa_q_head_g, gqa_k_head_g, pool_w, pool_scale, w_branch_mla,
        w_branch_gqa, w_branch_pool, w_out, ffn_norm_g, ffn_w_up, ffn_conv_w, ffn_conv_b,
        ffn_w_down,
    )
    return second_block(
        x, p_2, positions_2, w_in_sb_2, w_out_sb_2, w_in_dil_2, w_out_dil_2, w_in_dsa_2,
        w_out_dsa_2, w_in_moba_2, w_out_moba_2, g_mix_pre_2, g_mix_post_2, g_ffn_pre_2,
        g_ffn_post_2, w_ff_in_2, w_ff_out_2, g_ple_2, w_ple_gate_2, w_ple_2,
    )


_drawn_inputs = setup_inputs


def setup_inputs(seed=0):
    import zlib

    import numpy as np

    out = dict(_drawn_inputs(seed))
    spreads = {}
    factors = {'mla_q_norm_g': 5.753,
     'mla_kv_norm_g': 3.21,
     'mla_q_head_g': 5.183,
     'mla_k_head_g': 4.9,
     'gqa_q_head_g': 5.758,
     'gqa_k_head_g': 5.49,
     'ffn_conv_b': 4.636,
     'g_ple_2': 30.18}
    for name, (base, spread) in spreads.items():
        noise = np.random.default_rng([zlib.crc32(name.encode()), seed]).standard_normal(out[name].shape)
        drawn = base * np.exp(spread * noise) if base else spread * noise
        out[name] = __import__('jax').numpy.asarray(drawn.astype(out[name].dtype))
    for name, factor in factors.items():
        out[name] = (out[name] * factor).astype(out[name].dtype)
    return out
```

```python
from contextlib import ExitStack

import numpy as np

import concourse.bass as bass
from concourse import mybir

F32 = mybir.dt.float32
F32R = mybir.dt.float32r
I32 = mybir.dt.int32
ALU = mybir.AluOpType
ACT = mybir.ActivationFunctionType
AXIS_X = mybir.AxisListType.X

P = 128
SEQ = 256
TT = SEQ // P
D = 1024
DK = D // P
DEPTH = 2
EPS = 1e-6

MLA_H, Q_LORA, KV_LORA, NOPE, ROPE, MLA_V = 8, 256, 128, 64, 32, 64
MLA_QK = NOPE + ROPE
GQA_H, GQA_KV, HD = 8, 2, 64
POOL_WINDOWS = (2, 4, 8, 16)
POOL_G, POOL_W = 4, 512
D_FF = 2816
FT = D_FF // P
D_FF_2 = 4096
SB_H = 16
DIL = (1, 4, 16)
DIL_H, DIL_W = 8, 512
DIL_ROT = 16
PLE = 256
GRID_W = 64

PANEL = 512
UNIT = 1024
SPLIT_SLOTS = 4
RAW_SLOTS = 4
SPLIT_AHEAD = SPLIT_SLOTS - 1
MASKED = -1.0e30
POOL_PAD = max(POOL_WINDOWS) // 2



def panels_of(first, last, width=PANEL):
    return [(c, min(c + width, last)) for c in range(first, last, width)]


def weight_plan():
    plan = []
    c_mla = Q_LORA + KV_LORA + ROPE
    c_gqa = c_mla + (GQA_H + 2 * GQA_KV) * HD
    c_pool = c_gqa + POOL_W
    for l in range(DEPTH):
        plan += [
            ("proj", l, "w_in", D, [(0, c_mla)] + panels_of(c_mla, c_gqa) + [(c_gqa, c_pool)]),
            ("up_q", l, "mla_w_uq", Q_LORA, panels_of(0, MLA_H * MLA_QK)),
            ("up_kv", l, "mla_w_ukv", KV_LORA, panels_of(0, MLA_H * (NOPE + MLA_V))),
            ("gates", l, "w_in", D, panels_of(c_pool, c_pool + 3 * D)),
            ("branch_mla", l, "w_branch_mla", MLA_H * MLA_V, panels_of(0, D)),
            ("branch_gqa", l, "w_branch_gqa", GQA_H * HD, panels_of(0, D)),
            ("branch_pool", l, "w_branch_pool", POOL_W, panels_of(0, D)),
            ("out", l, "w_out", D, panels_of(0, D)),
            ("ffn_up", l, "ffn_w_up", D, [p for c0, c1 in panels_of(0, D_FF)
                                          for p in ((c0, c1), (D_FF + c0, D_FF + c1))]),
            ("ffn_down", l, "ffn_w_down", D_FF, panels_of(0, D)),
        ]
    for l in range(DEPTH):
        if l == 0:
            plan += [("sb_in", 0, "w_in_sb_2", D, panels_of(0, 3 * D)),
                     ("sb_out", 0, "w_out_sb_2", D, panels_of(0, D))]
        else:
            plan += [("dil_in", 0, "w_in_dil_2", D, panels_of(0, len(DIL) * 3 * DIL_W)),
                     ("dil_out", 0, "w_out_dil_2", DIL_W, panels_of(0, D))]
        plan += [("ff_in", l, "w_ff_in_2", D, panels_of(0, D_FF_2)),
                 ("ff_out", l, "w_ff_out_2", D_FF_2, panels_of(0, D)),
                 ("ple_up", l, "w_ple_2", PLE, panels_of(0, D)),
                 ("ple_gate", l, "w_ple_gate_2", D, panels_of(0, D))]
    return plan


def weight_units():
    units, loads, at = [], [], 0
    for name, layer, source, rows, panels in weight_plan():
        kts = rows // P
        own = []
        for n, (c0, c1) in enumerate(panels):
            w = c1 - c0
            step = max(1, min(kts, UNIT // w))
            for k0 in range(0, kts, step):
                own.append(dict(name=name, layer=layer, source=source, panel=n, c0=c0, w=w, k0=k0,
                                nk=min(step, kts - k0)))
        for i in range(0, len(own), 2):
            pair = own[i:i + 2]
            size = sum(u["w"] * u["nk"] for u in pair)
            inside = 0
            for u in pair:
                u["load"], u["inside"] = len(loads), inside
                inside += u["w"] * u["nk"]
            loads.append((at, size))
            at += P * size
        units += own
    return units, loads, at


FIRST_COLS, _n = {}, 0
for _name, _w in (("attn_g", DK), ("q_lora_g", 2), ("kv_lora_g", 1), ("q_head_g", 1), ("k_head_g", 1),
                  ("pool_scale", POOL_G), ("ffn_g", DK), ("conv_w", 3 * 2 * FT), ("conv_b", 2 * FT)):
    FIRST_COLS[_name] = (_n, _n + _w)
    _n += _w
N_FIRST_COLS = _n
SECOND_COLS, _n = {}, 0
for _name, _w in (("mix_g", DK), ("ffn_g", DK), ("ple_g", DK)):
    SECOND_COLS[_name] = (_n, _n + _w)
    _n += _w
N_SECOND_COLS = _n
ROW_QM, ROW_KM, ROW_QG, ROW_KG = (0, 32), (32, 64), (64, 128), (128, 192)
N_ROWS = 192

CONSTS, _n = {}, 0
for _name, _w in (("ident", P), ("not_below", P), ("ones", P), ("cos_m", TT * ROPE // 2),
                  ("sin_m", TT * ROPE // 2), ("cos_g", TT * HD // 2), ("sin_g", TT * HD // 2),
                  ("inv_freq", DIL_ROT // 2), ("sb_neg", 3 * P), ("sb_add", 3 * P),
                  ("dil_add", 9 * P), ("pool_edge", POOL_G * 2 * POOL_PAD)):
    CONSTS[_name] = (_n, _n + _w)
    _n += _w
N_CONSTS = _n


def constants():
    c = np.zeros((P, N_CONSTS), np.float32)

    def put(name, value):
        a, b = CONSTS[name]
        c[:, a:b] = np.asarray(value, np.float32).reshape(P, b - a)

    i = np.arange(P)
    put("ident", np.eye(P))
    put("not_below", i[:, None] >= i[None, :])
    put("ones", np.ones((P, P)))
    row, col = np.arange(SEQ) // GRID_W, np.arange(SEQ) % GRID_W
    for tag, rot in (("m", ROPE), ("g", HD)):
        n = rot // 4
        inv = (10000.0 ** (-np.arange(n) / n)).astype(np.float32)
        angle = np.concatenate([row[:, None].astype(np.float32) * inv, col[:, None].astype(np.float32) * inv], 1)
        for fn, f in (("cos_", np.cos), ("sin_", np.sin)):
            table = f(angle.astype(np.float64))
            put(fn + tag, table.reshape(TT, P, rot // 2).transpose(1, 0, 2))
    put("inv_freq", np.tile(500000.0 ** (-np.arange(0, DIL_ROT, 2) / DIL_ROT), (P, 1)))
    past = np.concatenate([i[:, None] < np.arange(SEQ)[None, :], i[:, None] < i[None, :]], 1)
    put("sb_neg", np.where(past, -1.0, 0.0))
    put("sb_add", np.where(past, 0.0, MASKED))
    parts = []
    for keys, q0 in ((P, 0), (SEQ, P)):
        for dil in DIL:
            dist = q0 + i[:, None] - np.arange(keys)[None, :]
            ok = (dist >= 0) & (dist % dil == 0) & (dist // dil <= P)
            parts.append(np.where(ok, 0.0, MASKED))
    put("dil_add", np.concatenate(parts, 1))
    t = np.concatenate([np.arange(POOL_PAD), np.arange(SEQ - POOL_PAD, SEQ)])
    edges = [w / (np.clip(t + w - w // 2, 0, SEQ) - np.clip(t - w // 2, 0, SEQ)) for w in POOL_WINDOWS]
    put("pool_edge", np.tile(np.concatenate(edges), (P, 1)))
    return c



class Engine:

    def __init__(self, done):
        self.done, self.count, self.steps, self.waited = done, 0, [], {}

    def wait(self, tokens):
        for token in tokens:
            if isinstance(token, list):
                self.wait(token)
            elif token is not None and self.waited.get(token[0].name, 0) < token[1]:
                self.waited[token[0].name] = token[1]
                self.steps.append((None, token, None, None))

    def run(self, op, *args, after=(), signal=True, **kw):
        self.wait(after)
        self.steps.append((op, args, kw, (self.done, 1) if signal else None))
        self.count += signal
        return (self.done, self.count) if signal else None

    def load(self, op, out, in_, done, count, after=()):
        self.wait(after)
        self.steps.append((op, (out, in_), {}, (done, 16)))
        return (done, count)

    def last(self):
        return (self.done, self.count) if self.count else None

    def play(self, eng):
        for op, args, kw, signal in self.steps:
            if op is None:
                eng.wait_ge(args[0], args[1])
            elif signal:
                op(*args, **kw).then_inc(*signal)
            else:
                op(*args, **kw)


class Program:
    def __init__(self, nc, ctx, dram, out):
        self.nc, self.ctx, self.dram, self.out = nc, ctx, dram, out
        self.pe, self.act, self.dve, self.pool, self.sp = (
            Engine(self.sem(n)) for n in ("pe_done", "act_done", "dve_done", "pool_done", "sp_done"))
        self.t, self.s, self.v, self.g = nc.tensor, nc.scalar, nc.vector, nc.gpsimd
        sb, ps = self.sb, self.ps
        self.consts = sb("consts", N_CONSTS)
        self.x = sb("residual", TT * D).rearrange("p (t n) -> p t n", t=TT)
        self.stat = sb("stat", 512)
        self.half = sb("minus_half", 64)
        self.cols = sb("cols", max(N_FIRST_COLS, N_SECOND_COLS))
        self.rows = sb("rows", D)
        self.raw = [sb(f"w_raw{i}", 2 * UNIT) for i in range(RAW_SLOTS)]
        self.wh = [sb(f"w_high{i}", UNIT, F32R) for i in range(SPLIT_SLOTS)]
        self.wl = [sb(f"w_low{i}", UNIT, F32R) for i in range(SPLIT_SLOTS)]
        self.xh = self.kt_view(sb("x_high", DK * SEQ, F32R))
        self.xl = self.kt_view(sb("x_low", DK * SEQ, F32R))
        self.scr = sb("scratch", 4 * UNIT)
        self.acc = [ps(f"acc{i}", 2 * PANEL) for i in range(2)]
        self.bank = [ps(f"bank{i}", PANEL) for i in range(4)]
        self.free = {}
        self.units, self.loads, self.total = weight_units()
        self.raw_sem = [self.sem(f"w_loaded{i}") for i in range(RAW_SLOTS)]
        self.n_loaded = self.n_split = self.n_used = 0
        self.load_token, self.high_token, self.low_token, self.used_token = [], [], [], []
        self.turn = 0

    def sem(self, name):
        return self.ctx.enter_context(self.nc.semaphore(name))

    def sb(self, name, floats, dt=F32, ctx=None):
        return (ctx or self.ctx).enter_context(self.nc.sbuf_tensor(name, [P, floats], dt))[:, :]

    def ps(self, name, floats):
        return self.ctx.enter_context(self.nc.psum_tensor(name, [P, floats], F32))[:, :]

    def kt_view(self, ap):
        return ap.rearrange("p (k s) -> p k s", s=SEQ)

    def const(self, name):
        a, b = CONSTS[name]
        return self.consts[:, a:b]

    def small_load(self, name, out, in_, after=()):
        return self.sp.load(self.nc.sync.dma_start, out, in_, self.sem(name), 16, after)

    def fence(self):
        done = [e.last() for e in (self.pe, self.act, self.dve, self.pool)]
        for e in (self.pe, self.act, self.dve, self.pool, self.sp):
            e.wait(done)

    def load_weights(self, n):
        at, size = self.loads[n]
        slot = n % RAW_SLOTS
        before = [u for u, unit in enumerate(self.units) if unit["load"] == n - RAW_SLOTS]
        src = self.dram["weights"][at:at + P * size].rearrange("(p n) -> p n", p=P)
        self.load_token.append(self.sp.load(
            self.nc.sync.dma_start, self.raw[slot][:, 0:size], src, self.raw_sem[slot],
            16 * (n // RAW_SLOTS + 1),
            after=[self.high_token[u] for u in before] + [self.low_token[u] for u in before]))

    def split_unit(self, n):
        u = self.units[n]
        size = u["w"] * u["nk"]
        slot = n % SPLIT_SLOTS
        raw = self.raw[u["load"] % RAW_SLOTS][:, u["inside"]:u["inside"] + size]
        left = self.used_token[n - SPLIT_SLOTS] if n >= SPLIT_SLOTS else None
        self.high_token.append(self.act.run(self.s.activation, self.wh[slot][:, 0:size], raw, ACT.Copy,
                                            after=[self.load_token[u["load"]], left]))
        self.low_token.append(self.dve.run(self.v.tensor_tensor, self.wl[slot][:, 0:size], raw,
                                           self.wh[slot][:, 0:size], ALU.subtract,
                                           after=[self.high_token[n], left]))

    def prefetch(self, n):
        last = min(n + SPLIT_AHEAD, len(self.units) - 1)
        while self.n_split <= last:
            reach = self.units[self.n_split]["load"] + RAW_SLOTS
            if self.n_split:
                reach = min(reach, self.units[self.n_split - 1]["load"] + RAW_SLOTS)
            while self.n_loaded < min(reach, len(self.loads)):
                self.load_weights(self.n_loaded)
                self.n_loaded += 1
            self.split_unit(self.n_split)
            self.n_split += 1

    def linear(self, name, layer, high, low, ready, feature_major, consume):
        first = True
        while self.n_used < len(self.units):
            u = self.units[self.n_used]
            if (u["name"], u["layer"]) != (name, layer):
                break
            n = self.n_used
            self.prefetch(n)
            w, slot = u["w"], n % SPLIT_SLOTS
            if u["k0"] == 0:
                acc = self.acc[self.turn % 2]
                self.pe.wait(self.free.get(("acc", self.turn % 2), []))
            by_feature = feature_major(u["panel"]) if callable(feature_major) else feature_major
            wh = self.wh[slot][:, 0:w * u["nk"]].rearrange("p (k n) -> p k n", n=w)
            wl = self.wl[slot][:, 0:w * u["nk"]].rearrange("p (k n) -> p k n", n=w)
            kts = KTS[name]
            self.pe.wait([self.low_token[n]])
            ops = []
            for j in range(u["nk"]):
                k = u["k0"] + j
                self.pe.wait([ready[k]])
                end = k == kts - 1
                if by_feature:
                    for f in range(w // P):
                        cut = slice(f * P, (f + 1) * P)
                        o = acc[:, f * SEQ:(f + 1) * SEQ]
                        bank_start = k == 0 and f % 2 == 0
                        ops += [(o, wh[:, j, cut], high[:, k, :], bank_start, False),
                                (o, wh[:, j, cut], low[:, k, :], False, False),
                                (o, wl[:, j, cut], high[:, k, :], False, end)]
                else:
                    for t in range(TT):
                        cut = slice(t * P, (t + 1) * P)
                        o = acc[:, t * PANEL:t * PANEL + w]
                        ops += [(o, high[:, k, cut], wh[:, j, :], k == 0, False),
                                (o, high[:, k, cut], wl[:, j, :], False, False),
                                (o, low[:, k, cut], wh[:, j, :], False, end)]
            for i, (o, a, b, start, stop) in enumerate(ops):
                token = self.pe.run(self.t.matmul, o, a, b, start=start, stop=stop,
                                    skip_group_check=True, signal=i == len(ops) - 1)
            self.used_token.append(token)
            self.n_used += 1
            if end:
                self.free[("acc", self.turn % 2)] = consume(u["panel"], acc, w, token)
                self.turn += 1
            yield

    def rstd(self, sums, n, count, out, after):
        t = self.pool.run(self.g.tensor_scalar, sums, sums, 1.0 / count, EPS, ALU.mult, ALU.add, after=after)
        return self.pool.run(self.g.tensor_tensor, out, sums, self.half[:, 0:n], ALU.pow, after=[t])

    def token_rstd(self, src, width, after):
        s = self.stat
        a = self.act.run(self.s.activation, self.scr[:, 2 * UNIT:2 * UNIT + width], src[:, 0, :], ACT.Square,
                         accum_out=s[:, 0:1], after=after)
        d = self.dve.run(self.v.tensor_tensor_reduce, self.scr[:, 3 * UNIT:3 * UNIT + width], src[:, 1, :],
                         src[:, 1, :], 1.0, 0.0, ALU.mult, ALU.add, s[:, 1:2], after=after)
        return self.rstd(s[:, 0:2], 2, width, s[:, 2:4], [a, d])

    def to_features(self, src, kts, ready, high, low, gain=None):
        tokens = []
        ident = self.const("ident")
        for pair in range(0, kts, 2):
            b = (pair // 2) % 4
            bank = self.bank[b]
            self.pe.wait(self.free.get(b, []))
            own = range(pair, min(pair + 2, kts))
            for k in own:
                for t in range(TT):
                    at = (k - pair) * SEQ + t * P
                    done = self.pe.run(self.t.transpose, bank[:, at:at + P], src[:, t, k * P:(k + 1) * P],
                                       ident, after=ready)
            got = [bank[:, (k - pair) * SEQ:(k - pair + 1) * SEQ] for k in own]
            g = [gain[:, k:k + 1] if gain is not None else 1.0 for k in own]
            for i, k in enumerate(own):
                a = self.act.run(self.s.activation, high[:, k, :], got[i], ACT.Copy, scale=g[i], after=[done])
            for i, k in enumerate(own):
                d = self.dve.run(self.v.scalar_tensor_tensor, low[:, k, :], got[i], g[i], high[:, k, :],
                                 ALU.mult, ALU.subtract, after=[done, a])
                tokens.append(d)
            self.free[b] = [a, d]
        return tokens

    def norm_to_features(self, gain, ready):
        r = self.token_rstd(self.x, D, ready)
        xn = self.scr[:, 0:TT * D].rearrange("p (t n) -> p t n", t=TT)
        a = self.act.run(self.s.activation, xn[:, 0, :], self.x[:, 0, :], ACT.Copy, scale=self.stat[:, 2:3],
                         after=[r, ready])
        d = self.dve.run(self.v.tensor_scalar, xn[:, 1, :], self.x[:, 1, :], self.stat[:, 3:4], None,
                         ALU.mult, after=[r])
        return self.to_features(xn, DK, [a, d], self.xh, self.xl, gain)

    def head_scale(self, tile, heads, width, after):
        n = TT * heads
        sq = self.scr[:, 0:n * width].rearrange("p (t h d) -> p t h d", t=TT, h=heads)
        s = self.stat[:, 16:16 + n]
        r = self.stat[:, 64:64 + n]
        a = self.dve.run(self.v.tensor_tensor, sq, tile, tile, ALU.mult, after=[after, self.dve.last()])
        a = self.dve.run(self.v.tensor_reduce, s.rearrange("p (t h) -> p t h", t=TT), sq, AXIS_X, ALU.add,
                         after=[a])
        a = self.rstd(s, n, width, r, [a])
        rb = r.rearrange("p (t h o) -> p t h o", t=TT, o=1).to_broadcast([P, TT, heads, width])
        return self.dve.run(self.v.tensor_tensor, tile, tile, rb, ALU.mult, after=[a])

    def rope_tables(self, tag, rot, gain, out, after):
        h = rot // 2
        for i, (fn, side) in enumerate((("cos_", 0), ("sin_", 1), ("sin_", 0), ("cos_", 1))):
            table = self.const(fn + tag).rearrange("p (t n) -> p t n", t=TT)
            g = gain[:, side * h:(side + 1) * h].rearrange("p (o n) -> p o n", o=1).to_broadcast([P, TT, h])
            o = out[:, i * TT * h:(i + 1) * TT * h].rearrange("p (t n) -> p t n", t=TT)
            t = self.dve.run(self.v.tensor_tensor, o, table, g, ALU.mult, after=after)
        return t

    def rotate(self, tile, heads, at, rot, tables, after, outs=None):
        h = rot // 2
        n = TT * heads * h
        x1, x2 = tile[:, :, :, at:at + h], tile[:, :, :, at + h:at + rot]
        tmp = [self.scr[:, 2 * UNIT + i * n:2 * UNIT + (i + 1) * n].rearrange("p (t h d) -> p t h d", t=TT, h=heads)
               for i in range(4)]
        assert 2 * UNIT + 4 * n <= 4 * UNIT
        after = [after, self.dve.last()]
        for i, (x, o) in enumerate(zip((x1, x2, x1, x2), tmp)):
            tb = tables[:, i * TT * h:(i + 1) * TT * h].rearrange("p (t o n) -> p t o n", t=TT, o=1)
            t = self.dve.run(self.v.tensor_tensor, o, x, tb.to_broadcast([P, TT, heads, h]), ALU.mult, after=after)
        for out in outs or [tile]:
            a = self.dve.run(self.v.tensor_tensor, out[:, :, :, at:at + h], tmp[0], tmp[1], ALU.subtract, after=[t])
            b = self.dve.run(self.v.tensor_tensor, out[:, :, :, at + h:at + rot], tmp[2], tmp[3], ALU.add, after=[t])
        return b

    def residual_add(self, panel, acc, w, token):
        c = panel * PANEL
        x = self.x[:, :, c:c + w]
        got = acc.rearrange("p (t n) -> p t n", t=TT)[:, :, 0:w]
        return [self.dve.run(self.v.tensor_tensor, x, x, got, ALU.add, after=[token])]

    def head_attention(self, h, q, k, v, scale, oh, ol, ready, tokens):
        b = h % 2
        s_bank, pt_bank, o_bank = self.bank[b], self.bank[2], self.bank[3]
        st = self.stat[:, 128 + 16 * b:144 + 16 * b]
        prob = self.scr[:, b * PANEL:(b + 1) * PANEL]
        probt = self.scr[:, (2 + b) * PANEL:(3 + b) * PANEL]
        self.pe.wait(self.free.get(b, []))
        for t in range(TT):
            done = self.pe.run(self.t.matmul, s_bank[:, t * SEQ:(t + 1) * SEQ], q[:, t * P:(t + 1) * P], k,
                               start=True, stop=True, after=ready, signal=t == TT - 1)
        a = self.dve.run(self.v.tensor_reduce, st[:, 0:2], s_bank.rearrange("p (t k) -> p t k", t=TT), AXIS_X,
                         ALU.max, after=[done, self.free.get(("stat", b))])
        a = self.dve.run(self.v.tensor_scalar, st[:, 2:4], st[:, 0:2], -scale, None, ALU.mult, after=[a])
        for t in range(TT):
            e = self.act.run(self.s.activation, prob[:, t * SEQ:(t + 1) * SEQ], s_bank[:, t * SEQ:(t + 1) * SEQ],
                             ACT.Exp, bias=st[:, 2 + t:3 + t], scale=scale, accum_out=st[:, 4 + t:5 + t],
                             after=[a, self.free.get(("prob", b))])
        self.free[b] = [a, e]
        self.free[("stat", b)] = e
        yield
        a = self.dve.run(self.v.reciprocal, st[:, 6:8], st[:, 4:6], after=[e])
        for t in range(TT):
            p = prob[:, t * SEQ:(t + 1) * SEQ]
            m = self.dve.run(self.v.tensor_scalar, p, p, st[:, 6 + t:7 + t], None, ALU.mult, after=[a])
        self.pe.wait(self.free.get(2, []))
        for kt in range(TT):
            for t in range(TT):
                done = self.pe.run(self.t.transpose, pt_bank[:, kt * SEQ + t * P:kt * SEQ + (t + 1) * P],
                                   prob[:, t * SEQ + kt * P:t * SEQ + (kt + 1) * P], self.const("ident"), after=[m])
        self.free[("prob", b)] = done
        c = self.act.run(self.s.activation, probt, pt_bank, ACT.Copy, after=[done, self.free.get(("probt", b))])
        self.free[2] = [c]
        yield
        at = HD * (h % 2)
        self.pe.wait(self.free.get(3, []))
        for kt in range(TT):
            done = self.pe.run(self.t.matmul, o_bank[at:at + HD, 0:SEQ], v(kt),
                               probt[:, kt * SEQ:(kt + 1) * SEQ], start=kt == 0, stop=kt == TT - 1,
                               after=[c], signal=kt == TT - 1)
        self.free[("probt", b)] = done
        if h % 2:
            self.free[3] = self.split_out(o_bank[:, 0:SEQ], h // 2, oh, ol, done)
            tokens.append(self.free[3][1])

    def split_out(self, got, k, oh, ol, done, scale=1.0):
        a = self.act.run(self.s.activation, oh[:, k, :], got, ACT.Copy, scale=scale, after=[done])
        d = self.dve.run(self.v.scalar_tensor_tensor, ol[:, k, :], got, scale, oh[:, k, :], ALU.mult,
                         ALU.subtract, after=[done, a])
        return [a, d]

    def transpose_pairs(self, src, blocks, rows, out, done, scale=None, free=None):
        for n in range(0, blocks, 2):
            b = (n // 2) % 2
            self.pe.wait(self.free.get(b, []))
            for i in range(2):
                for t in range(TT):
                    at = i * SEQ + t * P
                    d = self.pe.run(self.t.transpose, self.bank[b][0:rows, at:at + P], src(n + i, t),
                                    self.const("ident"), after=done)
            got = self.bank[b][0:rows, :].rearrange("p (k s) -> p k s", k=2)
            g = scale[0:rows, :] if scale is not None else 1.0
            if b:
                e = self.act.run(self.s.activation, out[0:rows, n:n + 2, :], got, ACT.Copy, scale=g, after=[d, free])
            else:
                e = self.dve.run(self.v.tensor_scalar, out[0:rows, n:n + 2, :], got, g, None, ALU.mult, after=[d, free])
            self.free[b] = [e]
        return [self.free[0], self.free[1]]

    def first_mixing(self, l):
        v, s, g = self.v, self.s, self.g
        cols = lambda name: self.cols[:, FIRST_COLS[name][0]:FIRST_COLS[name][1]]
        with ExitStack() as ctx:
            sb = lambda name, floats, dt=F32: self.sb(f"{name}_{l}", floats, dt, ctx)
            gates = self.kt_view(sb("gates", 3 * DK * SEQ))
            tok = sb("mla_tokens", 2 * TT * MLA_H * MLA_QK)
            n = TT * MLA_H * MLA_QK
            mq, mk = (tok[:, i * n:(i + 1) * n].rearrange("p (t h d) -> p t h d", t=TT, h=MLA_H) for i in range(2))
            qk = self.kt_view(sb("heads_q_k", 2 * MLA_H * SEQ))
            mv = sb("mla_v", TT * MLA_H * MLA_V).rearrange("p (t h d) -> p t h d", t=TT, h=MLA_H)
            gqk = sb("gqa_tokens", TT * (GQA_H + GQA_KV) * HD).rearrange("p (t h d) -> p t h d", t=TT, d=HD)
            gv = sb("gqa_v", TT * GQA_KV * HD).rearrange("p (t n) -> p t n", t=TT)
            n_c = Q_LORA + KV_LORA + ROPE
            c = sb("compressed", TT * n_c).rearrange("p (t n) -> p t n", t=TT)
            pw = SEQ + 2 * POOL_PAD
            pp = sb("pool_in", POOL_G * pw).rearrange("p (g n) -> p g n", g=POOL_G)
            oh = self.kt_view(sb("mixed_high", 4 * SEQ, F32R))
            ol = self.kt_view(sb("mixed_low", 4 * SEQ, F32R))
            tab = sb("rope_tables", 2 * 4 * TT * (ROPE + HD) // 2)
            tq, tk = tab[:, 0:128], tab[:, 128:256]
            tgq, tgk = tab[:, 256:512], tab[:, 512:768]
            pool_w = self.rows[:, 256:256 + POOL_G * P].rearrange("p (g n) -> p g n", g=POOL_G)

            self.fence()
            loaded = [
                self.small_load(f"cols_loaded_{l}", self.cols[:, 0:N_FIRST_COLS], self.dram["first_cols"][l]),
                self.small_load(f"rows_loaded_{l}", self.rows[:, 0:N_ROWS], self.dram["first_rows"][l].partition_broadcast(P))]
            pool_w_loaded = self.small_load(f"pool_w_loaded_{l}", pool_w, self.dram["pool_w"][l].rearrange("p (g n) -> p g n", g=POOL_G))
            pads = [self.pool.run(g.memset, pp[:, :, a:a + POOL_PAD], 0.0) for a in (0, POOL_PAD + SEQ)]
            row = lambda r: self.rows[:, r[0]:r[1]]
            for tag, rot, r, out in (("m", ROPE, ROW_QM, tq), ("m", ROPE, ROW_KM, tk), ("g", HD, ROW_QG, tgq),
                                     ("g", HD, ROW_KG, tgk)):
                tables = self.rope_tables(tag, rot, row(r), out, [loaded])
            ready = self.norm_to_features(cols("attn_g"), [self.x_ready, loaded])

            got = {}

            def take(panel, acc, w, done):
                a = acc.rearrange("p (t n) -> p t n", t=TT)
                if panel == 0:
                    copy = self.dve.run(v.tensor_copy, c, a[:, :, 0:w], after=[done])
                    n_n = Q_LORA + KV_LORA
                    sq = self.scr[:, 0:TT * n_n].rearrange("p (t n) -> p t n", t=TT)
                    t1 = self.dve.run(v.tensor_tensor, sq, c[:, :, 0:n_n], c[:, :, 0:n_n], ALU.mult, after=[copy])
                    st, r = self.stat[:, 0:4], self.stat[:, 4:8]
                    self.dve.run(v.tensor_reduce, st[:, 0:2], sq[:, :, 0:Q_LORA], AXIS_X, ALU.add, after=[t1])
                    t2 = self.dve.run(v.tensor_reduce, st[:, 2:4], sq[:, :, Q_LORA:n_n], AXIS_X, ALU.add, after=[t1])
                    self.pool.run(g.tensor_scalar, st[:, 0:2], st[:, 0:2], 1.0 / Q_LORA, EPS, ALU.mult, ALU.add, after=[t2])
                    t3 = self.pool.run(g.tensor_scalar, st[:, 2:4], st[:, 2:4], 1.0 / KV_LORA, EPS, ALU.mult, ALU.add)
                    t4 = self.pool.run(g.tensor_tensor, r, st, self.half[:, 0:4], ALU.pow, after=[t3])
                    for i, (c0, c1) in enumerate(((0, Q_LORA), (Q_LORA, n_n))):
                        rb = r[:, 2 * i:2 * i + 2].rearrange("p (t o) -> p t o", o=1).to_broadcast([P, TT, c1 - c0])
                        t5 = self.dve.run(v.tensor_tensor, c[:, :, c0:c1], c[:, :, c0:c1], rb, ALU.mult, after=[t4])
                    got["c"] = t5
                    return [copy]
                if panel == 1:
                    e = self.act.run(s.activation, gqk[:, :, 0:GQA_H, :], a.rearrange("p t (h d) -> p t h d", d=HD),
                                     ACT.Copy, after=[done])
                    return [e]
                if panel == 2:
                    n_k = GQA_KV * HD
                    self.act.run(s.activation, gqk[:, :, GQA_H:, :],
                                 a[:, :, 0:n_k].rearrange("p t (h d) -> p t h d", d=HD), ACT.Copy, after=[done])
                    got["gqa"] = self.act.run(s.activation, gv, a[:, :, n_k:2 * n_k], ACT.Copy)
                    return [got["gqa"]]
                got["pool"] = self.act.run(s.activation, pp[:, :, POOL_PAD:POOL_PAD + SEQ],
                                           acc.rearrange("p (g s) -> p g s", g=POOL_G), ACT.Copy, after=[done, pads])
                return [got["pool"]]

            run_all(self.linear("proj", l, self.xh, self.xl, ready, lambda p: p == 3, take))
            lora = self.to_features(c, 3, [got["c"]], oh, ol, 
                                    self.cols[:, FIRST_COLS["q_lora_g"][0]:FIRST_COLS["kv_lora_g"][1]])

            mq_flat = mq.rearrange("p t h d -> p t (h d)")

            def take_q(panel, acc, w, done):
                a = acc.rearrange("p (t n) -> p t n", t=TT)[:, :, 0:w]
                got["mq"] = self.act.run(s.activation, mq_flat[:, :, panel * PANEL:panel * PANEL + w], a, ACT.Copy, after=[done])
                return [got["mq"]]

            def take_kv(panel, acc, w, done):
                hp = w // (NOPE + MLA_V)
                a = acc.rearrange("p (t h d) -> p t h d", t=TT, d=NOPE + MLA_V)
                hs = slice(panel * hp, (panel + 1) * hp)
                self.dve.run(v.tensor_copy, mk[:, :, hs, 0:NOPE], a[:, :, :, 0:NOPE], after=[done])
                got["mv"] = self.dve.run(v.tensor_copy, mv[:, :, hs, :], a[:, :, :, NOPE:], after=[done])
                return [got["mv"]]

            run_all(self.linear("up_q", l, oh, ol, lora, False, take_q))
            run_all(self.linear("up_kv", l, oh[:, 2:3, :], ol[:, 2:3, :], lora[2:], False, take_kv))

            def mla():
                kr = c[:, :, Q_LORA + KV_LORA:].rearrange("p t (o d) -> p t o d", o=1).to_broadcast([P, TT, MLA_H, ROPE])
                t = self.dve.run(v.tensor_copy, mk[:, :, :, NOPE:], kr)
                t = self.head_scale(mk, MLA_H, MLA_QK, [t])
                tk_ready = self.rotate(mk, MLA_H, NOPE, ROPE, tk, [t])
                yield
                t = self.head_scale(mq, MLA_H, MLA_QK, [got["mq"]])
                tq_ready = self.rotate(mq, MLA_H, NOPE, ROPE, tq, [t])
                yield
                a = self.transpose_pairs(lambda h, t: mk[:, t, h, :], MLA_H, MLA_QK, qk[:, MLA_H:, :], [tk_ready],
                                         cols("k_head_g"))
                yield
                b = self.transpose_pairs(lambda h, t: mq[:, t, h, :], MLA_H, MLA_QK, qk[:, 0:MLA_H, :], [tq_ready],
                                         cols("q_head_g"))
                got["turned"] = self.pe.last()
                yield
                tokens = []
                yield from pipelined(
                    self.head_attention(h, qk[0:MLA_QK, h, :], qk[0:MLA_QK, MLA_H + h, :],
                                        lambda kt, h=h: mv[:, kt, h, :], MLA_QK ** -0.5, oh, ol, [a, b, got["mv"]], tokens)
                    for h in range(MLA_H))
                got["mla"] = tokens

            def take_gates(panel, acc, w, done):
                return [self.act.run(s.activation, gates[:, 4 * panel:4 * panel + 4, :], self.kt_view(acc), ACT.Copy,
                                     after=[done])]

            interleave(mla(), self.linear("gates", l, self.xh, self.xl, ready, True, take_gates), 2)
            for b in range(3):
                part = gates[:, b * DK:(b + 1) * DK, :]
                got["gate", b] = self.act.run(s.activation, part, part, ACT.Sigmoid, after=[self.act.last()])

            def gated(b):
                def take(panel, acc, w, done):
                    part = gates[:, b * DK + 4 * panel:b * DK + 4 * panel + 4, :]
                    got["merged", b, panel] = self.dve.run(v.tensor_tensor, part, part, self.kt_view(acc), ALU.mult,
                                                           after=[done, got["gate", b]])
                    return [got["merged", b, panel]]
                return take

            run_all(self.linear("branch_mla", l, oh, ol, got["mla"], True, gated(0)))

            kd = tok[:, 0:2 * TT * GQA_KV * HD].rearrange("p (t g u d) -> p t g u d", t=TT, g=GQA_KV, u=2)
            t = self.head_scale(gqk, GQA_H + GQA_KV, HD, [got["gqa"]])
            tq_ready = self.rotate(gqk[:, :, 0:GQA_H, :], GQA_H, 0, HD, tgq, [t])
            tk_ready = self.rotate(gqk[:, :, GQA_H:, :], GQA_KV, 0, HD, tgk, [t, got["turned"]],
                                   outs=[kd[:, :, :, u, :] for u in range(2)])
            flat = gqk.rearrange("p t h d -> p t (h d)")
            left = self.pe.last()
            a = self.transpose_pairs(lambda n, t: flat[:, t, n * P:(n + 1) * P], GQA_H // 2, P, qk[:, 0:4, :],
                                     [tq_ready], free=left)
            b = self.transpose_pairs(lambda n, t: kd[:, t, n, :, :], GQA_KV, P, qk[:, 4:6, :], [tk_ready], free=left)
            tokens = []
            half = lambda h: slice(HD * (h % 2), HD * (h % 2) + HD)
            run_all(pipelined(
                self.head_attention(h, qk[half(h), h // 2, :], qk[half(h), 4 + h // (GQA_H // GQA_KV), :],
                                    lambda kt, h=h: gv[:, kt, HD * (h // 4):HD * (h // 4) + HD],
                                    HD ** -0.5, oh, ol, [a, b, got["gqa"]], tokens)
                for h in range(GQA_H)))
            run_all(self.linear("branch_gqa", l, oh, ol, tokens, True, gated(1)))

            tmp = [tok[:, 512 + i * POOL_G * pw:512 + (i + 1) * POOL_G * pw].rearrange("p (g n) -> p g n", g=POOL_G)
                   for i in range(2)]
            src, t, sums = pp, self.pool.run(g.tensor_tensor, tmp[0][:, :, 1:pw], pp[:, :, 0:pw - 1], pp[:, :, 1:pw],
                                             ALU.add, after=[got["pool"], got["turned"]]), [tmp[0]]
            for n in range(1, POOL_G):
                r = 2 ** (n - 1)
                lo, hi = 2 * r, pw - 2 * r + 1
                a, b = sums[-1], tmp[n % 2]
                t = self.pool.run(g.tensor_tensor, b[:, n:, lo:hi], a[:, n:, lo - r:hi - r], a[:, n:, lo + r:hi + r],
                                  ALU.add, after=[t])
                sums.append(b)
            edge = self.const("pool_edge").rearrange("p (g n) -> p g n", g=POOL_G)
            mixed = pp[:, :, POOL_PAD:POOL_PAD + SEQ]
            for n, w in enumerate(POOL_WINDOWS):
                e = POOL_PAD
                for at, c0 in ((e, 0), (SEQ, e)):
                    part = sums[n][:, n, at:at + e]
                    t = self.pool.run(g.tensor_tensor, part, part, edge[:, n, c0:c0 + e], ALU.mult, after=[t])
                d = self.dve.run(v.scalar_tensor_tensor, mixed[:, n, :], sums[n][:, n, e:e + SEQ], 1.0 / w,
                                 mixed[:, n, :], ALU.mult, ALU.subtract, after=[t])
            tokens = []
            for n in range(POOL_G):
                b = n % 2
                self.pe.wait(self.free.get(b, []))
                done = self.pe.run(self.t.matmul, self.bank[b][:, 0:SEQ], pool_w[:, n, :], mixed[:, n, :],
                                   start=True, stop=True, after=[d, pool_w_loaded])
                self.free[b] = self.split_out(self.bank[b][:, 0:SEQ], n, oh, ol, done, cols("pool_scale")[:, n:n + 1])
                tokens.append(self.free[b][1])
            run_all(self.linear("branch_pool", l, oh, ol, tokens, True, gated(2)))

            ready = []
            for half_ in range(2):
                ks = slice(4 * half_, 4 * half_ + 4)
                m, m1, m2 = (gates[:, i * DK + 4 * half_:i * DK + 4 * half_ + 4, :] for i in range(3))
                t = self.dve.run(v.tensor_tensor, m, m, m1, ALU.add, after=[got["merged", 1, half_]])
                t = self.dve.run(v.tensor_tensor, m, m, m2, ALU.add, after=[t, got["merged", 2, half_]])
                a = self.act.run(s.activation, self.xh[:, ks, :], m, ACT.Copy, after=[t, self.pe.last()])
                d = self.dve.run(v.tensor_tensor, self.xl[:, ks, :], m, self.xh[:, ks, :], ALU.subtract, after=[a])
                ready += [d] * 4
            run_all(self.linear("out", l, self.xh, self.xl, ready, False, self.residual_add))
            self.x_ready = self.dve.last()

    def first_ffn(self, l):
        v, s = self.v, self.s
        cols = lambda name: self.cols[:, FIRST_COLS[name][0]:FIRST_COLS[name][1]]
        with ExitStack() as ctx:
            ah = self.kt_view(self.sb(f"ffn_high_{l}", FT * SEQ, F32R, ctx))
            al = self.kt_view(self.sb(f"ffn_low_{l}", FT * SEQ, F32R, ctx))
            self.fence()
            ready = self.norm_to_features(cols("ffn_g"), [self.x_ready])
            conv_w, conv_b = cols("conv_w"), cols("conv_b")
            acts = []

            def take(panel, acc, w, done):
                pair, value = panel // 2, panel % 2
                buf = self.scr[:, (pair % 2) * 2 * UNIT:(pair % 2 + 1) * 2 * UNIT]
                o = self.kt_view(buf[:, value * UNIT:value * UNIT + w * TT])
                u = self.kt_view(acc)
                readers = []
                def tap(i, f):
                    ft = i * 2 * FT + value * FT + pair * (PANEL // P) + f
                    return conv_w[:, ft:ft + 1]
                for bank in range(w // (2 * P)):
                    fs = (2 * bank, 2 * bank + 1)
                    for f in fs:
                        ft = value * FT + pair * (PANEL // P) + f
                        a = self.act.run(s.activation, o[:, f, :], u[:, f, :], ACT.Identity, scale=tap(1, f),
                                         bias=conv_b[:, ft:ft + 1], after=[done, self.free.get(("conv", pair % 2))])
                    for f in fs:
                        d = self.dve.run(v.scalar_tensor_tensor, o[:, f, 1:], u[:, f, 0:SEQ - 1], tap(0, f),
                                         o[:, f, 1:], ALU.mult, ALU.add, after=[done, a])
                    for f in fs:
                        d = self.dve.run(v.scalar_tensor_tensor, o[:, f, 0:SEQ - 1], u[:, f, 1:], tap(2, f),
                                         o[:, f, 0:SEQ - 1], ALU.mult, ALU.add, after=[d])
                    readers += [a, d]
                if value:
                    n = w * TT
                    gate, val = buf[:, 0:n], buf[:, UNIT:UNIT + n]
                    a = self.act.run(s.activation, gate, gate, ACT.Silu, after=[d])
                    m = self.dve.run(v.tensor_tensor, gate, gate, val, ALU.mult, after=[a])
                    ks = slice(pair * 4, pair * 4 + w // P)
                    a = self.act.run(s.activation, ah[:, ks, :], self.kt_view(gate), ACT.Copy, after=[m])
                    d = self.dve.run(v.tensor_tensor, al[:, ks, :], self.kt_view(gate), ah[:, ks, :], ALU.subtract, after=[a])
                    self.free[("conv", pair % 2)] = d
                    acts.extend([d] * (w // P))
                return readers

            run_all(self.linear("ffn_up", l, self.xh, self.xl, ready, True, take))
            run_all(self.linear("ffn_down", l, ah, al, acts, False, self.residual_add))
            self.x_ready = self.dve.last()

    def take_to_scratch(self):
        y = self.scr[:, 0:TT * D].rearrange("p (t n) -> p t n", t=TT)
        tokens = []

        def take(panel, acc, w, done):
            a = acc.rearrange("p (t n) -> p t n", t=TT)
            tokens.append(self.act.run(self.s.activation, y[:, :, panel * PANEL:panel * PANEL + w], a, ACT.Copy,
                                       after=[done]))
            return [tokens[-1]]
        return y, tokens, take

    def post_norm(self, y, tokens, gain_loaded):
        r = self.token_rstd(y, D, tokens)
        for t in range(TT):
            a = self.dve.run(self.v.scalar_tensor_tensor, y[:, t, :], y[:, t, :], self.stat[:, 2 + t:3 + t],
                             self.rows[:, 0:D], ALU.mult, ALU.mult, after=[r, gain_loaded])
            self.x_ready = self.dve.run(self.v.tensor_tensor, self.x[:, t, :], self.x[:, t, :], y[:, t, :],
                                        ALU.add, after=[a])

    def stick_breaking(self, l):
        v, s = self.v, self.s
        cols = lambda name: self.cols[:, SECOND_COLS[name][0]:SECOND_COLS[name][1]]
        with ExitStack() as ctx:
            sb = lambda name, floats, dt=F32: self.sb(f"{name}_{l}", floats, dt, ctx)
            q, k = self.kt_view(sb("sb_q", DK * SEQ)), self.kt_view(sb("sb_k", DK * SEQ))
            val = sb("sb_v", TT * D).rearrange("p (t n) -> p t n", t=TT)
            oh, ol = self.kt_view(sb("sb_out_high", DK * SEQ, F32R)), self.kt_view(sb("sb_out_low", DK * SEQ, F32R))
            NZ = 3 * P
            weights = [sb(f"sb_weights{i}", 2 * NZ).rearrange("p (j n) -> p j n", j=2) for i in range(2)]
            self.fence()
            loaded = [
                self.small_load(f"second_cols_loaded_{l}", self.cols[:, 0:N_SECOND_COLS], self.dram["second_cols"][l]),
                self.small_load(f"mix_gain_loaded_{l}", self.rows, self.dram["second_rows"][l, 0].partition_broadcast(P))]
            ready = self.norm_to_features(cols("mix_g"), [self.x_ready, loaded])
            got = {}

            def take(panel, acc, w, done):
                part = slice(4 * (panel % 2), 4 * (panel % 2) + 4)
                if panel < 2:
                    got["q"] = self.act.run(s.activation, q[:, part, :], self.kt_view(acc), ACT.Copy, scale=HD ** -0.5,
                                            after=[done])
                    return [got["q"]]
                if panel < 4:
                    got["k"] = self.dve.run(v.tensor_copy, k[:, part, :], self.kt_view(acc), after=[done])
                    return [got["k"]]
                c = (panel - 4) * PANEL
                got["v"] = self.act.run(s.activation, val[:, :, c:c + w], acc.rearrange("p (t n) -> p t n", t=TT), ACT.Copy,
                                        after=[done])
                return [got["v"]]

            run_all(self.linear("sb_in", l, self.xh, self.xl, ready, lambda p: p < 4, take))
            neg, add = (self.const(n).rearrange("p (o n) -> p o n", o=1).to_broadcast([P, 2, NZ]) for n in ("sb_neg", "sb_add"))
            not_below, ones = self.const("not_below"), self.const("ones")
            tokens = []

            def pair(j):
                b = j % 2
                z = self.acc[b].rearrange("p (j n) -> p j n", j=2)
                zs = z[:, :, 0:NZ]
                soft, fail = (self.scr[:, (2 * b + i) * UNIT:(2 * b + i) * UNIT + 2 * NZ].rearrange("p (j n) -> p j n", j=2)
                              for i in range(2))
                w = weights[b]
                self.pe.wait(self.free.get(("acc", b), []))
                for i in range(2):
                    rows = slice(HD * i, HD * i + HD)
                    self.pe.run(self.t.matmul, z[:, i, 0:SEQ], k[rows, j, 0:P], q[rows, j, :], start=True, stop=True,
                                after=[got["q"], got["k"]], signal=False, skip_group_check=True)
                    done = self.pe.run(self.t.matmul, z[:, i, SEQ:NZ], k[rows, j, P:SEQ], q[rows, j, P:SEQ],
                                       start=False, stop=True, skip_group_check=True)
                a = self.act.run(s.activation, soft, zs, ACT.Abs, after=[done, self.free.get(("soft", b))])
                a = self.act.run(s.activation, soft, soft, ACT.Exp, scale=-1.0, after=[a])
                a = self.act.run(s.activation, soft, soft, ACT.Ln, bias=1.0, after=[a])
                d = self.dve.run(v.scalar_tensor_tensor, fail, zs, 0.0, soft, ALU.max, ALU.add,
                                 after=[a, self.free.get(("fail", b))])
                d = self.dve.run(v.tensor_tensor, fail, fail, neg, ALU.mult, after=[d])
                yield
                for i in range(2):
                    for o, m, r in ((z[:, i, 0:SEQ], not_below, fail[:, i, 0:SEQ]),
                                    (z[:, i, P:SEQ], ones, fail[:, i, SEQ:NZ]),
                                    (z[:, i, SEQ:NZ], not_below, fail[:, i, SEQ:NZ])):
                        done = self.pe.run(self.t.matmul, o, m, r, start=False, stop=True, after=[d],
                                           skip_group_check=True)
                self.free[("fail", b)] = done
                d = self.dve.run(v.scalar_tensor_tensor, soft, zs, 0.0, add, ALU.min, ALU.add, after=[done])
                a = self.act.run(s.activation, w, soft, ACT.Exp, after=[d, self.free.get(("weights", b))])
                self.free[("acc", b)] = [d, a]
                self.free[("soft", b)] = a
                yield
                o_bank = self.bank[b]
                self.pe.wait(self.free.get(b, []))
                for i in range(2):
                    h = 2 * j + i
                    o = o_bank[HD * i:HD * i + HD, :]
                    self.pe.run(self.t.matmul, o[:, 0:SEQ], val[:, 0, HD * h:HD * h + HD], w[:, i, 0:SEQ], start=True,
                                stop=True, after=[a, got["v"]], signal=False, skip_group_check=True)
                    done = self.pe.run(self.t.matmul, o[:, P:SEQ], val[:, 1, HD * h:HD * h + HD], w[:, i, SEQ:NZ],
                                       start=False, stop=True, skip_group_check=True)
                self.free[("weights", b)] = done
                self.free[b] = self.split_out(o_bank[:, 0:SEQ], j, oh, ol, done)
                tokens.append(self.free[b][1])

            run_all(pipelined(pair(j) for j in range(SB_H // 2)))
            self.turn = 0
            y, ys, take_y = self.take_to_scratch()
            self.act.wait([self.dve.last(), self.pe.last()])
            run_all(self.linear("sb_out", l, oh, ol, tokens, False, take_y))
            self.post_norm(y, ys, loaded)

    def position_tables(self, pos, ang, out):
        v = self.v
        loaded = self.small_load("positions_loaded", pos, self.dram["positions"])
        n = DIL_ROT // 2
        parts, rest = [], 2 * np.pi
        for bits in (8, 8, 8):
            e = 2.0 ** (bits - 1 - np.floor(np.log2(rest)))
            parts.append(float(np.floor(rest * e) / e))
            rest -= parts[-1]
        parts.append(float(np.float32(rest)))
        a0, turns, a1 = (ang[:, i * TT * n:(i + 1) * TT * n] for i in range(3))
        t3 = lambda ap: ap.rearrange("p (t n) -> p t n", t=TT)
        magic = 1.5 * 2.0 ** 23
        posf = ang[:, 3 * TT * n:3 * TT * n + TT]
        t = self.dve.run(v.tensor_copy, posf, pos, after=[loaded])
        t = self.dve.run(v.tensor_tensor, t3(a0), posf.rearrange("p (t o) -> p t o", o=1).to_broadcast([P, TT, n]),
                         self.const("inv_freq").rearrange("p (o n) -> p o n", o=1).to_broadcast([P, TT, n]),
                         ALU.mult, after=[t])
        t = self.dve.run(v.tensor_scalar, turns, a0, 1.0 / (2 * np.pi), magic, ALU.mult, ALU.add, after=[t])
        t = self.dve.run(v.tensor_scalar, turns, turns, magic, None, ALU.subtract, after=[t])
        for part in parts:
            t = self.dve.run(v.scalar_tensor_tensor, a0, turns, -part, a0, ALU.mult, ALU.add, after=[t])
        t = self.dve.run(v.tensor_scalar, a1, a0, np.pi / 2, None, ALU.add, after=[t])
        t = self.dve.run(v.tensor_scalar, turns, a1, np.pi, -2 * np.pi, ALU.is_gt, ALU.mult, after=[t])
        t = self.dve.run(v.tensor_tensor, a1, a1, turns, ALU.add, after=[t])
        for a in (a0, a1):
            t = self.dve.run(v.tensor_scalar, a, a, 3.1415925, -3.1415925, ALU.min, ALU.max, after=[t])
        c, sn = out[:, 0:TT * n], out[:, TT * n:2 * TT * n]
        a = self.act.run(self.s.activation, c, a1, ACT.Sin, after=[t])
        b = self.act.run(self.s.activation, sn, a0, ACT.Sin)
        self.dve.run(v.tensor_copy, out[:, 2 * TT * n:3 * TT * n], sn, after=[a, b])
        return self.dve.run(v.tensor_copy, out[:, 3 * TT * n:], c)

    def dilated(self, l):
        v, s = self.v, self.s
        cols = lambda name: self.cols[:, SECOND_COLS[name][0]:SECOND_COLS[name][1]]
        G = len(DIL)
        with ExitStack() as ctx:
            sb = lambda name, floats, dt=F32: self.sb(f"{name}_{l}", floats, dt, ctx)
            tok = [sb(f"dil_tokens{i}", TT * DIL_W).rearrange("p (t h d) -> p t h d", t=TT, d=HD) for i in range(2)]
            qt = [self.kt_view(sb(f"dil_q{i}", 4 * SEQ)) for i in range(G)]
            kt_ = [self.kt_view(sb(f"dil_k{i}", 4 * SEQ)) for i in range(G)]
            val = [sb(f"dil_v{i}", TT * DIL_W).rearrange("p (t n) -> p t n", t=TT) for i in range(G)]
            oh, ol = self.kt_view(sb("dil_out_high", 4 * SEQ, F32R)), self.kt_view(sb("dil_out_low", 4 * SEQ, F32R))
            pos = sb("positions", TT, I32)
            ang = sb("angles", 64)
            tab = sb("dil_tables", 4 * TT * DIL_ROT // 2)
            self.fence()
            loaded = [
                self.small_load(f"second_cols_loaded_{l}", self.cols[:, 0:N_SECOND_COLS], self.dram["second_cols"][l]),
                self.small_load(f"mix_gain_loaded_{l}", self.rows, self.dram["second_rows"][l, 0].partition_broadcast(P))]
            ready = self.norm_to_features(cols("mix_g"), [self.x_ready, loaded])
            tables = self.position_tables(pos, ang, tab)
            got, late = {}, []

            def turn_late():
                if late:
                    n, out, t = late.pop()
                    flat = tok[n].rearrange("p t h d -> p t (h d)")
                    got["turned"] = self.transpose_pairs(lambda i, t: flat[:, t, i * P:(i + 1) * P], 4, P, out, [t])
                    self.free[("tok", n)] = self.pe.last()

            def take(panel, acc, w, done):
                g, what = panel // 3, panel % 3
                a = acc.rearrange("p (t n) -> p t n", t=TT)
                if what == 2:
                    got["v"] = self.act.run(s.activation, val[g], a, ACT.Copy, after=[done])
                    turn_late()
                    return [got["v"]]
                n = what
                c = self.act.run(s.activation, tok[n], a.rearrange("p t (h d) -> p t h d", d=HD), ACT.Copy,
                                 scale=HD ** -0.5 if what == 0 else 1.0, after=[done, self.free.get(("tok", n))])
                t = self.rotate(tok[n], DIL_H, 0, DIL_ROT, tab, [c, tables])
                turn_late()
                late.append((n, (qt, kt_)[what][g], t))
                return [c]

            run_all(self.linear("dil_in", 0, self.xh, self.xl, ready, False, take))
            turn_late()
            turned = [got["turned"], self.act.last(), self.dve.last()]
            mask = self.const("dil_add")
            tokens = []

            def unit(h, t):
                b = h % 2
                keys = (t + 1) * P
                n = G * keys
                s_ps = self.acc[b][:, 0:n] if t else self.bank[0][:, 0:n]
                s_free = ("acc", b) if t else 0
                base = (0 if t == 0 else G * P)
                st = self.stat[:, 128 + 16 * t:136 + 16 * t]
                prob = self.scr[:, t * 2 * UNIT:t * 2 * UNIT + n]
                probt = self.scr[:, t * 2 * UNIT + UNIT:t * 2 * UNIT + UNIT + n]
                half = slice(HD * b, HD * b + HD)
                self.pe.wait(self.free.get(s_free, []))
                for g in range(G):
                    done = self.pe.run(self.t.matmul, s_ps[:, g * keys:(g + 1) * keys], qt[g][half, h // 2, t * P:(t + 1) * P],
                                       kt_[g][half, h // 2, 0:keys], start=True, stop=True, after=[turned],
                                       signal=g == G - 1)
                a = self.dve.run(v.tensor_tensor_reduce, prob, s_ps, mask[:, base:base + n], 1.0, MASKED, ALU.add,
                                 ALU.max, st[:, 0:1], after=[done, self.free.get(("prob", t)), self.free.get(("stat", t))])
                self.free[s_free] = [a]
                a = self.dve.run(v.tensor_scalar, st[:, 1:2], st[:, 0:1], -1.0, None, ALU.mult, after=[a])
                e = self.act.run(s.activation, prob, prob, ACT.Exp, bias=st[:, 1:2], accum_out=st[:, 2:3], after=[a])
                self.free[("stat", t)] = e
                yield
                a = self.dve.run(v.reciprocal, st[:, 3:4], st[:, 2:3], after=[e])
                m = self.dve.run(v.tensor_scalar, prob, prob, st[:, 3:4], None, ALU.mult, after=[a])
                for i in range(n // P):
                    bank = 2 + i // 4
                    self.pe.wait(self.free.get(bank, []))
                    done = self.pe.run(self.t.transpose, self.bank[bank][:, (i % 4) * P:(i % 4 + 1) * P],
                                       prob[:, i * P:(i + 1) * P], self.const("ident"), after=[m])
                self.free[("prob", t)] = done
                for c0 in range(0, n, PANEL):
                    c1 = min(n, c0 + PANEL)
                    c = self.act.run(s.activation, probt[:, c0:c1], self.bank[2 + c0 // PANEL][:, 0:c1 - c0], ACT.Copy,
                                     after=[done, self.free.get(("probt", t))])
                    self.free[2 + c0 // PANEL] = [c]
                yield
                o = self.bank[1][half, t * P:(t + 1) * P]
                self.pe.wait(self.free.get(1, []))
                blocks = [(g, kt) for g in range(G) for kt in range(t + 1)]
                for i, (g, kt) in enumerate(blocks):
                    done = self.pe.run(self.t.matmul, o, val[g][:, kt, HD * h:HD * h + HD], probt[:, i * P:(i + 1) * P],
                                       start=i == 0, stop=i == len(blocks) - 1, after=[c, got["v"]],
                                       skip_group_check=True)
                self.free[("probt", t)] = done
                if t == TT - 1 and h % 2:
                    self.free[1] = self.split_out(self.bank[1][:, 0:SEQ], h // 2, oh, ol, done)
                    tokens.append(self.free[1][1])

            run_all(pipelined(unit(h, t) for h in range(DIL_H) for t in range(TT)))
            self.turn = 0
            y, ys, take_y = self.take_to_scratch()
            self.act.wait([self.dve.last(), self.pe.last()])
            run_all(self.linear("dil_out", 0, oh, ol, tokens, False, take_y))
            self.post_norm(y, ys, loaded)

    def second_ffn(self, l):
        v, s = self.v, self.s
        cols = lambda name: self.cols[:, SECOND_COLS[name][0]:SECOND_COLS[name][1]]
        with ExitStack() as ctx:
            sb = lambda name, floats, dt=F32: self.sb(f"{name}_{l}", floats, dt, ctx)
            n_f = D_FF_2 // P
            ah, al = self.kt_view(sb("ff_high", n_f * SEQ, F32R)), self.kt_view(sb("ff_low", n_f * SEQ, F32R))
            emb = sb("ple_tokens", TT * PLE).rearrange("p (t n) -> p t n", t=TT)
            eh, el = self.kt_view(sb("ple_high", 2 * SEQ, F32R)), self.kt_view(sb("ple_low", 2 * SEQ, F32R))
            up = sb("ple_up", TT * D).rearrange("p (t n) -> p t n", t=TT)
            self.fence()
            loaded = self.small_load(f"ffn_gain_loaded_{l}", self.rows, self.dram["second_rows"][l, 1].partition_broadcast(P))
            emb_loaded = self.small_load(f"ple_loaded_{l}", emb, self.dram["ple"][l].rearrange("(t p) n -> p t n", p=P))
            ready = self.norm_to_features(cols("ffn_g"), [self.x_ready])
            emb_ready = self.to_features(emb, PLE // P, [emb_loaded], eh, el)
            acts = []

            def take(panel, acc, w, done):
                r = self.scr[:, (panel % 2) * UNIT:(panel % 2 + 1) * UNIT]
                relu = self.act.run(s.activation, r, acc, ACT.Relu, after=[done, self.free.get(("act", panel % 2))])
                d = self.dve.run(v.tensor_tensor, r, r, r, ALU.mult, after=[relu])
                ks = slice(4 * panel, 4 * panel + 4)
                a = self.act.run(s.activation, ah[:, ks, :], self.kt_view(r), ACT.Copy, after=[d])
                e = self.dve.run(v.tensor_tensor, al[:, ks, :], self.kt_view(r), ah[:, ks, :], ALU.subtract, after=[a])
                self.free[("act", panel % 2)] = e
                acts.extend([e] * 4)
                return [relu]

            run_all(self.linear("ff_in", l, self.xh, self.xl, ready, True, take))
            y, ys, take_y = self.take_to_scratch()
            self.act.wait([self.dve.last()])
            run_all(self.linear("ff_out", l, ah, al, acts, False, take_y))
            self.post_norm(y, ys, [loaded])

            def take_up(panel, acc, w, done):
                t = self.act.run(s.activation, up[:, :, panel * PANEL:panel * PANEL + w],
                                 acc.rearrange("p (t n) -> p t n", t=TT), ACT.Copy, after=[done])
                return [t]

            run_all(self.linear("ple_up", l, eh, el, emb_ready, False, take_up))
            ready = self.norm_to_features(cols("ple_g"), [self.x_ready])
            free = self.pe.last()

            def take_gate(panel, acc, w, done):
                c = slice(panel * PANEL, panel * PANEL + w)
                gate = self.scr[:, panel * UNIT:(panel + 1) * UNIT].rearrange("p (t n) -> p t n", t=TT)
                a = self.act.run(s.activation, gate, acc.rearrange("p (t n) -> p t n", t=TT), ACT.Sigmoid,
                                 after=[done, free])
                d = self.dve.run(v.tensor_tensor, gate, gate, up[:, :, c], ALU.mult, after=[a])
                self.x_ready = self.dve.run(v.tensor_tensor, self.x[:, :, c], self.x[:, :, c], gate, ALU.add, after=[d])
                return [a]

            run_all(self.linear("ple_gate", l, self.xh, self.xl, ready, False, take_gate))

    def build(self, stages=8):
        sp = self.nc.sync.dma_start
        self.pool.run(self.g.memset, self.half, -0.5)
        tables = self.small_load("consts_loaded", self.consts, self.dram["consts"])
        first = self.small_load("x_loaded", self.x, self.dram["x"].rearrange("(t p) n -> p t n", p=P))
        self.x_ready = first
        for e in (self.pe, self.act, self.dve, self.pool):
            e.wait([first, tables])
        steps = [lambda: self.first_mixing(0), lambda: self.first_ffn(0), lambda: self.first_mixing(1),
                 lambda: self.first_ffn(1), lambda: self.stick_breaking(0), lambda: self.second_ffn(0),
                 lambda: self.dilated(1), lambda: self.second_ffn(1)]
        for step in steps[:stages]:
            step()
        stored = self.small_load("out_stored", self.out.rearrange("(t p) n -> p t n", p=P), self.x, after=[self.x_ready])
        self.sp.wait([stored])

        with self.nc.Block() as block:
            @block.sync
            def _(eng):
                self.sp.play(eng)

            @block.tensor
            def _(eng):
                self.pe.play(eng)

            @block.scalar
            def _(eng):
                self.act.play(eng)

            @block.vector
            def _(eng):
                self.dve.play(eng)

            @block.gpsimd
            def _(eng):
                self.pool.play(eng)


def run_all(gen):
    for _ in gen:
        pass


def pipelined(gens):
    active = []
    for gen in gens:
        next(gen)
        active = [g for g in active if advance(g)]
        active.append(gen)
        yield
    while active:
        active = [g for g in active if advance(g)]
        yield


def advance(gen):
    for _ in gen:
        return True
    return False


def interleave(front, back, per):
    for _ in front:
        for _ in range(per):
            advance(back)
    run_all(back)


KTS = {p[0]: p[3] // P for p in weight_plan()}



def pack(inputs):
    f = {k: np.asarray(v) for k, v in inputs.items()}
    units, loads, total = weight_units()
    flat = np.empty(total, np.float32)
    by_load = {}
    for u in units:
        by_load.setdefault(u["load"], []).append(u)
    for n, (at, size) in enumerate(loads):
        parts = []
        for u in by_load[n]:
            w = f[u["source"]][u["layer"]][u["k0"] * P:(u["k0"] + u["nk"]) * P, u["c0"]:u["c0"] + u["w"]]
            parts.append(w.reshape(u["nk"], P, u["w"]).transpose(1, 0, 2).reshape(P, -1))
        flat[at:at + P * size] = np.concatenate(parts, 1).reshape(-1)

    def col(a):
        return a.reshape(-1, P).T

    def head_col(g):
        return np.concatenate([g[:NOPE], np.ones(P - NOPE, np.float32)])[:, None]

    first_cols = np.stack([np.concatenate(
        [col(f["attn_norm_g"][l]), col(f["mla_q_norm_g"][l]), col(f["mla_kv_norm_g"][l]),
         head_col(f["mla_q_head_g"][l]), head_col(f["mla_k_head_g"][l]), col(f["pool_scale"][l]),
         col(f["ffn_norm_g"][l])] + [col(f["ffn_conv_w"][l, i]) for i in range(3)] + [col(f["ffn_conv_b"][l])], 1)
        for l in range(DEPTH)])
    first_rows = np.stack([np.concatenate(
        [f["mla_q_head_g"][l, NOPE:], f["mla_k_head_g"][l, NOPE:], f["gqa_q_head_g"][l], f["gqa_k_head_g"][l]])
        for l in range(DEPTH)])
    second_cols = np.stack([np.concatenate([col(f[n][l]) for n in ("g_mix_pre_2", "g_ffn_pre_2", "g_ple_2")], 1)
                            for l in range(DEPTH)])
    second_rows = np.stack([np.stack([f["g_mix_post_2"][l], f["g_ffn_post_2"][l]]) for l in range(DEPTH)])
    arrays = {
        "weights": flat, "x": f["x"][0], "first_cols": first_cols, "first_rows": first_rows,
        "pool_w": f["pool_w"].transpose(0, 2, 1, 3).reshape(DEPTH, P, POOL_G * P), "second_cols": second_cols,
        "second_rows": second_rows, "ple": f["p_2"][:, 0], "positions": f["positions_2"].reshape(TT, P).T,
        "consts": constants(),
    }
    return {k: np.ascontiguousarray(v) for k, v in arrays.items()}


def kernel(**inputs):
    import concourse.bacc as bacc
    from concourse.bass_utils import run_bass_kernel_spmd

    nc = bacc.Bacc("TRN2", target_bir_lowering=False, num_devices=1)
    arrays = pack(inputs)
    dram = {n: nc.dram_tensor("in_" + n, a.shape, mybir.dt.from_np(a.dtype), kind="ExternalInput").ap()
            for n, a in arrays.items()}
    out = nc.dram_tensor("out", (SEQ, D), F32, kind="ExternalOutput").ap()
    with ExitStack() as ctx:
        Program(nc, ctx, dram, out).build()
    got = run_bass_kernel_spmd(nc, [{"in_" + n: a for n, a in arrays.items()}], core_ids=[0]).results[0]["out"]
    return np.asarray(got).reshape(1, SEQ, D)
```

```python
from contextlib import ExitStack

import numpy as np

import concourse.bass as bass
from concourse import mybir

F32 = mybir.dt.float32
F32R = mybir.dt.float32r
I32 = mybir.dt.int32
ALU = mybir.AluOpType
ACT = mybir.ActivationFunctionType
AXIS_X = mybir.AxisListType.X

P = 128
SEQ = 256
TT = SEQ // P
D = 1024
DK = D // P
DEPTH = 2
EPS = 1e-6

MLA_H, Q_LORA, KV_LORA, NOPE, ROPE, MLA_V = 8, 256, 128, 64, 32, 64
MLA_QK = NOPE + ROPE
GQA_H, GQA_KV, HD = 8, 2, 64
POOL_WINDOWS = (2, 4, 8, 16)
POOL_G, POOL_W = 4, 512
D_FF = 2816
FT = D_FF // P
D_FF_2 = 4096
SB_H = 16
DIL = (1, 4, 16)
DIL_H, DIL_W = 8, 512
DIL_ROT = 16
PLE = 256
GRID_W = 64

PANEL = 512
UNIT = 1024
SPLIT_SLOTS = 4
RAW_SLOTS = 4
SPLIT_AHEAD = SPLIT_SLOTS - 1
MASKED = -1.0e30
POOL_PAD = max(POOL_WINDOWS) // 2



def panels_of(first, last, width=PANEL):
    return [(c, min(c + width, last)) for c in range(first, last, width)]


def weight_plan():
    plan = []
    c_mla = Q_LORA + KV_LORA + ROPE
    c_gqa = c_mla + (GQA_H + 2 * GQA_KV) * HD
    c_pool = c_gqa + POOL_W
    for l in range(DEPTH):
        plan += [
            ("proj", l, "w_in", D, [(0, c_mla)] + panels_of(c_mla, c_gqa) + [(c_gqa, c_pool)]),
            ("gates_early", l, "w_in", D, panels_of(c_pool, c_pool + PANEL)),
            ("up_q", l, "mla_w_uq", Q_LORA, panels_of(0, MLA_H * MLA_QK)),
            ("up_kv", l, "mla_w_ukv", KV_LORA, panels_of(0, MLA_H * (NOPE + MLA_V))),
            ("gates", l, "w_in", D, panels_of(c_pool + PANEL, c_pool + 3 * D)),
            ("branch_gqa", l, "w_branch_gqa", GQA_H * HD, panels_of(0, D)),
            ("branch_mla", l, "w_branch_mla", MLA_H * MLA_V, panels_of(0, D)),
            ("branch_pool", l, "w_branch_pool", POOL_W, panels_of(0, D)),
            ("out", l, "w_out", D, panels_of(0, D)),
            ("ffn_up", l, "ffn_w_up", D, [p for c0, c1 in panels_of(0, D_FF)
                                          for p in ((c0, c1), (D_FF + c0, D_FF + c1))]),
            ("ffn_down", l, "ffn_w_down", D_FF, panels_of(0, D)),
        ]
    for l in range(DEPTH):
        if l == 0:
            plan += [("sb_in", 0, "w_in_sb_2", D, panels_of(0, 3 * D)),
                     ("sb_out", 0, "w_out_sb_2", D, panels_of(0, D))]
        else:
            plan += [("dil_in", 0, "w_in_dil_2", D, panels_of(0, len(DIL) * 3 * DIL_W)),
                     ("dil_out", 0, "w_out_dil_2", DIL_W, panels_of(0, D))]
        plan += [("ff_in", l, "w_ff_in_2", D, panels_of(0, D_FF_2)),
                 ("ff_out", l, "w_ff_out_2", D_FF_2, panels_of(0, D)),
                 ("ple_up", l, "w_ple_2", PLE, panels_of(0, D)),
                 ("ple_gate", l, "w_ple_gate_2", D, panels_of(0, D))]
    return plan


def weight_units():
    units, loads, at = [], [], 0
    for name, layer, source, rows, panels in weight_plan():
        kts = rows // P
        own = []
        for n, (c0, c1) in enumerate(panels):
            w = c1 - c0
            step = max(1, min(kts, UNIT // w))
            for k0 in range(0, kts, step):
                own.append(dict(name=name, layer=layer, source=source, panel=n, c0=c0, w=w, k0=k0,
                                nk=min(step, kts - k0)))
        for i in range(0, len(own), 2):
            pair = own[i:i + 2]
            size = sum(u["w"] * u["nk"] for u in pair)
            inside = 0
            for u in pair:
                u["load"], u["inside"] = len(loads), inside
                inside += u["w"] * u["nk"]
            loads.append((at, size))
            at += P * size
        units += own
    return units, loads, at


FIRST_COLS, _n = {}, 0
for _name, _w in (("attn_g", DK), ("q_lora_g", 2), ("kv_lora_g", 1), ("q_head_g", 1), ("k_head_g", 1),
                  ("pool_scale", POOL_G), ("ffn_g", DK), ("conv_w", 3 * 2 * FT), ("conv_b", 2 * FT)):
    FIRST_COLS[_name] = (_n, _n + _w)
    _n += _w
N_FIRST_COLS = _n
SECOND_COLS, _n = {}, 0
for _name, _w in (("mix_g", DK), ("ffn_g", DK), ("ple_g", DK)):
    SECOND_COLS[_name] = (_n, _n + _w)
    _n += _w
N_SECOND_COLS = _n
ROW_QM, ROW_KM, ROW_QG, ROW_KG = (0, 32), (32, 64), (64, 128), (128, 192)
N_ROWS = 192

CONSTS, _n = {}, 0
for _name, _w in (("ident", P), ("not_below", P), ("ones", P), ("cos_m", TT * ROPE // 2),
                  ("sin_m", TT * ROPE // 2), ("cos_g", TT * HD // 2), ("sin_g", TT * HD // 2),
                  ("inv_freq", DIL_ROT // 2), ("pool_edge", POOL_G * 2 * POOL_PAD), ("sb_neg", 3 * P),
                  ("sb_add", 3 * P), ("dil_add", 9 * P)):
    CONSTS[_name] = (_n, _n + _w)
    _n += _w
N_CONSTS = _n
N_HELD = CONSTS["sb_neg"][0]


def constants():
    c = np.zeros((P, N_CONSTS), np.float32)

    def put(name, value):
        a, b = CONSTS[name]
        c[:, a:b] = np.asarray(value, np.float32).reshape(P, b - a)

    i = np.arange(P)
    put("ident", np.eye(P))
    put("not_below", i[:, None] >= i[None, :])
    put("ones", np.ones((P, P)))
    row, col = np.arange(SEQ) // GRID_W, np.arange(SEQ) % GRID_W
    for tag, rot in (("m", ROPE), ("g", HD)):
        n = rot // 4
        inv = (10000.0 ** (-np.arange(n) / n)).astype(np.float32)
        angle = np.concatenate([row[:, None].astype(np.float32) * inv, col[:, None].astype(np.float32) * inv], 1)
        for fn, f in (("cos_", np.cos), ("sin_", np.sin)):
            table = f(angle.astype(np.float64))
            put(fn + tag, table.reshape(TT, P, rot // 2).transpose(1, 0, 2))
    put("inv_freq", np.tile(500000.0 ** (-np.arange(0, DIL_ROT, 2) / DIL_ROT), (P, 1)))
    past = np.concatenate([i[:, None] < np.arange(SEQ)[None, :], i[:, None] < i[None, :]], 1)
    put("sb_neg", np.where(past, -1.0, 0.0))
    put("sb_add", np.where(past, 0.0, MASKED))
    parts = []
    for keys, q0 in ((P, 0), (SEQ, P)):
        for dil in DIL:
            dist = q0 + i[:, None] - np.arange(keys)[None, :]
            ok = (dist >= 0) & (dist % dil == 0) & (dist // dil <= P)
            parts.append(np.where(ok, 0.0, MASKED))
    put("dil_add", np.concatenate(parts, 1))
    t = np.concatenate([np.arange(POOL_PAD), np.arange(SEQ - POOL_PAD, SEQ)])
    edges = [w / (np.clip(t + w - w // 2, 0, SEQ) - np.clip(t - w // 2, 0, SEQ)) for w in POOL_WINDOWS]
    put("pool_edge", np.tile(np.concatenate(edges), (P, 1)))
    return c



class Engine:

    def __init__(self, done):
        self.done, self.count, self.steps, self.waited = done, 0, [], {}

    def wait(self, tokens):
        for token in tokens:
            if isinstance(token, list):
                self.wait(token)
            elif token is not None and self.waited.get(token[0].name, 0) < token[1]:
                self.waited[token[0].name] = token[1]
                self.steps.append((None, token, None, None))

    def run(self, op, *args, after=(), signal=True, **kw):
        self.wait(after)
        self.steps.append((op, args, kw, (self.done, 1) if signal else None))
        self.count += signal
        return (self.done, self.count) if signal else None

    def load(self, op, out, in_, done, count, after=()):
        self.wait(after)
        self.steps.append((op, (out, in_), {}, (done, 16)))
        return (done, count)

    def last(self):
        return (self.done, self.count) if self.count else None

    def play(self, eng):
        for op, args, kw, signal in self.steps:
            if op is None:
                eng.wait_ge(args[0], args[1])
            elif signal:
                op(*args, **kw).then_inc(*signal)
            else:
                op(*args, **kw)


class Program:
    def __init__(self, nc, ctx, dram, out):
        self.nc, self.ctx, self.dram, self.out = nc, ctx, dram, out
        self.pe, self.act, self.dve, self.pool, self.sp = (
            Engine(self.sem(n)) for n in ("pe_done", "act_done", "dve_done", "pool_done", "sp_done"))
        self.t, self.s, self.v, self.g = nc.tensor, nc.scalar, nc.vector, nc.gpsimd
        sb, ps = self.sb, self.ps
        self.consts = sb("consts", N_HELD)
        self.x = sb("residual", TT * D).rearrange("p (t n) -> p t n", t=TT)
        self.stat = sb("stat", 320)
        self.junk = [sb(f"squares{i}", PANEL) for i in range(TT)]
        self.r_row = sb("rstd_row", SEQ)
        self.diag = self.junk[0][:, 0:TT * P]
        self.half = sb("minus_half", 32)
        self.cols = sb("cols", DEPTH * (N_FIRST_COLS + N_SECOND_COLS))
        self.rows = sb("rows", D)
        self.raw = [sb(f"w_raw{i}", 2 * UNIT) for i in range(RAW_SLOTS)]
        self.wh = [sb(f"w_high{i}", UNIT, F32R) for i in range(SPLIT_SLOTS)]
        self.wl = [sb(f"w_low{i}", UNIT, F32R) for i in range(SPLIT_SLOTS)]
        self.xh = self.kt_view(sb("x_high", DK * SEQ, F32R))
        self.xl = self.kt_view(sb("x_low", DK * SEQ, F32R))
        self.scr = sb("scratch", 4 * UNIT)
        psum = ps("psum", 8 * PANEL)
        self.bank = [psum[:, i * PANEL:(i + 1) * PANEL] for i in range(8)]
        self.slot = [psum[:, 2 * i * PANEL:2 * (i + 1) * PANEL] for i in range(4)]
        self.free = {}
        self.units, self.loads, self.total = weight_units()
        self.raw_sem = [self.sem(f"w_loaded{i}") for i in range(RAW_SLOTS)]
        self.n_loaded = self.n_split = self.n_used = 0
        self.load_token, self.high_token, self.low_token, self.used_token = [], [], [], []
        self.later = []

    def sem(self, name):
        return self.ctx.enter_context(self.nc.semaphore(name))

    def sb(self, name, floats, dt=F32, ctx=None):
        return (ctx or self.ctx).enter_context(self.nc.sbuf_tensor(name, [P, floats], dt))[:, :]

    def ps(self, name, floats):
        return self.ctx.enter_context(self.nc.psum_tensor(name, [P, floats], F32))[:, :]

    def kt_view(self, ap):
        return ap.rearrange("p (k s) -> p k s", s=SEQ)

    def const(self, name):
        a, b = CONSTS[name]
        return self.consts[:, a:b]

    def small_load(self, name, out, in_, after=()):
        return self.sp.load(self.nc.sync.dma_start, out, in_, self.sem(name), 16, after)

    def fence(self):
        done = [e.last() for e in (self.pe, self.act, self.dve, self.pool)]
        for e in (self.act, self.dve, self.pool, self.sp):
            e.wait(done)

    def load_weights(self, n):
        at, size = self.loads[n]
        slot = n % RAW_SLOTS
        before = [u for u, unit in enumerate(self.units) if unit["load"] == n - RAW_SLOTS]
        src = self.dram["weights"][at:at + P * size].rearrange("(p n) -> p n", p=P)
        self.load_token.append(self.sp.load(
            self.nc.sync.dma_start, self.raw[slot][:, 0:size], src, self.raw_sem[slot],
            16 * (n // RAW_SLOTS + 1),
            after=[self.high_token[u] for u in before] + [self.low_token[u] for u in before]))

    def split_unit(self, n):
        u = self.units[n]
        size = u["w"] * u["nk"]
        slot = n % SPLIT_SLOTS
        raw = self.raw[u["load"] % RAW_SLOTS][:, u["inside"]:u["inside"] + size]
        left = self.used_token[n - SPLIT_SLOTS] if n >= SPLIT_SLOTS else None
        self.high_token.append(self.act.run(self.s.activation, self.wh[slot][:, 0:size], raw, ACT.Copy,
                                            after=[self.load_token[u["load"]], left]))
        self.low_token.append(self.dve.run(self.v.tensor_tensor, self.wl[slot][:, 0:size], raw,
                                           self.wh[slot][:, 0:size], ALU.subtract,
                                           after=[self.high_token[n], left]))

    def prefetch(self, n):
        last = min(n + SPLIT_AHEAD, len(self.units) - 1)
        while self.n_split <= last:
            reach = self.units[self.n_split]["load"] + RAW_SLOTS
            if self.n_split:
                reach = min(reach, self.units[self.n_split - 1]["load"] + RAW_SLOTS)
            while self.n_loaded < min(reach, len(self.loads)):
                self.load_weights(self.n_loaded)
                self.n_loaded += 1
            self.split_unit(self.n_split)
            self.n_split += 1

    def linear(self, name, layer, high, low, ready, feature_major, consume, slots=(0, 1)):
        kts = KTS[name]
        while self.n_used < len(self.units):
            n = self.n_used
            u = self.units[n]
            if (u["name"], u["layer"]) != (name, layer):
                break
            self.prefetch(n)
            w, held, slot = u["w"], n % SPLIT_SLOTS, slots[u["panel"] % len(slots)]
            acc = self.slot[slot]
            if u["k0"] == 0:
                self.pe.wait([self.free.get(2 * slot), self.free.get(2 * slot + 1)])
            by_feature = feature_major(u["panel"]) if callable(feature_major) else feature_major
            wh = self.wh[held][:, 0:w * u["nk"]].rearrange("p (k n) -> p k n", n=w)
            wl = self.wl[held][:, 0:w * u["nk"]].rearrange("p (k n) -> p k n", n=w)
            self.pe.wait([self.low_token[n]])
            for j in range(u["nk"]):
                k = u["k0"] + j
                ops = []
                end = k == kts - 1
                if by_feature:
                    for f in range(w // P):
                        cut = slice(f * P, (f + 1) * P)
                        o = acc[:, f * SEQ:(f + 1) * SEQ]
                        bank_start = k == 0 and f % 2 == 0
                        ops += [(o, wh[:, j, cut], high[:, k, :], bank_start, False),
                                (o, wh[:, j, cut], low[:, k, :], False, False),
                                (o, wl[:, j, cut], high[:, k, :], False, end)]
                else:
                    for t in range(TT):
                        cut = slice(t * P, (t + 1) * P)
                        o = acc[:, t * PANEL:t * PANEL + w]
                        ops += [(o, high[:, k, cut], wh[:, j, :], k == 0, False),
                                (o, high[:, k, cut], wl[:, j, :], False, False),
                                (o, low[:, k, cut], wh[:, j, :], False, end)]
                for i, (o, a, b, start, stop) in enumerate(ops):
                    token = self.pe.run(self.t.matmul, o, a, b, start=start, stop=stop, skip_group_check=True,
                                        after=[ready[k]], signal=j == u["nk"] - 1 and i == len(ops) - 1)
            self.used_token.append(token)
            self.n_used += 1
            for item in self.later:
                item[0] -= 1
            while self.later and self.later[0][0] <= 0:
                self.later.pop(0)[1]()
            if end:
                self.free[2 * slot] = self.free[2 * slot + 1] = consume(u["panel"], acc, w, token)
            yield

    def rstd(self, sums, n, count, out, after):
        t = self.pool.run(self.g.tensor_scalar, sums, sums, 1.0 / count, EPS, ALU.mult, ALU.add, after=after)
        return self.pool.run(self.g.tensor_tensor, out, sums, self.half[:, 0:n], ALU.pow, after=[t])

    def squares(self, src, half, sums):
        c = slice(half * PANEL, (half + 1) * PANEL)
        at = lambda t: sums[:, 2 * half + t:2 * half + t + 1]
        return [self.act.run(self.s.activation, self.junk[0], src[:, 0, c], ACT.Square, accum_out=at(0),
                             after=[self.act.last()]),
                self.dve.run(self.v.tensor_tensor_reduce, self.junk[1], src[:, 1, c], src[:, 1, c], 1.0, 0.0,
                             ALU.mult, ALU.add, at(1), after=[self.dve.last()])]

    def token_rstd(self, sums, out, after):
        s = sums[:, 0:2]
        t = self.pool.run(self.g.tensor_tensor, s, s, sums[:, 2:4], ALU.add,
                          after=[after, self.act.last(), self.dve.last()])
        return self.rstd(s, 2, D, out, [t])

    def to_features(self, src, kts, ready, high, low, gain=None, banks=(4, 5, 6, 7)):
        tokens = []
        for n in range(0, len(kts), 2):
            b = banks[(n // 2) % len(banks)]
            bank = self.bank[b]
            own = kts[n:n + 2]
            for i, k in enumerate(own):
                for t in range(TT):
                    at = i * SEQ + t * P
                    done = self.pe.run(self.t.transpose, bank[:, at:at + P], src[:, t, k * P:(k + 1) * P],
                                       self.const("ident"), after=[ready, self.free.get(b)])
            g = [gain[:, k:k + 1] if gain is not None else 1.0 for k in own]
            for i, k in enumerate(own):
                a = self.act.run(self.s.activation, high[:, k, :], bank[:, i * SEQ:(i + 1) * SEQ], ACT.Copy,
                                 scale=g[i], after=[done])
            for i, k in enumerate(own):
                d = self.dve.run(self.v.scalar_tensor_tensor, low[:, k, :], bank[:, i * SEQ:(i + 1) * SEQ], g[i],
                                 high[:, k, :], ALU.mult, ALU.subtract, after=[a])
                tokens.append(d)
            self.free[b] = [a, d]
        return tokens

    def half_done(self, half, token, gain, scaled, banks):
        sums, r = self.stat[:, 0:4], self.stat[:, 4:6]
        self.act.wait([token])
        self.sums_done += self.squares(self.x, half, sums)
        ks = list(range(4 * half, 4 * half + 4))
        if half:
            self.r_ready = self.token_rstd(sums, r, self.sums_done)
        if not scaled:
            self.features += self.to_features(self.x, ks, [token], self.xh, self.xl, gain, banks)
            return
        if half:
            xn = self.scr[:, 0:TT * D].rearrange("p (t n) -> p t n", t=TT)
            for h in range(2):
                c = slice(h * PANEL, (h + 1) * PANEL)
                a = self.act.run(self.s.activation, xn[:, 0, c], self.x[:, 0, c], ACT.Copy, scale=r[:, 0:1],
                                 after=[self.r_ready, self.dve.last()])
                d = self.dve.run(self.v.tensor_scalar, xn[:, 1, c], self.x[:, 1, c], r[:, 1:2], None, ALU.mult,
                                 after=[self.r_ready, self.act.last()])
                self.features += self.to_features(xn, list(range(4 * h, 4 * h + 4)), [a, d], self.xh, self.xl, gain,
                                                  banks)

    def start_features(self):
        self.features, self.sums_done = [], []

    def residual_add(self, gain, scaled=False, banks=(4, 5, 6, 7)):
        self.start_features()

        def take(panel, acc, w, done):
            c = slice(panel * PANEL, panel * PANEL + w)
            got = acc.rearrange("p (t n) -> p t n", t=TT)
            for t in range(TT):
                token = self.dve.run(self.v.tensor_tensor, self.x[:, t, c], self.x[:, t, c], got[:, t, 0:w], ALU.add,
                                     after=[done])
            self.x_ready = token
            step = lambda: self.half_done(panel, token, gain, scaled, banks)
            if panel:
                step()
            else:
                self.later.append([2, step])
            return [token]
        return take

    def scale_row(self, after):
        for t in range(TT):
            d = self.dve.run(self.v.tensor_scalar, self.diag[:, t * P:(t + 1) * P], self.const("ident"),
                             self.stat[:, 4 + t:5 + t], None, ALU.mult, after=[after, self.pe.last(), self.free.get("row")])
        for t in range(TT):
            done = self.pe.run(self.t.matmul, self.bank[7][:, t * P:(t + 1) * P], self.const("ones"),
                               self.diag[:, t * P:(t + 1) * P], start=True, stop=True, after=[d, self.free.get(7)])
        e = self.act.run(self.s.activation, self.r_row, self.bank[7][:, 0:SEQ], ACT.Copy, after=[done, self.dve.last()])
        self.free[7] = [e]
        self.row_ready = e
        return self.r_row.rearrange("p (o s) -> p o s", o=1)

    def head_scale(self, tile, heads, width, after, place=0):
        n = TT * heads
        sq = self.scr[:, 0:n * width].rearrange("p (t h d) -> p t h d", t=TT, h=heads)
        s = self.stat[:, 16 + 48 * place:16 + 48 * place + n]
        a = self.dve.run(self.v.tensor_tensor, sq, tile, tile, ALU.mult, after=[after, self.dve.last()])
        a = self.dve.run(self.v.tensor_reduce, s.rearrange("p (t h) -> p t h", t=TT), sq, AXIS_X, ALU.add, after=[a])
        r = self.stat[:, 40 + 48 * place:40 + 48 * place + n]
        a = self.rstd(s, n, width, r, [a])
        yield
        rb = r.rearrange("p (t h o) -> p t h o", t=TT, o=1).to_broadcast([P, TT, heads, width])
        yield self.dve.run(self.v.tensor_tensor, tile, tile, rb, ALU.mult, after=[a])

    def rope_tables(self, tag, rot, gain, out, after):
        h = rot // 2
        for i, (fn, side) in enumerate((("cos_", 0), ("sin_", 1), ("sin_", 0), ("cos_", 1))):
            table = self.const(fn + tag).rearrange("p (t n) -> p t n", t=TT)
            g = gain[:, side * h:(side + 1) * h].rearrange("p (o n) -> p o n", o=1).to_broadcast([P, TT, h])
            o = out[:, i * TT * h:(i + 1) * TT * h].rearrange("p (t n) -> p t n", t=TT)
            t = self.dve.run(self.v.tensor_tensor, o, table, g, ALU.mult, after=after)
        return t

    def rotate(self, tile, heads, at, rot, tables, after, outs=None):
        h = rot // 2
        n = TT * heads * h
        x1, x2 = tile[:, :, :, at:at + h], tile[:, :, :, at + h:at + rot]
        tmp = [self.scr[:, 2 * UNIT + i * n:2 * UNIT + (i + 1) * n].rearrange("p (t h d) -> p t h d", t=TT, h=heads)
               for i in range(4)]
        assert 2 * UNIT + 4 * n <= 4 * UNIT
        after = [after, self.dve.last()]
        for i, (x, o) in enumerate(zip((x1, x2, x1, x2), tmp)):
            tb = tables[:, i * TT * h:(i + 1) * TT * h].rearrange("p (t o n) -> p t o n", t=TT, o=1)
            t = self.dve.run(self.v.tensor_tensor, o, x, tb.to_broadcast([P, TT, heads, h]), ALU.mult, after=after)
        for out in outs or [tile]:
            a = self.dve.run(self.v.tensor_tensor, out[:, :, :, at:at + h], tmp[0], tmp[1], ALU.subtract, after=[t])
            b = self.dve.run(self.v.tensor_tensor, out[:, :, :, at + h:at + rot], tmp[2], tmp[3], ALU.add, after=[t])
        return b

    def head_attention(self, n, h, q, k, v, scale, oh, ol, work, ready, tokens):
        sb, pt_bank, o_bank = 4 + n % 2, 6, 7
        b, c = n % 3, n % 2
        s_bank = self.bank[sb]
        st = self.stat[:, 128 + 16 * b:144 + 16 * b]
        prob, probt = work[b], work[3 + c]
        for t in range(TT):
            done = self.pe.run(self.t.matmul, s_bank[:, t * SEQ:(t + 1) * SEQ], q[:, t * P:(t + 1) * P], k,
                               start=True, stop=True, after=[ready, self.free.get(sb)], signal=t == TT - 1)
        a = self.dve.run(self.v.tensor_reduce, st[:, 0:2], s_bank.rearrange("p (t k) -> p t k", t=TT), AXIS_X,
                         ALU.max, after=[done, self.free.get(("stat", b))])
        a = self.dve.run(self.v.tensor_scalar, st[:, 2:4], st[:, 0:2], -scale, None, ALU.mult, after=[a])
        for t in range(TT):
            e = self.act.run(self.s.activation, prob[:, t * SEQ:(t + 1) * SEQ], s_bank[:, t * SEQ:(t + 1) * SEQ],
                             ACT.Exp, bias=st[:, 2 + t:3 + t], scale=scale, accum_out=st[:, 4 + t:5 + t],
                             after=[a, self.free.get(("prob", b))])
        self.free[sb] = [a, e]
        yield
        a = self.dve.run(self.v.reciprocal, st[:, 6:8], st[:, 4:6], after=[e])
        for t in range(TT):
            p = prob[:, t * SEQ:(t + 1) * SEQ]
            m = self.dve.run(self.v.tensor_scalar, p, p, st[:, 6 + t:7 + t], None, ALU.mult, after=[a])
        self.free[("stat", b)] = m
        yield
        for kt in range(TT):
            for t in range(TT):
                done = self.pe.run(self.t.transpose,
                                   self.bank[pt_bank][:, kt * SEQ + t * P:kt * SEQ + (t + 1) * P],
                                   prob[:, t * SEQ + kt * P:t * SEQ + (kt + 1) * P], self.const("ident"),
                                   after=[m, self.free.get(pt_bank)])
        self.free[("prob", b)] = done
        e = self.act.run(self.s.activation, probt, self.bank[pt_bank], ACT.Copy,
                         after=[done, self.free.get(("probt", c))])
        self.free[pt_bank] = [e]
        yield
        at = HD * (h % 2)
        for kt in range(TT):
            done = self.pe.run(self.t.matmul, self.bank[o_bank][at:at + HD, 0:SEQ], v(kt),
                               probt[:, kt * SEQ:(kt + 1) * SEQ], start=kt == 0, stop=kt == TT - 1,
                               after=[e, self.free.get(o_bank)], signal=kt == TT - 1)
        self.free[("probt", c)] = done
        if h % 2:
            self.free[o_bank] = self.split_out(self.bank[o_bank][:, 0:SEQ], h // 2, oh, ol, done)
            tokens.append(self.free[o_bank][1])

    def split_out(self, got, k, oh, ol, done, scale=1.0):
        a = self.act.run(self.s.activation, oh[:, k, :], got, ACT.Copy, scale=scale, after=[done])
        d = self.dve.run(self.v.scalar_tensor_tensor, ol[:, k, :], got, scale, oh[:, k, :], ALU.mult,
                         ALU.subtract, after=[done, a])
        return [a, d]

    def transpose_pairs(self, src, blocks, rows, out, done, scale=None, free=None, banks=(4, 5)):
        for n in range(0, blocks, 2):
            b = banks[(n // 2) % len(banks)]
            self.pe.wait([self.free.get(b)])
            for i in range(2):
                for t in range(TT):
                    at = i * SEQ + t * P
                    d = self.pe.run(self.t.transpose, self.bank[b][0:rows, at:at + P], src(n + i, t),
                                    self.const("ident"), after=done)
            got = self.bank[b][0:rows, :].rearrange("p (k s) -> p k s", k=2)
            g = scale[0:rows, :] if scale is not None else 1.0
            if (n // 2) % 2:
                e = self.act.run(self.s.activation, out[0:rows, n:n + 2, :], got, ACT.Copy, scale=g, after=[d, free])
            else:
                e = self.dve.run(self.v.tensor_scalar, out[0:rows, n:n + 2, :], got, g, None, ALU.mult, after=[d, free])
            self.free[b] = [e]
        return [self.free[b] for b in banks]

    def first_col(self, l, name):
        a, b = FIRST_COLS[name]
        return self.cols[:, l * N_FIRST_COLS + a:l * N_FIRST_COLS + b]

    def second_col(self, l, name):
        a, b = SECOND_COLS[name]
        at = DEPTH * N_FIRST_COLS + l * N_SECOND_COLS
        return self.cols[:, at + a:at + b]

    def first_mixing(self, l):
        v, s, g = self.v, self.s, self.g
        cols = lambda name: self.first_col(l, name)
        ready = self.features
        r = [self.stat[:, 4 + t:5 + t] for t in range(TT)]
        with ExitStack() as ctx:
            sb = lambda name, floats, dt=F32: self.sb(f"{name}_{l}", floats, dt, ctx)
            gates = self.kt_view(sb("gates", 3 * DK * SEQ))
            tok = sb("mla_tokens", 2 * TT * MLA_H * MLA_QK)
            n = TT * MLA_H * MLA_QK
            mq, mk = (tok[:, i * n:(i + 1) * n].rearrange("p (t h d) -> p t h d", t=TT, h=MLA_H) for i in range(2))
            qk = self.kt_view(sb("mla_heads", 2 * MLA_H * SEQ))
            gh = self.kt_view(sb("gqa_heads", (GQA_H // 2 + GQA_KV) * SEQ))
            mv = sb("mla_v", TT * MLA_H * MLA_V).rearrange("p (t h d) -> p t h d", t=TT, h=MLA_H)
            gqk = sb("gqa_tokens", TT * (GQA_H + GQA_KV) * HD).rearrange("p (t h d) -> p t h d", t=TT, d=HD)
            gv = sb("gqa_v", TT * GQA_KV * HD).rearrange("p (t n) -> p t n", t=TT)
            n_c = Q_LORA + KV_LORA + ROPE
            c = sb("compressed", TT * n_c).rearrange("p (t n) -> p t n", t=TT)
            pw = SEQ + 2 * POOL_PAD
            pp = sb("pool_in", POOL_G * pw).rearrange("p (g n) -> p g n", g=POOL_G)
            mixh = self.kt_view(sb("mixed_high", DK * SEQ, F32R))
            mixl = self.kt_view(sb("mixed_low", DK * SEQ, F32R))
            gqa_h, gqa_l, mla_h, mla_l = mixh[:, 0:4, :], mixl[:, 0:4, :], mixh[:, 4:8, :], mixl[:, 4:8, :]
            work = sb("head_work", 4 * PANEL)
            work = [work[:, i * PANEL:(i + 1) * PANEL] for i in range(4)] + [self.scr[:, 3 * PANEL:4 * PANEL]]
            tab = sb("rope_tables", 2 * 4 * TT * (ROPE + HD) // 2)
            tq, tk = tab[:, 0:128], tab[:, 128:256]
            tgq, tgk = tab[:, 256:512], tab[:, 512:768]
            pool_w = self.rows[:, 0:POOL_G * P].rearrange("p (g n) -> p g n", g=POOL_G)
            rows = self.rows[:, POOL_G * P:POOL_G * P + N_ROWS]

            self.fence()
            rows_loaded = self.small_load(f"rows_loaded_{l}", rows, self.dram["first_rows"][l].partition_broadcast(P))
            pool_w_loaded = self.small_load(f"pool_w_loaded_{l}", pool_w,
                                            self.dram["pool_w"][l].rearrange("p (g n) -> p g n", g=POOL_G))
            row = self.scale_row([self.r_ready])
            pads = [self.pool.run(g.memset, pp[:, :, a:a + POOL_PAD], 0.0) for a in (0, POOL_PAD + SEQ)]
            got = {}

            def scaled(out, part, done, extra=None):
                for t in range(TT):
                    e = self.act.run(s.activation, out[:, t], part[:, t], ACT.Copy, scale=r[t],
                                     after=[done, self.r_ready, extra])
                return e

            def take(panel, acc, w, done):
                a = acc.rearrange("p (t n) -> p t n", t=TT)
                if panel == 0:
                    got["c"] = scaled(c, a[:, :, 0:w], done)
                    return [got["c"]]
                if panel == 1:
                    got["gq"] = scaled(gqk[:, :, 0:GQA_H, :], a.rearrange("p t (h d) -> p t h d", d=HD), done)
                    return [got["gq"]]
                if panel == 2:
                    n_k = GQA_KV * HD
                    scaled(gqk[:, :, GQA_H:, :], a[:, :, 0:n_k].rearrange("p t (h d) -> p t h d", d=HD), done)
                    got["gqa"] = scaled(gv, a[:, :, n_k:2 * n_k], done)
                    return [got["gqa"]]
                got["pool"] = self.dve.run(v.tensor_tensor, pp[:, :, POOL_PAD:POOL_PAD + SEQ],
                                           acc.rearrange("p (g s) -> p g s", g=POOL_G),
                                           row.to_broadcast([P, POOL_G, SEQ]), ALU.mult, after=[done, pads, self.row_ready])
                return [got["pool"]]

            run_all(self.linear("proj", l, self.xh, self.xl, ready, lambda p: p == 3, take, (0, 1, 2)))

            def early():
                n_n = Q_LORA + KV_LORA
                sq = self.scr[:, 0:TT * n_n].rearrange("p (t n) -> p t n", t=TT)
                t1 = self.dve.run(v.tensor_tensor, sq, c[:, :, 0:n_n], c[:, :, 0:n_n], ALU.mult, after=[got["c"]])
                st, rr = self.stat[:, 300:304], self.stat[:, 304:308]
                self.dve.run(v.tensor_reduce, st[:, 0:2], sq[:, :, 0:Q_LORA], AXIS_X, ALU.add, after=[t1])
                t2 = self.dve.run(v.tensor_reduce, st[:, 2:4], sq[:, :, Q_LORA:n_n], AXIS_X, ALU.add, after=[t1])
                self.pool.run(g.tensor_scalar, st[:, 0:2], st[:, 0:2], 1.0 / Q_LORA, EPS, ALU.mult, ALU.add, after=[t2])
                t3 = self.pool.run(g.tensor_scalar, st[:, 2:4], st[:, 2:4], 1.0 / KV_LORA, EPS, ALU.mult, ALU.add)
                t4 = self.pool.run(g.tensor_tensor, rr, st, self.half[:, 0:4], ALU.pow, after=[t3])
                for tag, rot, at, out in (("m", ROPE, ROW_QM, tq), ("m", ROPE, ROW_KM, tk), ("g", HD, ROW_QG, tgq),
                                          ("g", HD, ROW_KG, tgk)):
                    self.rope_tables(tag, rot, rows[:, at[0]:at[1]], out, [rows_loaded])
                scale = self.head_scale(gqk, GQA_H + GQA_KV, HD, [got["gqa"], got["gq"]])
                next(scale)
                for i, (c0, c1) in enumerate(((0, Q_LORA), (Q_LORA, n_n))):
                    rb = rr[:, 2 * i:2 * i + 2].rearrange("p (t o) -> p t o", o=1).to_broadcast([P, TT, c1 - c0])
                    t5 = self.dve.run(v.tensor_tensor, c[:, :, c0:c1], c[:, :, c0:c1], rb, ALU.mult, after=[t4])
                yield
                a, b = FIRST_COLS["q_lora_g"][0], FIRST_COLS["kv_lora_g"][1]
                gain = self.cols[:, l * N_FIRST_COLS + a:l * N_FIRST_COLS + b]
                got["lora"] = self.to_features(c, [0, 1, 2], [t5], gqa_h, gqa_l, gain, (4, 5))
                tmp = [tok[:, 512 + i * POOL_G * pw:512 + (i + 1) * POOL_G * pw].rearrange("p (g n) -> p g n", g=POOL_G)
                       for i in range(2)]
                t = self.pool.run(g.tensor_tensor, tmp[0][:, :, 1:pw], pp[:, :, 0:pw - 1], pp[:, :, 1:pw], ALU.add,
                                  after=[got["pool"]])
                sums = [tmp[0]]
                for n in range(1, POOL_G):
                    d = 2 ** (n - 1)
                    lo, hi = 2 * d, pw - 2 * d + 1
                    t = self.pool.run(g.tensor_tensor, tmp[n % 2][:, n:, lo:hi], sums[-1][:, n:, lo - d:hi - d],
                                      sums[-1][:, n:, lo + d:hi + d], ALU.add, after=[t])
                    sums.append(tmp[n % 2])
                edge = self.const("pool_edge").rearrange("p (g n) -> p g n", g=POOL_G)
                for n in range(POOL_G):
                    for at, c0 in ((POOL_PAD, 0), (SEQ, POOL_PAD)):
                        part = sums[n][:, n, at:at + POOL_PAD]
                        t = self.pool.run(g.tensor_tensor, part, part, edge[:, n, c0:c0 + POOL_PAD], ALU.mult, after=[t])
                for n, w in enumerate(POOL_WINDOWS):
                    part = pp[:, n, POOL_PAD:POOL_PAD + SEQ]
                    t1 = self.pool.run(g.tensor_scalar, sums[n][:, n, POOL_PAD:POOL_PAD + SEQ],
                                       sums[n][:, n, POOL_PAD:POOL_PAD + SEQ], 1.0 / w, None, ALU.mult, after=[t])
                    t = self.pool.run(g.tensor_tensor, part, sums[n][:, n, POOL_PAD:POOL_PAD + SEQ], part, ALU.subtract,
                                      after=[t1])
                got["mixed"] = t
                yield
                kd = tok[:, 0:2 * TT * GQA_KV * HD].rearrange("p (t g u d) -> p t g u d", t=TT, g=GQA_KV, u=2)
                t = next(scale)
                tq_ready = self.rotate(gqk[:, :, 0:GQA_H, :], GQA_H, 0, HD, tgq, [t])
                yield
                tk_ready = self.rotate(gqk[:, :, GQA_H:, :], GQA_KV, 0, HD, tgk, [t],
                                       outs=[kd[:, :, :, u, :] for u in range(2)])
                flat = gqk.rearrange("p t h d -> p t (h d)")
                yield
                a = self.transpose_pairs(lambda n, t: flat[:, t, n * P:(n + 1) * P], GQA_H // 2, P, gh[:, 0:4, :], [tq_ready])
                b = self.transpose_pairs(lambda n, t: kd[:, t, n, :, :], GQA_KV, P, gh[:, 4:6, :], [tk_ready], banks=(4,))
                got["gqa_turned"] = [a, b]
                got["tokens_free"] = [self.pe.last(), got["mixed"]]

            def take_gates(first):
                def take(panel, acc, w, done):
                    part = gates[:, 4 * (panel + first):4 * (panel + first) + 4, :]
                    got["gates"] = self.dve.run(v.tensor_tensor, part, self.kt_view(acc), row.to_broadcast([P, 4, SEQ]),
                                                ALU.mult, after=[done, self.row_ready])
                    return [got["gates"]]
                return take

            interleave(early(), self.linear("gates_early", l, self.xh, self.xl, ready, True, take_gates(0), (3,)), 1)

            mq_flat = mq.rearrange("p t h d -> p t (h d)")

            def take_q(panel, acc, w, done):
                a = acc.rearrange("p (t n) -> p t n", t=TT)[:, :, 0:w]
                got["mq"] = self.act.run(s.activation, mq_flat[:, :, panel * PANEL:panel * PANEL + w], a, ACT.Copy,
                                         after=[done, got["tokens_free"]])
                return [got["mq"]]

            def take_kv(panel, acc, w, done):
                hp = w // (NOPE + MLA_V)
                a = acc.rearrange("p (t h d) -> p t h d", t=TT, d=NOPE + MLA_V)
                hs = slice(panel * hp, (panel + 1) * hp)
                got["mk"] = self.act.run(s.activation, mk[:, :, hs, 0:NOPE], a[:, :, :, 0:NOPE], ACT.Copy,
                                         after=[done, got["tokens_free"]])
                got["mv"] = self.act.run(s.activation, mv[:, :, hs, :], a[:, :, :, NOPE:], ACT.Copy)
                return [got["mv"]]

            lora = got["lora"]
            run_all(self.linear("up_q", l, gqa_h, gqa_l, lora, False, take_q, (0, 1)))
            run_all(self.linear("up_kv", l, gqa_h[:, 2:3, :], gqa_l[:, 2:3, :], lora[2:], False, take_kv, (0, 1)))

            def mla_heads():
                kr = c[:, :, Q_LORA + KV_LORA:].rearrange("p t (o d) -> p t o d", o=1).to_broadcast([P, TT, MLA_H, ROPE])
                t = self.dve.run(v.tensor_copy, mk[:, :, :, NOPE:], kr, after=[got["tokens_free"]])
                scale_k = self.head_scale(mk, MLA_H, MLA_QK, [t, got["mk"]])
                next(scale_k)
                yield
                scale_q = self.head_scale(mq, MLA_H, MLA_QK, [got["mq"]], 1)
                next(scale_q)
                yield
                tk_ready = self.rotate(mk, MLA_H, NOPE, ROPE, tk, [next(scale_k)])
                yield
                tq_ready = self.rotate(mq, MLA_H, NOPE, ROPE, tq, [next(scale_q)])
                yield
                a = self.transpose_pairs(lambda h, t: mk[:, t, h, :], MLA_H, MLA_QK, qk[:, MLA_H:, :], [tk_ready],
                                         cols("k_head_g"))
                yield
                b = self.transpose_pairs(lambda h, t: mq[:, t, h, :], MLA_H, MLA_QK, qk[:, 0:MLA_H, :], [tq_ready],
                                         cols("q_head_g"))
                got["mla_turned"] = [a, b]

            gqa_tokens, mla_tokens = [], []
            prepare = mla_heads()

            def heads():
                rep = GQA_H // GQA_KV
                for h in range(GQA_H):
                    half = slice(HD * (h % 2), HD * (h % 2) + HD)
                    yield self.head_attention(h, h, gh[half, h // 2, :], gh[half, 4 + h // rep, :],
                                              lambda kt, h=h: gv[:, kt, HD * (h // rep):HD * (h // rep) + HD],
                                              HD ** -0.5, gqa_h, gqa_l, work, [got["gqa_turned"], got["gqa"]], gqa_tokens)
                run_all(prepare)
                for h in range(MLA_H):
                    yield self.head_attention(GQA_H + h, h, qk[0:MLA_QK, h, :], qk[0:MLA_QK, MLA_H + h, :],
                                              lambda kt, h=h: mv[:, kt, h, :], MLA_QK ** -0.5, mla_h, mla_l, work,
                                              [got["mla_turned"], got["mv"]], mla_tokens)

            def rounds():
                for _ in pipelined(heads()):
                    advance(prepare)
                    yield

            interleave(rounds(), self.linear("gates", l, self.xh, self.xl, ready, True, take_gates(1), (0, 1)), 1)
            for b in range(3):
                part = gates[:, b * DK:(b + 1) * DK, :]
                got["gate", b] = self.act.run(s.activation, part, part, ACT.Sigmoid, after=[got["gates"]])

            def gated(b):
                def take(panel, acc, w, done):
                    part = gates[:, b * DK + 4 * panel:b * DK + 4 * panel + 4, :]
                    got["merged", b, panel] = self.dve.run(v.tensor_tensor, part, part, self.kt_view(acc), ALU.mult,
                                                           after=[done, got["gate", b]])
                    return [got["merged", b, panel]]
                return take

            run_all(self.linear("branch_gqa", l, gqa_h, gqa_l, gqa_tokens, True, gated(1), (0, 1)))
            tokens = []
            for n in range(POOL_G):
                b = 4 + n
                done = self.pe.run(self.t.matmul, self.bank[b][:, 0:SEQ], pool_w[:, n, :],
                                   pp[:, n, POOL_PAD:POOL_PAD + SEQ], start=True, stop=True,
                                   after=[got["mixed"], pool_w_loaded, self.free.get(b)])
                self.free[b] = self.split_out(self.bank[b][:, 0:SEQ], n, gqa_h, gqa_l, done, cols("pool_scale")[:, n:n + 1])
                tokens.append(self.free[b][1])
            run_all(self.linear("branch_mla", l, mla_h, mla_l, mla_tokens, True, gated(0), (0, 1)))
            run_all(self.linear("branch_pool", l, gqa_h, gqa_l, tokens, True, gated(2), (2, 3)))

            ready = []
            for i in range(2):
                ks = slice(4 * i, 4 * i + 4)
                m, m1, m2 = (gates[:, j * DK + 4 * i:j * DK + 4 * i + 4, :] for j in range(3))
                t = self.dve.run(v.tensor_tensor, m, m, m1, ALU.add, after=[got["merged", 1, i], got["merged", 0, i]])
                t = self.dve.run(v.tensor_tensor, m, m, m2, ALU.add, after=[t, got["merged", 2, i]])
                for k in range(0, 4, 2):
                    kk = slice(4 * i + k, 4 * i + k + 2)
                    a = self.act.run(s.activation, mixh[:, kk, :], m[:, k:k + 2, :], ACT.Copy, after=[t, self.pe.last()])
                    d = self.dve.run(v.tensor_tensor, mixl[:, kk, :], m[:, k:k + 2, :], mixh[:, kk, :], ALU.subtract, after=[a])
                    ready += [d] * 2
            run_all(self.linear("out", l, mixh, mixl, ready, False, self.residual_add(cols("ffn_g"), scaled=True), (0, 1)))

    def first_ffn(self, l):
        v, s = self.v, self.s
        cols = lambda name: self.first_col(l, name)
        ready = self.features
        with ExitStack() as ctx:
            ah = self.kt_view(self.sb(f"ffn_high_{l}", FT * SEQ, F32R, ctx))
            al = self.kt_view(self.sb(f"ffn_low_{l}", FT * SEQ, F32R, ctx))
            self.fence()
            conv_w, conv_b = cols("conv_w"), cols("conv_b")
            acts = []

            def take(panel, acc, w, done):
                pair, value = panel // 2, panel % 2
                buf = self.scr[:, (pair % 2) * 2 * UNIT:(pair % 2 + 1) * 2 * UNIT]
                o = self.kt_view(buf[:, value * UNIT:value * UNIT + w * TT])
                u = self.kt_view(acc)
                readers = []
                def tap(i, f):
                    ft = i * 2 * FT + value * FT + pair * (PANEL // P) + f
                    return conv_w[:, ft:ft + 1]
                for bank in range(w // (2 * P)):
                    fs = (2 * bank, 2 * bank + 1)
                    for f in fs:
                        ft = value * FT + pair * (PANEL // P) + f
                        a = self.act.run(s.activation, o[:, f, :], u[:, f, :], ACT.Identity, scale=tap(1, f),
                                         bias=conv_b[:, ft:ft + 1], after=[done, self.free.get(("conv", pair % 2))])
                    for f in fs:
                        d = self.dve.run(v.scalar_tensor_tensor, o[:, f, 1:], u[:, f, 0:SEQ - 1], tap(0, f),
                                         o[:, f, 1:], ALU.mult, ALU.add, after=[done, a])
                    for f in fs:
                        d = self.dve.run(v.scalar_tensor_tensor, o[:, f, 0:SEQ - 1], u[:, f, 1:], tap(2, f),
                                         o[:, f, 0:SEQ - 1], ALU.mult, ALU.add, after=[d])
                    readers += [a, d]
                if value:
                    n = w * TT
                    gate, val = buf[:, 0:n], buf[:, UNIT:UNIT + n]
                    a = self.act.run(s.activation, gate, gate, ACT.Silu, after=[d])
                    m = self.dve.run(v.tensor_tensor, gate, gate, val, ALU.mult, after=[a])
                    ks = slice(pair * 4, pair * 4 + w // P)
                    a = self.act.run(s.activation, ah[:, ks, :], self.kt_view(gate), ACT.Copy, after=[m])
                    d = self.dve.run(v.tensor_tensor, al[:, ks, :], self.kt_view(gate), ah[:, ks, :], ALU.subtract, after=[a])
                    self.free[("conv", pair % 2)] = d
                    acts.extend([d] * (w // P))
                return readers

            run_all(self.linear("ffn_up", l, self.xh, self.xl, ready, True, take, (0, 1, 2, 3)))
            gain = self.first_col(l + 1, "attn_g") if l + 1 < DEPTH else self.second_col(0, "mix_g")
            run_all(self.linear("ffn_down", l, ah, al, acts, False, self.residual_add(gain), (0, 1)))

    def post_norm(self, gain, banks):
        sums, r = self.stat[:, 8:12], self.stat[:, 12:14]
        held, squared = [], []

        def take(panel, acc, w, done):
            held.append(acc.rearrange("p (t n) -> p t n", t=TT))
            for t in range(TT):
                squared.append(self.act.run(self.s.activation, self.junk[t], held[-1][:, t, 0:w], ACT.Square,
                                            accum_out=sums[:, 2 * panel + t:2 * panel + t + 1],
                                            after=[done, self.free.get(("junk", t))]))
                self.free["junk", t] = squared[-1]
            return [squared[-1]]

        def finish(slots):
            ready = self.token_rstd(sums, r, squared)
            self.start_features()
            for half in range(2):
                c = slice(half * PANEL, (half + 1) * PANEL)
                y = self.scr[:, half * UNIT:(half + 1) * UNIT].rearrange("p (t n) -> p t n", t=TT)
                for t in range(TT):
                    d = self.dve.run(self.v.scalar_tensor_tensor, y[:, t, :], held[half][:, t, :], r[:, t:t + 1],
                                     self.rows[:, c], ALU.mult, ALU.mult, after=[ready, self.rows_ready, self.dve.last()])
                for b in (2 * slots[half], 2 * slots[half] + 1):
                    self.free[b] = [d]
                for t in range(TT):
                    d = self.dve.run(self.v.tensor_tensor, self.x[:, t, c], self.x[:, t, c], y[:, t, :], ALU.add,
                                     after=[self.dve.last()])
                self.x_ready = d
                self.half_done(half, d, gain, False, banks)
        return take, finish

    def stick_breaking(self, l):
        v, s = self.v, self.s
        ready = self.features
        with ExitStack() as ctx:
            sb = lambda name, floats, dt=F32: self.sb(f"{name}_{l}", floats, dt, ctx)
            q, k = self.kt_view(sb("sb_q", DK * SEQ)), self.kt_view(sb("sb_k", DK * SEQ))
            val = sb("sb_v", TT * D).rearrange("p (t n) -> p t n", t=TT)
            oh, ol = self.kt_view(sb("sb_out_high", DK * SEQ, F32R)), self.kt_view(sb("sb_out_low", DK * SEQ, F32R))
            NZ = 3 * P
            masks = sb("sb_masks", 2 * NZ)
            weights = [sb(f"sb_weights{i}", 2 * NZ).rearrange("p (j n) -> p j n", j=2) for i in range(2)]
            part = lambda i: self.scr[:, i * 2 * NZ:(i + 1) * 2 * NZ].rearrange("p (j n) -> p j n", j=2)
            softs, fails = [part(i) for i in range(3)], [part(i) for i in range(3, 5)]
            self.fence()
            self.rows_ready = self.small_load(f"mix_gain_loaded_{l}", self.rows,
                                              self.dram["second_rows"][l, 0].partition_broadcast(P))
            at = CONSTS["sb_neg"][0]
            masks_loaded = self.small_load("sb_masks_loaded", masks, self.dram["consts"][:, at:at + 2 * NZ])
            row = self.scale_row([self.r_ready])
            r = [self.stat[:, 4 + t:5 + t] for t in range(TT)]
            got = {}

            def take(panel, acc, w, done):
                part = slice(4 * (panel % 2), 4 * (panel % 2) + 4)
                if panel < 4:
                    t = self.dve.run(v.scalar_tensor_tensor, (q if panel < 2 else k)[:, part, :], self.kt_view(acc),
                                     HD ** -0.5 if panel < 2 else 1.0, row.to_broadcast([P, 4, SEQ]), ALU.mult, ALU.mult,
                                     after=[done, self.row_ready])
                    got["qk"] = t
                    return [t]
                c = (panel - 4) * PANEL
                a = acc.rearrange("p (t n) -> p t n", t=TT)
                for t in range(TT):
                    got["v"] = self.act.run(s.activation, val[:, t, c:c + w], a[:, t], ACT.Copy, scale=r[t],
                                            after=[done, self.r_ready])
                return [got["v"]]

            run_all(self.linear("sb_in", l, self.xh, self.xl, ready, lambda p: p < 4, take, (0, 1, 2)))
            self.act.run(s.preload_act_table_set, "natural_log_exp_and_others", signal=False)
            neg, add = (masks[:, i * NZ:(i + 1) * NZ].rearrange("p (o n) -> p o n", o=1).to_broadcast([P, 2, NZ])
                        for i in range(2))
            not_below, ones = self.const("not_below"), self.const("ones")
            tokens = []

            def pair(j):
                b, c = j % 3, j % 2
                z = self.slot[b].rearrange("p (j n) -> p j n", j=2)
                zs = z[:, :, 0:NZ]
                soft, fail, w = softs[b], fails[c], weights[c]
                self.pe.wait([self.free.get(2 * b), self.free.get(2 * b + 1)])
                for i in range(2):
                    rows = slice(HD * i, HD * i + HD)
                    self.pe.run(self.t.matmul, z[:, i, 0:SEQ], k[rows, j, 0:P], q[rows, j, :], start=True, stop=True,
                                after=[got["qk"]], signal=False, skip_group_check=True)
                    done = self.pe.run(self.t.matmul, z[:, i, SEQ:NZ], k[rows, j, P:SEQ], q[rows, j, P:SEQ],
                                       start=False, stop=True, skip_group_check=True)
                a = self.act.run(s.activation, soft, zs, ACT.Abs, after=[done, self.free.get(("soft", b))])
                a = self.act.run(s.activation, soft, soft, ACT.Exp, scale=-1.0, after=[a])
                a = self.act.run(s.activation, soft, soft, ACT.Ln, bias=1.0, after=[a])
                yield
                d = self.dve.run(v.scalar_tensor_tensor, fail, zs, 0.0, soft, ALU.max, ALU.add,
                                 after=[a, self.free.get(("fail", c))])
                d = self.dve.run(v.tensor_tensor, fail, fail, neg, ALU.mult, after=[d, masks_loaded])
                yield
                for i in range(2):
                    for o, m, r in ((z[:, i, 0:SEQ], not_below, fail[:, i, 0:SEQ]),
                                    (z[:, i, P:SEQ], ones, fail[:, i, SEQ:NZ]),
                                    (z[:, i, SEQ:NZ], not_below, fail[:, i, SEQ:NZ])):
                        done = self.pe.run(self.t.matmul, o, m, r, start=False, stop=True, after=[d],
                                           skip_group_check=True)
                self.free[("fail", c)] = done
                d = self.dve.run(v.scalar_tensor_tensor, soft, zs, 0.0, add, ALU.min, ALU.add, after=[done])
                a = self.act.run(s.activation, w, soft, ACT.Exp, after=[d, self.free.get(("weights", c))])
                self.free[2 * b] = self.free[2 * b + 1] = [d, a]
                self.free[("soft", b)] = a
                yield
                o_bank = self.bank[6 + c]
                self.pe.wait([self.free.get(6 + c)])
                for i in range(2):
                    h = 2 * j + i
                    o = o_bank[HD * i:HD * i + HD, :]
                    self.pe.run(self.t.matmul, o[:, 0:SEQ], val[:, 0, HD * h:HD * h + HD], w[:, i, 0:SEQ], start=True,
                                stop=True, after=[a, got["v"]], signal=False, skip_group_check=True)
                    done = self.pe.run(self.t.matmul, o[:, P:SEQ], val[:, 1, HD * h:HD * h + HD], w[:, i, SEQ:NZ],
                                       start=False, stop=True, skip_group_check=True)
                self.free[("weights", c)] = done
                self.free[6 + c] = self.split_out(o_bank[:, 0:SEQ], j, oh, ol, done)
                tokens.append(self.free[6 + c][1])

            run_all(pipelined(pair(j) for j in range(SB_H // 2)))
            take_y, finish = self.post_norm(self.second_col(l, "ffn_g"), (4, 5, 6, 7))
            run_all(self.linear("sb_out", l, oh, ol, tokens, False, take_y, (0, 1)))
            finish((0, 1))

    def position_tables(self, pos, ang, out):
        v = self.v
        loaded = self.small_load("positions_loaded", pos, self.dram["positions"])
        n = DIL_ROT // 2
        parts, rest = [], 2 * np.pi
        for bits in (8, 8, 8):
            e = 2.0 ** (bits - 1 - np.floor(np.log2(rest)))
            parts.append(float(np.floor(rest * e) / e))
            rest -= parts[-1]
        parts.append(float(np.float32(rest)))
        a0, turns, a1 = (ang[:, i * TT * n:(i + 1) * TT * n] for i in range(3))
        t3 = lambda ap: ap.rearrange("p (t n) -> p t n", t=TT)
        magic = 1.5 * 2.0 ** 23
        posf = ang[:, 3 * TT * n:3 * TT * n + TT]
        t = self.dve.run(v.tensor_copy, posf, pos, after=[loaded])
        t = self.dve.run(v.tensor_tensor, t3(a0), posf.rearrange("p (t o) -> p t o", o=1).to_broadcast([P, TT, n]),
                         self.const("inv_freq").rearrange("p (o n) -> p o n", o=1).to_broadcast([P, TT, n]),
                         ALU.mult, after=[t])
        t = self.dve.run(v.tensor_scalar, turns, a0, 1.0 / (2 * np.pi), magic, ALU.mult, ALU.add, after=[t])
        t = self.dve.run(v.tensor_scalar, turns, turns, magic, None, ALU.subtract, after=[t])
        for part in parts:
            t = self.dve.run(v.scalar_tensor_tensor, a0, turns, -part, a0, ALU.mult, ALU.add, after=[t])
        t = self.dve.run(v.tensor_scalar, a1, a0, np.pi / 2, None, ALU.add, after=[t])
        t = self.dve.run(v.tensor_scalar, turns, a1, np.pi, -2 * np.pi, ALU.is_gt, ALU.mult, after=[t])
        t = self.dve.run(v.tensor_tensor, a1, a1, turns, ALU.add, after=[t])
        for a in (a0, a1):
            t = self.dve.run(v.tensor_scalar, a, a, 3.1415925, -3.1415925, ALU.min, ALU.max, after=[t])
        c, sn = out[:, 0:TT * n], out[:, TT * n:2 * TT * n]
        a = self.act.run(self.s.activation, c, a1, ACT.Sin, after=[t])
        b = self.act.run(self.s.activation, sn, a0, ACT.Sin)
        self.dve.run(v.tensor_copy, out[:, 2 * TT * n:3 * TT * n], sn, after=[a, b])
        return self.dve.run(v.tensor_copy, out[:, 3 * TT * n:], c)

    def dilated(self, l):
        v, s = self.v, self.s
        ready = self.features
        G = len(DIL)
        with ExitStack() as ctx:
            sb = lambda name, floats, dt=F32: self.sb(f"{name}_{l}", floats, dt, ctx)
            tok = [sb(f"dil_tokens{i}", TT * DIL_W).rearrange("p (t h d) -> p t h d", t=TT, d=HD) for i in range(2)]
            qt = [self.kt_view(sb(f"dil_q{i}", 4 * SEQ)) for i in range(G)]
            kt_ = [self.kt_view(sb(f"dil_k{i}", 4 * SEQ)) for i in range(G)]
            val = [sb(f"dil_v{i}", TT * DIL_W).rearrange("p (t n) -> p t n", t=TT) for i in range(G)]
            oh, ol = self.kt_view(sb("dil_out_high", 4 * SEQ, F32R)), self.kt_view(sb("dil_out_low", 4 * SEQ, F32R))
            mask = sb("dil_masks", 9 * P)
            pos = sb("positions", TT, I32)
            ang = sb("angles", 64)
            tab = sb("dil_tables", 4 * TT * DIL_ROT // 2)
            self.fence()
            self.rows_ready = self.small_load(f"mix_gain_loaded_{l}", self.rows,
                                              self.dram["second_rows"][l, 0].partition_broadcast(P))
            at = CONSTS["dil_add"][0]
            mask_loaded = self.small_load("dil_masks_loaded", mask, self.dram["consts"][:, at:at + 9 * P])
            r_ready = self.pool.run(self.g.tensor_scalar, self.stat[:, 6:8], self.stat[:, 4:6], HD ** -0.5, None,
                                    ALU.mult, after=[self.r_ready])
            tables = self.position_tables(pos, ang, tab)
            got, late = {}, []

            def scaled(out, part, at, after):
                for t in range(TT):
                    e = self.act.run(s.activation, out[:, t], part[:, t], ACT.Copy,
                                     scale=self.stat[:, at + t:at + t + 1], after=[r_ready, after])
                return e

            def turn_late():
                if late:
                    n, out, t = late.pop()
                    flat = tok[n].rearrange("p t h d -> p t (h d)")
                    got["turned"] = self.transpose_pairs(lambda i, t: flat[:, t, i * P:(i + 1) * P], 4, P, out, [t],
                                                         banks=(6, 7))
                    self.free[("tok", n)] = self.pe.last()

            def take(panel, acc, w, done):
                g, what = panel // 3, panel % 3
                a = acc.rearrange("p (t n) -> p t n", t=TT)
                if what == 2:
                    got["v"] = scaled(val[g], a, 4, [done])
                    turn_late()
                    return [got["v"]]
                c = scaled(tok[what], a.rearrange("p t (h d) -> p t h d", d=HD), 4 if what else 6,
                           [done, self.free.get(("tok", what))])
                t = self.rotate(tok[what], DIL_H, 0, DIL_ROT, tab, [c, tables])
                turn_late()
                late.append((what, (qt, kt_)[what][g], t))
                return [c]

            run_all(self.linear("dil_in", 0, self.xh, self.xl, ready, False, take, (0, 1, 2)))
            turn_late()
            turned = [got["turned"], self.act.last(), self.dve.last(), mask_loaded]
            tokens = []
            wide = G * SEQ
            buffer = lambda i: self.scr[:, i * wide:(i + 1) * wide]

            def unit(m):
                h, t = m // TT, m % TT
                keys = (t + 1) * P
                n = G * keys
                b, c = m % 3, m % 2
                banks = (2 * (h % 2), 2 * (h % 2) + 1) if t else (4,)
                s_ps = (self.slot[h % 2] if t else self.bank[4])[:, 0:n]
                base = (0 if t == 0 else G * P)
                st = self.stat[:, 128 + 16 * b:136 + 16 * b]
                prob, probt = buffer(b)[:, 0:n], buffer(3 + c)[:, 0:n]
                half = slice(HD * (h % 2), HD * (h % 2) + HD)
                self.pe.wait([self.free.get(i) for i in banks])
                for g in range(G):
                    done = self.pe.run(self.t.matmul, s_ps[:, g * keys:(g + 1) * keys], qt[g][half, h // 2, t * P:(t + 1) * P],
                                       kt_[g][half, h // 2, 0:keys], start=True, stop=True, after=[turned],
                                       signal=g == G - 1)
                a = self.dve.run(v.tensor_tensor_reduce, prob, s_ps, mask[:, base:base + n], 1.0, MASKED, ALU.add,
                                 ALU.max, st[:, 0:1], after=[done, self.free.get(("prob", b)), self.free.get(("stat", b))])
                for i in banks:
                    self.free[i] = [a]
                a = self.dve.run(v.tensor_scalar, st[:, 1:2], st[:, 0:1], -1.0, None, ALU.mult, after=[a])
                e = self.act.run(s.activation, prob, prob, ACT.Exp, bias=st[:, 1:2], accum_out=st[:, 2:3], after=[a])
                yield
                a = self.dve.run(v.reciprocal, st[:, 3:4], st[:, 2:3], after=[e])
                p_ready = self.dve.run(v.tensor_scalar, prob, prob, st[:, 3:4], None, ALU.mult, after=[a])
                self.free[("stat", b)] = p_ready
                yield
                for i in range(n // P):
                    bank = 5 + i // 4
                    done = self.pe.run(self.t.transpose, self.bank[bank][:, (i % 4) * P:(i % 4 + 1) * P],
                                       prob[:, i * P:(i + 1) * P], self.const("ident"),
                                       after=[p_ready, self.free.get(bank)])
                self.free[("prob", b)] = done
                c1 = min(n, PANEL)
                e = self.act.run(s.activation, probt[:, 0:c1], self.bank[5][:, 0:c1], ACT.Copy,
                                 after=[done, self.free.get(("probt", c))])
                self.free[5] = [e]
                d = None
                if n > PANEL:
                    d = self.dve.run(v.tensor_copy, probt[:, c1:n], self.bank[6][:, 0:n - c1],
                                     after=[done, self.free.get(("probt", c))])
                    self.free[6] = [d]
                yield
                o = self.bank[7][half, t * P:(t + 1) * P]
                blocks = [(g, kt) for g in range(G) for kt in range(t + 1)]
                for i, (g, kt) in enumerate(blocks):
                    done = self.pe.run(self.t.matmul, o, val[g][:, kt, HD * h:HD * h + HD], probt[:, i * P:(i + 1) * P],
                                       start=i == 0, stop=i == len(blocks) - 1,
                                       after=[e, d, got["v"], self.free.get(7)], skip_group_check=True)
                self.free[("probt", c)] = done
                if t == TT - 1 and h % 2:
                    self.free[7] = self.split_out(self.bank[7][:, 0:SEQ], h // 2, oh, ol, done)
                    tokens.append(self.free[7][1])

            run_all(pipelined(unit(m) for m in range(DIL_H * TT)))
            take_y, finish = self.post_norm(self.second_col(l, "ffn_g"), (4, 5, 6, 7))
            run_all(self.linear("dil_out", 0, oh, ol, tokens, False, take_y, (0, 1)))
            finish((0, 1))

    def second_ffn(self, l):
        v, s = self.v, self.s
        ready = self.features
        with ExitStack() as ctx:
            sb = lambda name, floats, dt=F32: self.sb(f"{name}_{l}", floats, dt, ctx)
            n_f = D_FF_2 // P
            ah, al = self.kt_view(sb("ff_high", n_f * SEQ, F32R)), self.kt_view(sb("ff_low", n_f * SEQ, F32R))
            emb = sb("ple_tokens", TT * PLE).rearrange("p (t n) -> p t n", t=TT)
            eh, el = self.kt_view(sb("ple_high", 2 * SEQ, F32R)), self.kt_view(sb("ple_low", 2 * SEQ, F32R))
            up = sb("ple_up", TT * D).rearrange("p (t n) -> p t n", t=TT)
            self.fence()
            self.rows_ready = self.small_load(f"ffn_gain_loaded_{l}", self.rows,
                                              self.dram["second_rows"][l, 1].partition_broadcast(P))
            emb_loaded = self.small_load(f"ple_loaded_{l}", emb, self.dram["ple"][l].rearrange("(t p) n -> p t n", p=P))
            row = self.scale_row([self.r_ready]).to_broadcast([P, 4, SEQ])
            acts = []

            def take(panel, acc, w, done):
                i = panel % 2
                a, sq = (self.scr[:, (2 * i + j) * UNIT:(2 * i + j + 1) * UNIT] for j in range(2))
                relu = self.dve.run(v.scalar_tensor_tensor, self.kt_view(a), self.kt_view(acc), 0.0, row, ALU.max,
                                    ALU.mult, after=[done, self.row_ready, self.free.get(("act", i))])
                t = self.act.run(s.activation, sq, a, ACT.Square, after=[relu, self.free.get(("act", i))])
                self.free[("act", i)] = t
                ks = slice(4 * panel, 4 * panel + 4)
                t = self.act.run(s.activation, ah[:, ks, :], self.kt_view(sq), ACT.Copy, after=[t])
                e = self.dve.run(v.tensor_tensor, al[:, ks, :], self.kt_view(sq), ah[:, ks, :], ALU.subtract, after=[t])
                self.free[("act", i)] = e
                acts.extend([e] * 4)
                return [relu]

            run_all(self.linear("ff_in", l, self.xh, self.xl, ready, True, take, (0, 1, 2, 3)))
            emb_ready = self.to_features(emb, [0, 1], [emb_loaded], eh, el)
            take_y, finish = self.post_norm(self.second_col(l, "ple_g"), (4, 5, 6, 7))
            run_all(self.linear("ff_out", l, ah, al, acts, False, take_y, (0, 1)))

            def take_up(panel, acc, w, done):
                t = self.act.run(s.activation, up[:, :, panel * PANEL:panel * PANEL + w],
                                 acc.rearrange("p (t n) -> p t n", t=TT), ACT.Copy, after=[done])
                return [t]

            run_all(self.linear("ple_up", l, eh, el, emb_ready, False, take_up, (2, 3)))
            finish((0, 1))

            ready, high, low = self.features, self.xh, self.xl
            self.xh, self.xl, self.xh_next, self.xl_next = self.xh_next, self.xl_next, self.xh, self.xl
            r = [self.stat[:, 14 + t:15 + t] for t in range(TT)]
            r_kept = self.pool.run(self.g.tensor_copy, self.stat[:, 14:16], self.stat[:, 4:6], after=[self.r_ready, self.act.last()])
            self.start_features()

            def take_gate(panel, acc, w, done):
                c = slice(panel * PANEL, panel * PANEL + w)
                a = acc.rearrange("p (t n) -> p t n", t=TT)
                gate = self.scr[:, panel * UNIT:(panel + 1) * UNIT].rearrange("p (t n) -> p t n", t=TT)
                for t in range(TT):
                    e = self.act.run(s.activation, gate[:, t, :], a[:, t, :], ACT.Sigmoid, scale=r[t],
                                     after=[done, r_kept, self.dve.last()])
                    d = self.dve.run(v.tensor_tensor, gate[:, t, :], gate[:, t, :], up[:, t, c], ALU.mult, after=[e])
                    d = self.dve.run(v.tensor_tensor, self.x[:, t, c], self.x[:, t, c], gate[:, t, :], ALU.add, after=[d])
                self.x_ready = d
                if l + 1 < DEPTH:
                    step = lambda: self.half_done(panel, d, self.second_col(l + 1, "mix_g"), False, (4, 5, 6, 7))
                    if panel:
                        step()
                    else:
                        self.later.append([2, step])
                return [e]

            run_all(self.linear("ple_gate", l, high, low, ready, False, take_gate, (0, 1)))

    def build(self, stages=8):
        self.pool.run(self.g.memset, self.half, -0.5)
        src = self.dram["x"].rearrange("(t p) n -> p t n", p=P)
        x_loaded = [self.small_load(f"x_loaded{i}", self.x[:, :, i * PANEL:(i + 1) * PANEL],
                                    src[:, :, i * PANEL:(i + 1) * PANEL]) for i in range(2)]
        tables = [self.small_load("consts_loaded", self.consts, self.dram["consts"][:, 0:N_HELD])]
        n = DEPTH * N_FIRST_COLS
        cols = lambda ap, width: ap.rearrange("p (l n) -> p l n", n=width)
        tables += [self.small_load("first_cols_loaded", cols(self.cols[:, 0:n], N_FIRST_COLS),
                                   self.dram["first_cols"].rearrange("l p n -> p l n")),
                   self.small_load("second_cols_loaded", cols(self.cols[:, n:], N_SECOND_COLS),
                                   self.dram["second_cols"].rearrange("l p n -> p l n"))]
        for e in (self.pe, self.act, self.dve, self.pool):
            e.wait(tables)
        self.start_features()
        for i in range(2):
            self.half_done(i, x_loaded[i], self.first_col(0, "attn_g"), False, (4, 5, 6, 7))
        self.x_ready = x_loaded
        steps = [lambda: self.first_mixing(0), lambda: self.first_ffn(0), lambda: self.first_mixing(1),
                 lambda: self.first_ffn(1), lambda: self.stick_breaking(0), lambda: self.second_ffn(0),
                 lambda: self.dilated(1), lambda: self.second_ffn(1)]
        for n, step in enumerate(steps[:stages]):
            if n == 2 * DEPTH:
                self.xh_next = self.kt_view(self.sb("x_high_next", DK * SEQ, F32R))
                self.xl_next = self.kt_view(self.sb("x_low_next", DK * SEQ, F32R))
            step()
        stored = self.small_load("out_stored", self.out.rearrange("(t p) n -> p t n", p=P), self.x, after=[self.x_ready])
        self.sp.wait([stored])

        with self.nc.Block() as block:
            @block.sync
            def _(eng):
                self.sp.play(eng)

            @block.tensor
            def _(eng):
                self.pe.play(eng)

            @block.scalar
            def _(eng):
                self.act.play(eng)

            @block.vector
            def _(eng):
                self.dve.play(eng)

            @block.gpsimd
            def _(eng):
                self.pool.play(eng)


def run_all(gen):
    for _ in gen:
        pass


def pipelined(gens):
    active = []
    for gen in gens:
        next(gen)
        active = [g for g in active if advance(g)]
        active.append(gen)
        yield
    while active:
        active = [g for g in active if advance(g)]
        yield


def advance(gen):
    for _ in gen:
        return True
    return False


def interleave(front, back, per):
    for _ in front:
        for _ in range(per):
            advance(back)
    run_all(back)


KTS = {p[0]: p[3] // P for p in weight_plan()}



def pack(inputs):
    f = {k: np.asarray(v) for k, v in inputs.items()}
    units, loads, total = weight_units()
    flat = np.empty(total, np.float32)
    by_load = {}
    for u in units:
        by_load.setdefault(u["load"], []).append(u)
    for n, (at, size) in enumerate(loads):
        parts = []
        for u in by_load[n]:
            w = f[u["source"]][u["layer"]][u["k0"] * P:(u["k0"] + u["nk"]) * P, u["c0"]:u["c0"] + u["w"]]
            parts.append(w.reshape(u["nk"], P, u["w"]).transpose(1, 0, 2).reshape(P, -1))
        flat[at:at + P * size] = np.concatenate(parts, 1).reshape(-1)

    def col(a):
        return a.reshape(-1, P).T

    def head_col(g):
        return np.concatenate([g[:NOPE], np.ones(P - NOPE, np.float32)])[:, None]

    first_cols = np.stack([np.concatenate(
        [col(f["attn_norm_g"][l]), col(f["mla_q_norm_g"][l]), col(f["mla_kv_norm_g"][l]),
         head_col(f["mla_q_head_g"][l]), head_col(f["mla_k_head_g"][l]), col(f["pool_scale"][l]),
         col(f["ffn_norm_g"][l])] + [col(f["ffn_conv_w"][l, i]) for i in range(3)] + [col(f["ffn_conv_b"][l])], 1)
        for l in range(DEPTH)])
    first_rows = np.stack([np.concatenate(
        [f["mla_q_head_g"][l, NOPE:], f["mla_k_head_g"][l, NOPE:], f["gqa_q_head_g"][l], f["gqa_k_head_g"][l]])
        for l in range(DEPTH)])
    second_cols = np.stack([np.concatenate([col(f[n][l]) for n in ("g_mix_pre_2", "g_ffn_pre_2", "g_ple_2")], 1)
                            for l in range(DEPTH)])
    second_rows = np.stack([np.stack([f["g_mix_post_2"][l], f["g_ffn_post_2"][l]]) for l in range(DEPTH)])
    arrays = {
        "weights": flat, "x": f["x"][0], "first_cols": first_cols, "first_rows": first_rows,
        "pool_w": f["pool_w"].transpose(0, 2, 1, 3).reshape(DEPTH, P, POOL_G * P), "second_cols": second_cols,
        "second_rows": second_rows, "ple": f["p_2"][:, 0], "positions": f["positions_2"].reshape(TT, P).T,
        "consts": constants(),
    }
    return {k: np.ascontiguousarray(v) for k, v in arrays.items()}


def kernel(**inputs):
    import concourse.bacc as bacc
    from concourse.bass_utils import run_bass_kernel_spmd

    nc = bacc.Bacc("TRN2", target_bir_lowering=False, num_devices=1, dynamic_dma_scratch_size=1024)
    arrays = pack(inputs)
    dram = {n: nc.dram_tensor("in_" + n, a.shape, mybir.dt.from_np(a.dtype), kind="ExternalInput").ap()
            for n, a in arrays.items()}
    out = nc.dram_tensor("out", (SEQ, D), F32, kind="ExternalOutput").ap()
    with ExitStack() as ctx:
        Program(nc, ctx, dram, out).build()
    got = run_bass_kernel_spmd(nc, [{"in_" + n: a for n, a in arrays.items()}], core_ids=[0]).results[0]["out"]
    return np.asarray(got).reshape(1, SEQ, D)
```

```python
from contextlib import ExitStack

import numpy as np

import concourse.bass as bass
from concourse import mybir

F32 = mybir.dt.float32
F32R = mybir.dt.float32r
I32 = mybir.dt.int32
ALU = mybir.AluOpType
ACT = mybir.ActivationFunctionType
AXIS_X = mybir.AxisListType.X

P = 128
SEQ = 256
TT = SEQ // P
D = 1024
DK = D // P
DEPTH = 2
EPS = 1e-6

MLA_H, Q_LORA, KV_LORA, NOPE, ROPE, MLA_V = 8, 256, 128, 64, 32, 64
MLA_QK = NOPE + ROPE
GQA_H, GQA_KV, HD = 8, 2, 64
POOL_WINDOWS = (2, 4, 8, 16)
POOL_G, POOL_W = 4, 512
D_FF = 2816
FT = D_FF // P
D_FF_2 = 4096
SB_H = 16
DIL = (1, 4, 16)
DIL_H, DIL_W = 8, 512
DIL_ROT = 16
PLE = 256
GRID_W = 64

PANEL = 512
UNIT = 1024
SPLIT_SLOTS = 4
RAW_SLOTS = 4
SPLIT_AHEAD = SPLIT_SLOTS - 1
MASKED = -1.0e30
POOL_PAD = max(POOL_WINDOWS) // 2



def panels_of(first, last, width=PANEL):
    return [(c, min(c + width, last)) for c in range(first, last, width)]


def weight_plan():
    plan = []
    c_mla = Q_LORA + KV_LORA + ROPE
    c_gqa = c_mla + (GQA_H + 2 * GQA_KV) * HD
    c_pool = c_gqa + POOL_W
    for l in range(DEPTH):
        plan += [
            ("proj", l, "w_in", D, [(0, c_mla)] + panels_of(c_mla, c_gqa) + [(c_gqa, c_pool)]),
            ("gates_early", l, "w_in", D, panels_of(c_pool, c_pool + PANEL)),
            ("up_q", l, "mla_w_uq", Q_LORA, panels_of(0, MLA_H * MLA_QK)),
            ("up_kv", l, "mla_w_ukv", KV_LORA, panels_of(0, MLA_H * (NOPE + MLA_V))),
            ("gates", l, "w_in", D, panels_of(c_pool + PANEL, c_pool + 3 * D)),
            ("branch_gqa", l, "w_branch_gqa", GQA_H * HD, panels_of(0, D)),
            ("branch_pool", l, "w_branch_pool", POOL_W, panels_of(0, D)),
            ("branch_mla", l, "w_branch_mla", MLA_H * MLA_V, panels_of(0, D)),
            ("out", l, "w_out", D, panels_of(0, D)),
            ("ffn_up", l, "ffn_w_up", D, [p for c0, c1 in panels_of(0, D_FF)
                                          for p in ((c0, c1), (D_FF + c0, D_FF + c1))]),
            ("ffn_down", l, "ffn_w_down", D_FF, panels_of(0, D)),
        ]
    for l in range(DEPTH):
        if l == 0:
            plan += [("sb_in", 0, "w_in_sb_2", D, panels_of(0, 2 * D)),
                     ("sb_values", 0, "w_in_sb_2", D, panels_of(2 * D, 3 * D)),
                     ("sb_out", 0, "w_out_sb_2", D, panels_of(0, D))]
        else:
            plan += [("dil_in", 0, "w_in_dil_2", D, panels_of(0, len(DIL) * 3 * DIL_W)),
                     ("dil_out", 0, "w_out_dil_2", DIL_W, panels_of(0, D))]
        plan += [("ff_in", l, "w_ff_in_2", D, panels_of(0, D_FF_2)),
                 ("ff_out", l, "w_ff_out_2", D_FF_2, panels_of(0, D)),
                 ("ple_up", l, "w_ple_2", PLE, panels_of(0, D)),
                 ("ple_gate", l, "w_ple_gate_2", D, panels_of(0, D))]
    return plan


def weight_units():
    units, loads, at = [], [], 0
    for name, layer, source, rows, panels in weight_plan():
        kts = rows // P
        own = []
        for n, (c0, c1) in enumerate(panels):
            w = c1 - c0
            step = max(1, min(kts, UNIT // w))
            for k0 in range(0, kts, step):
                own.append(dict(name=name, layer=layer, source=source, panel=n, c0=c0, w=w, k0=k0,
                                nk=min(step, kts - k0)))
        for i in range(0, len(own), 2):
            pair = own[i:i + 2]
            size = sum(u["w"] * u["nk"] for u in pair)
            inside = 0
            for u in pair:
                u["load"], u["inside"] = len(loads), inside
                inside += u["w"] * u["nk"]
            loads.append((at, size))
            at += P * size
        units += own
    return units, loads, at


FIRST_COLS, _n = {}, 0
for _name, _w in (("attn_g", DK), ("q_lora_g", 2), ("kv_lora_g", 1), ("q_head_g", 1), ("k_head_g", 1),
                  ("pool_scale", POOL_G), ("ffn_g", DK), ("conv_w", 3 * 2 * FT), ("conv_b", 2 * FT)):
    FIRST_COLS[_name] = (_n, _n + _w)
    _n += _w
N_FIRST_COLS = _n
SECOND_COLS, _n = {}, 0
for _name, _w in (("mix_g", DK), ("ffn_g", DK), ("ple_g", DK)):
    SECOND_COLS[_name] = (_n, _n + _w)
    _n += _w
N_SECOND_COLS = _n
ROW_QM, ROW_KM, ROW_QG, ROW_KG = (0, 32), (32, 64), (64, 128), (128, 192)
N_ROWS = 192

CONSTS, _n = {}, 0
for _name, _w in (("ident", P), ("not_below", P), ("ones", P), ("cos_m", TT * ROPE // 2),
                  ("sin_m", TT * ROPE // 2), ("cos_g", TT * HD // 2), ("sin_g", TT * HD // 2),
                  ("inv_freq", DIL_ROT // 2), ("pool_edge", POOL_G * 2 * POOL_PAD), ("sb_neg", 3 * P),
                  ("sb_add", 3 * P), ("dil_add", 9 * P)):
    CONSTS[_name] = (_n, _n + _w)
    _n += _w
N_CONSTS = _n
N_HELD = CONSTS["sb_neg"][0]


def constants():
    c = np.zeros((P, N_CONSTS), np.float32)

    def put(name, value):
        a, b = CONSTS[name]
        c[:, a:b] = np.asarray(value, np.float32).reshape(P, b - a)

    i = np.arange(P)
    put("ident", np.eye(P))
    put("not_below", i[:, None] >= i[None, :])
    put("ones", np.ones((P, P)))
    row, col = np.arange(SEQ) // GRID_W, np.arange(SEQ) % GRID_W
    for tag, rot in (("m", ROPE), ("g", HD)):
        n = rot // 4
        inv = (10000.0 ** (-np.arange(n) / n)).astype(np.float32)
        angle = np.concatenate([row[:, None].astype(np.float32) * inv, col[:, None].astype(np.float32) * inv], 1)
        for fn, f in (("cos_", np.cos), ("sin_", np.sin)):
            table = f(angle.astype(np.float64))
            put(fn + tag, table.reshape(TT, P, rot // 2).transpose(1, 0, 2))
    put("inv_freq", np.tile(500000.0 ** (-np.arange(0, DIL_ROT, 2) / DIL_ROT), (P, 1)))
    past = np.concatenate([i[:, None] < np.arange(SEQ)[None, :], i[:, None] < i[None, :]], 1)
    put("sb_neg", np.where(past, -1.0, 0.0))
    put("sb_add", np.where(past, 0.0, MASKED))
    parts = []
    for keys, q0 in ((P, 0), (SEQ, P)):
        for dil in DIL:
            dist = q0 + i[:, None] - np.arange(keys)[None, :]
            ok = (dist >= 0) & (dist % dil == 0) & (dist // dil <= P)
            parts.append(np.where(ok, 0.0, MASKED))
    put("dil_add", np.concatenate(parts, 1))
    t = np.concatenate([np.arange(POOL_PAD), np.arange(SEQ - POOL_PAD, SEQ)])
    edges = [w / (np.clip(t + w - w // 2, 0, SEQ) - np.clip(t - w // 2, 0, SEQ)) for w in POOL_WINDOWS]
    put("pool_edge", np.tile(np.concatenate(edges), (P, 1)))
    return c



class Engine:

    def __init__(self, done):
        self.done, self.count, self.steps, self.waited = done, 0, [], {}

    def wait(self, tokens):
        for token in tokens:
            if isinstance(token, list):
                self.wait(token)
            elif token is not None and self.waited.get(token[0].name, 0) < token[1]:
                self.waited[token[0].name] = token[1]
                self.steps.append((None, token, None, None))

    def run(self, op, *args, after=(), signal=True, **kw):
        self.wait(after)
        self.steps.append((op, args, kw, (self.done, 1) if signal else None))
        self.count += signal
        return (self.done, self.count) if signal else None

    def load(self, op, out, in_, done, count, after=()):
        self.wait(after)
        self.steps.append((op, (out, in_), {}, (done, 16)))
        return (done, count)

    def last(self):
        return (self.done, self.count) if self.count else None

    def play(self, eng):
        for op, args, kw, signal in self.steps:
            if op is None:
                eng.wait_ge(args[0], args[1])
            elif signal:
                op(*args, **kw).then_inc(*signal)
            else:
                op(*args, **kw)


class Program:
    def __init__(self, nc, ctx, dram, out):
        self.nc, self.ctx, self.dram, self.out = nc, ctx, dram, out
        self.pe, self.act, self.dve, self.pool, self.sp = (
            Engine(self.sem(n)) for n in ("pe_done", "act_done", "dve_done", "pool_done", "sp_done"))
        self.t, self.s, self.v, self.g = nc.tensor, nc.scalar, nc.vector, nc.gpsimd
        sb, ps = self.sb, self.ps
        self.consts = sb("consts", N_HELD)
        self.x = sb("residual", TT * D).rearrange("p (t n) -> p t n", t=TT)
        self.stat = sb("stat", 320)
        self.junk = [sb(f"squares{i}", PANEL) for i in range(TT)]
        self.r_row = sb("rstd_row", SEQ)
        self.diag = self.junk[0][:, 0:TT * P]
        self.half = sb("minus_half", 32)
        self.cols = sb("cols", DEPTH * (N_FIRST_COLS + N_SECOND_COLS))
        self.rows = sb("rows", D)
        self.raw = [sb(f"w_raw{i}", 2 * UNIT) for i in range(RAW_SLOTS)]
        self.wh = [sb(f"w_high{i}", UNIT, F32R) for i in range(SPLIT_SLOTS)]
        self.wl = [sb(f"w_low{i}", UNIT, F32R) for i in range(SPLIT_SLOTS)]
        self.xh = self.kt_view(sb("x_high", DK * SEQ, F32R))
        self.xl = self.kt_view(sb("x_low", DK * SEQ, F32R))
        self.scr = sb("scratch", 4 * UNIT)
        psum = ps("psum", 8 * PANEL)
        self.bank = [psum[:, i * PANEL:(i + 1) * PANEL] for i in range(8)]
        self.slot = [psum[:, 2 * i * PANEL:2 * (i + 1) * PANEL] for i in range(4)]
        self.free = {}
        self.units, self.loads, self.total = weight_units()
        self.raw_sem = [self.sem(f"w_loaded{i}") for i in range(RAW_SLOTS)]
        self.n_loaded = self.n_split = self.n_used = 0
        self.load_token, self.high_token, self.low_token, self.used_token = [], [], [], []
        self.later = []

    def sem(self, name):
        return self.ctx.enter_context(self.nc.semaphore(name))

    def sb(self, name, floats, dt=F32, ctx=None):
        return (ctx or self.ctx).enter_context(self.nc.sbuf_tensor(name, [P, floats], dt))[:, :]

    def ps(self, name, floats):
        return self.ctx.enter_context(self.nc.psum_tensor(name, [P, floats], F32))[:, :]

    def kt_view(self, ap):
        return ap.rearrange("p (k s) -> p k s", s=SEQ)

    def const(self, name):
        a, b = CONSTS[name]
        return self.consts[:, a:b]

    def small_load(self, name, out, in_, after=()):
        return self.sp.load(self.nc.sync.dma_start, out, in_, self.sem(name), 16, after)

    def fence(self):
        done = [e.last() for e in (self.pe, self.act, self.dve, self.pool)]
        for e in (self.act, self.dve, self.pool, self.sp):
            e.wait(done)

    def load_weights(self, n):
        at, size = self.loads[n]
        slot = n % RAW_SLOTS
        before = [u for u, unit in enumerate(self.units) if unit["load"] == n - RAW_SLOTS]
        src = self.dram["weights"][at:at + P * size].rearrange("(p n) -> p n", p=P)
        self.load_token.append(self.sp.load(
            self.nc.sync.dma_start, self.raw[slot][:, 0:size], src, self.raw_sem[slot],
            16 * (n // RAW_SLOTS + 1),
            after=[self.high_token[u] for u in before] + [self.low_token[u] for u in before]))

    def split_unit(self, n):
        u = self.units[n]
        size = u["w"] * u["nk"]
        slot = n % SPLIT_SLOTS
        raw = self.raw[u["load"] % RAW_SLOTS][:, u["inside"]:u["inside"] + size]
        left = self.used_token[n - SPLIT_SLOTS] if n >= SPLIT_SLOTS else None
        self.high_token.append(self.act.run(self.s.activation, self.wh[slot][:, 0:size], raw, ACT.Copy,
                                            after=[self.load_token[u["load"]], left]))
        self.low_token.append(self.dve.run(self.v.tensor_tensor, self.wl[slot][:, 0:size], raw,
                                           self.wh[slot][:, 0:size], ALU.subtract,
                                           after=[self.high_token[n], left]))

    def prefetch(self, n):
        last = min(n + SPLIT_AHEAD, len(self.units) - 1)
        while self.n_split <= last:
            reach = self.units[self.n_split]["load"] + RAW_SLOTS
            if self.n_split:
                reach = min(reach, self.units[self.n_split - 1]["load"] + RAW_SLOTS)
            while self.n_loaded < min(reach, len(self.loads)):
                self.load_weights(self.n_loaded)
                self.n_loaded += 1
            self.split_unit(self.n_split)
            self.n_split += 1

    def linear(self, name, layer, high, low, ready, feature_major, consume, slots=(0, 1)):
        kts = KTS[name]
        while self.n_used < len(self.units):
            n = self.n_used
            u = self.units[n]
            if (u["name"], u["layer"]) != (name, layer):
                break
            self.prefetch(n)
            w, held, slot = u["w"], n % SPLIT_SLOTS, slots[u["panel"] % len(slots)]
            acc = self.slot[slot]
            if u["k0"] == 0:
                self.pe.wait([self.free.get(2 * slot), self.free.get(2 * slot + 1)])
            by_feature = feature_major(u["panel"]) if callable(feature_major) else feature_major
            wh = self.wh[held][:, 0:w * u["nk"]].rearrange("p (k n) -> p k n", n=w)
            wl = self.wl[held][:, 0:w * u["nk"]].rearrange("p (k n) -> p k n", n=w)
            self.pe.wait([self.low_token[n]])
            for j in range(u["nk"]):
                k = u["k0"] + j
                ops = []
                end = k == kts - 1
                if by_feature:
                    for f in range(w // P):
                        cut = slice(f * P, (f + 1) * P)
                        o = acc[:, f * SEQ:(f + 1) * SEQ]
                        bank_start = k == 0 and f % 2 == 0
                        ops += [(o, wh[:, j, cut], high[:, k, :], bank_start, False),
                                (o, wh[:, j, cut], low[:, k, :], False, False),
                                (o, wl[:, j, cut], high[:, k, :], False, end)]
                else:
                    for t in range(TT):
                        cut = slice(t * P, (t + 1) * P)
                        o = acc[:, t * PANEL:t * PANEL + w]
                        ops += [(o, high[:, k, cut], wh[:, j, :], k == 0, False),
                                (o, high[:, k, cut], wl[:, j, :], False, False),
                                (o, low[:, k, cut], wh[:, j, :], False, end)]
                for i, (o, a, b, start, stop) in enumerate(ops):
                    token = self.pe.run(self.t.matmul, o, a, b, start=start, stop=stop, skip_group_check=True,
                                        after=[ready[k]], signal=j == u["nk"] - 1 and i == len(ops) - 1)
            self.used_token.append(token)
            self.n_used += 1
            self.queue_due()
            if end:
                self.free[2 * slot] = self.free[2 * slot + 1] = consume(u["panel"], acc, w, token)
            yield

    def after_units(self, units, step):
        self.later.append([units, step])

    def queue_due(self):
        for item in self.later:
            item[0] -= 1
        due = [item[1] for item in self.later if item[0] <= 0]
        self.later = [item for item in self.later if item[0] > 0]
        for step in due:
            step()

    def rstd(self, sums, n, count, out, after):
        t = self.pool.run(self.g.tensor_scalar, sums, sums, 1.0 / count, EPS, ALU.mult, ALU.add, after=after)
        return self.pool.run(self.g.tensor_tensor, out, sums, self.half[:, 0:n], ALU.pow, after=[t])

    def squares(self, src, half, sums):
        c = slice(half * PANEL, (half + 1) * PANEL)
        at = lambda t: sums[:, 2 * half + t:2 * half + t + 1]
        return [self.act.run(self.s.activation, self.junk[0], src[:, 0, c], ACT.Square, accum_out=at(0),
                             after=[self.act.last()]),
                self.dve.run(self.v.tensor_tensor_reduce, self.junk[1], src[:, 1, c], src[:, 1, c], 1.0, 0.0,
                             ALU.mult, ALU.add, at(1), after=[self.dve.last()])]

    def token_rstd(self, sums, out, after):
        s = sums[:, 0:2]
        t = self.pool.run(self.g.tensor_tensor, s, s, sums[:, 2:4], ALU.add,
                          after=[after, self.act.last(), self.dve.last()])
        return self.rstd(s, 2, D, out, [t])

    def to_features(self, src, kts, ready, high, low, gain=None, banks=(4, 5, 6, 7)):
        tokens = []
        for n in range(0, len(kts), 2):
            b = banks[(n // 2) % len(banks)]
            bank = self.bank[b]
            own = kts[n:n + 2]
            for i, k in enumerate(own):
                for t in range(TT):
                    at = i * SEQ + t * P
                    done = self.pe.run(self.t.transpose, bank[:, at:at + P], src[:, t, k * P:(k + 1) * P],
                                       self.const("ident"), after=[ready, self.free.get(b)])
            g = [gain[:, k:k + 1] if gain is not None else 1.0 for k in own]
            for i, k in enumerate(own):
                a = self.act.run(self.s.activation, high[:, k, :], bank[:, i * SEQ:(i + 1) * SEQ], ACT.Copy,
                                 scale=g[i], after=[done])
            for i, k in enumerate(own):
                d = self.dve.run(self.v.scalar_tensor_tensor, low[:, k, :], bank[:, i * SEQ:(i + 1) * SEQ], g[i],
                                 high[:, k, :], ALU.mult, ALU.subtract, after=[a])
                tokens.append(d)
            self.free[b] = [a, d]
        return tokens

    def half_done(self, half, token, gain, scaled, banks):
        sums, r, features = self.stat[:, 0:4], self.stat[:, 4:6], self.features
        high, low = self.xh, self.xl
        self.act.wait([token])
        self.dve.wait([token])
        self.sums_done += self.squares(self.x, half, sums)
        if half:
            self.r_ready = self.token_rstd(sums, r, self.sums_done)

        def make(src, half, ready):
            step = lambda: features.extend(
                self.to_features(src, list(range(4 * half, 4 * half + 4)), ready, high, low, gain, banks))
            if half:
                self.after_units(2, step)
            else:
                step()

        if not scaled:
            make(self.x, half, [token])
        elif half:
            xn = self.scr[:, 0:TT * D].rearrange("p (t n) -> p t n", t=TT)
            for h in range(2):
                c = slice(h * PANEL, (h + 1) * PANEL)
                a = self.act.run(self.s.activation, xn[:, 0, c], self.x[:, 0, c], ACT.Copy, scale=r[:, 0:1],
                                 after=[self.r_ready, self.dve.last()])
                d = self.dve.run(self.v.tensor_scalar, xn[:, 1, c], self.x[:, 1, c], r[:, 1:2], None, ALU.mult,
                                 after=[self.r_ready, self.act.last()])
                make(xn, h, [a, d])

    def start_features(self):
        self.features, self.sums_done = [], []

    def residual_add(self, gain, scaled=False, banks=(4, 5, 6, 7)):
        self.start_features()

        def take(panel, acc, w, done):
            c = slice(panel * PANEL, panel * PANEL + w)
            got = acc.rearrange("p (t n) -> p t n", t=TT)
            for t in range(TT):
                token = self.dve.run(self.v.tensor_tensor, self.x[:, t, c], self.x[:, t, c], got[:, t, 0:w], ALU.add,
                                     after=[done])
            self.x_ready = token
            step = lambda: self.half_done(panel, token, gain, scaled, banks)
            if panel:
                step()
            else:
                self.after_units(2, step)
            return [token]
        return take

    def scale_row(self, after):
        def make():
            for t in range(TT):
                d = self.dve.run(self.v.tensor_scalar, self.diag[:, t * P:(t + 1) * P], self.const("ident"),
                                 self.stat[:, 4 + t:5 + t], None, ALU.mult, after=[after, self.pe.last()])
            for t in range(TT):
                done = self.pe.run(self.t.matmul, self.bank[7][:, t * P:(t + 1) * P], self.const("ones"),
                                   self.diag[:, t * P:(t + 1) * P], start=True, stop=True, after=[d, self.free.get(7)])
            e = self.act.run(self.s.activation, self.r_row, self.bank[7][:, 0:SEQ], ACT.Copy,
                             after=[done, self.dve.last()])
            self.free[7] = [e]
            self.row_ready = e

        self.after_units(3, make)
        return self.r_row.rearrange("p (o s) -> p o s", o=1)

    def head_scale(self, tile, heads, width, after, place=0, on_pool=False):
        eng, op = (self.pool, self.g) if on_pool else (self.dve, self.v)
        n = TT * heads
        sq = self.scr[:, 0:n * width].rearrange("p (t h d) -> p t h d", t=TT, h=heads)
        s = self.stat[:, 16 + 48 * place:16 + 48 * place + n]
        a = eng.run(op.tensor_tensor, sq, tile, tile, ALU.mult, after=[after, self.dve.last()])
        a = self.dve.run(self.v.tensor_reduce, s.rearrange("p (t h) -> p t h", t=TT), sq, AXIS_X, ALU.add, after=[a])
        r = self.stat[:, 40 + 48 * place:40 + 48 * place + n]
        a = self.rstd(s, n, width, r, [a])
        yield
        rb = r.rearrange("p (t h o) -> p t h o", t=TT, o=1).to_broadcast([P, TT, heads, width])
        yield eng.run(op.tensor_tensor, tile, tile, rb, ALU.mult, after=[a])

    def rope_tables(self, tag, rot, gain, out, after):
        h = rot // 2
        for i, (fn, side) in enumerate((("cos_", 0), ("sin_", 1), ("sin_", 0), ("cos_", 1))):
            table = self.const(fn + tag).rearrange("p (t n) -> p t n", t=TT)
            g = gain[:, side * h:(side + 1) * h].rearrange("p (o n) -> p o n", o=1).to_broadcast([P, TT, h])
            o = out[:, i * TT * h:(i + 1) * TT * h].rearrange("p (t n) -> p t n", t=TT)
            t = self.dve.run(self.v.tensor_tensor, o, table, g, ALU.mult, after=after)
        return t

    def rotate(self, tile, heads, at, rot, tables, after, outs=None):
        h = rot // 2
        n = TT * heads * h
        x1, x2 = tile[:, :, :, at:at + h], tile[:, :, :, at + h:at + rot]
        tmp = [self.scr[:, 2 * UNIT + i * n:2 * UNIT + (i + 1) * n].rearrange("p (t h d) -> p t h d", t=TT, h=heads)
               for i in range(4)]
        assert 2 * UNIT + 4 * n <= 4 * UNIT
        after = [after, self.dve.last()]
        for i, (x, o) in enumerate(zip((x1, x2, x1, x2), tmp)):
            tb = tables[:, i * TT * h:(i + 1) * TT * h].rearrange("p (t o n) -> p t o n", t=TT, o=1)
            t = self.dve.run(self.v.tensor_tensor, o, x, tb.to_broadcast([P, TT, heads, h]), ALU.mult, after=after)
        for out in outs or [tile]:
            a = self.dve.run(self.v.tensor_tensor, out[:, :, :, at:at + h], tmp[0], tmp[1], ALU.subtract, after=[t])
            b = self.dve.run(self.v.tensor_tensor, out[:, :, :, at + h:at + rot], tmp[2], tmp[3], ALU.add, after=[t])
        return b

    def head_attention(self, n, h, q, k, v, scale, oh, ol, work, ready, tokens):
        sb, pt_bank, o_bank = 4 + n % 2, 6, 7
        b, c = n % 3, n % 2
        s_bank = self.bank[sb]
        st = self.stat[:, 128 + 16 * b:144 + 16 * b]
        prob, probt = work[b], work[3 + c]
        for t in range(TT):
            done = self.pe.run(self.t.matmul, s_bank[:, t * SEQ:(t + 1) * SEQ], q[:, t * P:(t + 1) * P], k,
                               start=True, stop=True, after=[ready, self.free.get(sb)], signal=t == TT - 1)
        a = self.dve.run(self.v.tensor_reduce, st[:, 0:2], s_bank.rearrange("p (t k) -> p t k", t=TT), AXIS_X,
                         ALU.max, after=[done, self.free.get(("stat", b))])
        a = self.dve.run(self.v.tensor_scalar, st[:, 2:4], st[:, 0:2], -scale, None, ALU.mult, after=[a])
        for t in range(TT):
            e = self.act.run(self.s.activation, prob[:, t * SEQ:(t + 1) * SEQ], s_bank[:, t * SEQ:(t + 1) * SEQ],
                             ACT.Exp, bias=st[:, 2 + t:3 + t], scale=scale, accum_out=st[:, 4 + t:5 + t],
                             after=[a, self.free.get(("prob", b))])
        self.free[sb] = [a, e]
        yield
        a = self.dve.run(self.v.reciprocal, st[:, 6:8], st[:, 4:6], after=[e])
        for t in range(TT):
            p = prob[:, t * SEQ:(t + 1) * SEQ]
            m = self.dve.run(self.v.tensor_scalar, p, p, st[:, 6 + t:7 + t], None, ALU.mult, after=[a])
        self.free[("stat", b)] = m
        yield
        for kt in range(TT):
            for t in range(TT):
                done = self.pe.run(self.t.transpose,
                                   self.bank[pt_bank][:, kt * SEQ + t * P:kt * SEQ + (t + 1) * P],
                                   prob[:, t * SEQ + kt * P:t * SEQ + (kt + 1) * P], self.const("ident"),
                                   after=[m, self.free.get(pt_bank)])
        self.free[("prob", b)] = done
        e = self.act.run(self.s.activation, probt, self.bank[pt_bank], ACT.Copy,
                         after=[done, self.free.get(("probt", c))])
        self.free[pt_bank] = [e]
        yield
        at = HD * (h % 2)
        for kt in range(TT):
            done = self.pe.run(self.t.matmul, self.bank[o_bank][at:at + HD, 0:SEQ], v(kt),
                               probt[:, kt * SEQ:(kt + 1) * SEQ], start=kt == 0, stop=kt == TT - 1,
                               after=[e, self.free.get(o_bank)], signal=kt == TT - 1)
        self.free[("probt", c)] = done
        if h % 2:
            self.free[o_bank] = self.split_out(self.bank[o_bank][:, 0:SEQ], h // 2, oh, ol, done)
            tokens.append(self.free[o_bank][1])

    def split_out(self, got, k, oh, ol, done, scale=1.0):
        a = self.act.run(self.s.activation, oh[:, k, :], got, ACT.Copy, scale=scale, after=[done])
        d = self.dve.run(self.v.scalar_tensor_tensor, ol[:, k, :], got, scale, oh[:, k, :], ALU.mult,
                         ALU.subtract, after=[done, a])
        return [a, d]

    def transpose_pairs(self, src, blocks, rows, out, done, scale=None, free=None, banks=(4, 5)):
        for n in range(0, blocks, 2):
            b = banks[(n // 2) % len(banks)]
            self.pe.wait([self.free.get(b)])
            for i in range(2):
                for t in range(TT):
                    at = i * SEQ + t * P
                    d = self.pe.run(self.t.transpose, self.bank[b][0:rows, at:at + P], src(n + i, t),
                                    self.const("ident"), after=done)
            got = self.bank[b][0:rows, :].rearrange("p (k s) -> p k s", k=2)
            g = scale[0:rows, :] if scale is not None else 1.0
            if (n // 2) % 2:
                e = self.act.run(self.s.activation, out[0:rows, n:n + 2, :], got, ACT.Copy, scale=g, after=[d, free])
            else:
                e = self.dve.run(self.v.tensor_scalar, out[0:rows, n:n + 2, :], got, g, None, ALU.mult, after=[d, free])
            self.free[b] = [e]
        return [self.free[b] for b in banks]

    def first_col(self, l, name):
        a, b = FIRST_COLS[name]
        return self.cols[:, l * N_FIRST_COLS + a:l * N_FIRST_COLS + b]

    def second_col(self, l, name):
        a, b = SECOND_COLS[name]
        at = DEPTH * N_FIRST_COLS + l * N_SECOND_COLS
        return self.cols[:, at + a:at + b]

    def first_mixing(self, l):
        v, s, g = self.v, self.s, self.g
        cols = lambda name: self.first_col(l, name)
        ready = self.features
        r = [self.stat[:, 4 + t:5 + t] for t in range(TT)]
        with ExitStack() as ctx:
            sb = lambda name, floats, dt=F32: self.sb(f"{name}_{l}", floats, dt, ctx)
            gates = self.kt_view(sb("gates", 3 * DK * SEQ))
            tok = sb("mla_tokens", 2 * TT * MLA_H * MLA_QK)
            n = TT * MLA_H * MLA_QK
            mq, mk = (tok[:, i * n:(i + 1) * n].rearrange("p (t h d) -> p t h d", t=TT, h=MLA_H) for i in range(2))
            qk = self.kt_view(sb("mla_heads", 2 * MLA_H * SEQ))
            gh = self.kt_view(sb("gqa_heads", (GQA_H // 2 + GQA_KV) * SEQ))
            mv = sb("mla_v", TT * MLA_H * MLA_V).rearrange("p (t h d) -> p t h d", t=TT, h=MLA_H)
            gqk = sb("gqa_tokens", TT * (GQA_H + GQA_KV) * HD).rearrange("p (t h d) -> p t h d", t=TT, d=HD)
            gv = sb("gqa_v", TT * GQA_KV * HD).rearrange("p (t n) -> p t n", t=TT)
            n_c = Q_LORA + KV_LORA + ROPE
            c = sb("compressed", TT * n_c).rearrange("p (t n) -> p t n", t=TT)
            pw = SEQ + 2 * POOL_PAD
            pp = sb("pool_in", POOL_G * pw).rearrange("p (g n) -> p g n", g=POOL_G)
            mixh = self.kt_view(sb("mixed_high", DK * SEQ, F32R))
            mixl = self.kt_view(sb("mixed_low", DK * SEQ, F32R))
            gqa_h, gqa_l, mla_h, mla_l = mixh[:, 0:4, :], mixl[:, 0:4, :], mixh[:, 4:8, :], mixl[:, 4:8, :]
            work = sb("head_work", 4 * PANEL)
            work = [work[:, i * PANEL:(i + 1) * PANEL] for i in range(4)] + [self.scr[:, 3 * PANEL:4 * PANEL]]
            tab = sb("rope_tables", 2 * 4 * TT * (ROPE + HD) // 2)
            tq, tk = tab[:, 0:128], tab[:, 128:256]
            tgq, tgk = tab[:, 256:512], tab[:, 512:768]
            pool_w = self.rows[:, 0:POOL_G * P].rearrange("p (g n) -> p g n", g=POOL_G)
            rows = self.rows[:, POOL_G * P:POOL_G * P + N_ROWS]

            self.fence()
            rows_loaded = self.small_load(f"rows_loaded_{l}", rows, self.dram["first_rows"][l].partition_broadcast(P))
            pool_w_loaded = self.small_load(f"pool_w_loaded_{l}", pool_w,
                                            self.dram["pool_w"][l].rearrange("p (g n) -> p g n", g=POOL_G))
            row = self.scale_row([self.r_ready])
            pads = [self.pool.run(g.memset, pp[:, :, a:a + POOL_PAD], 0.0) for a in (0, POOL_PAD + SEQ)]
            got = {}

            def scaled(out, part, done, extra=None):
                for t in range(TT):
                    e = self.act.run(s.activation, out[:, t], part[:, t], ACT.Copy, scale=r[t],
                                     after=[done, self.r_ready, extra])
                return e

            def take(panel, acc, w, done):
                a = acc.rearrange("p (t n) -> p t n", t=TT)
                if panel == 0:
                    got["c"] = scaled(c, a[:, :, 0:w], done)
                    norm = compressed_norm()
                    self.after_units(1, lambda: advance(norm))
                    self.after_units(2, lambda: advance(norm))
                    self.after_units(4, compressed_features)
                    return [got["c"]]
                if panel == 1:
                    got["gq"] = scaled(gqk[:, :, 0:GQA_H, :], a.rearrange("p t (h d) -> p t h d", d=HD), done)
                    return [got["gq"]]
                if panel == 2:
                    n_k = GQA_KV * HD
                    scaled(gqk[:, :, GQA_H:, :], a[:, :, 0:n_k].rearrange("p t (h d) -> p t h d", d=HD), done)
                    got["gqa"] = scaled(gv, a[:, :, n_k:2 * n_k], done)
                    heads = grouped_heads()
                    for i in range(6):
                        self.after_units((1, 4, 5, 6, 7, 8)[i], lambda: advance(heads))
                    return [got["gqa"]]
                got["pool"] = self.dve.run(v.tensor_tensor, pp[:, :, POOL_PAD:POOL_PAD + SEQ],
                                           acc.rearrange("p (g s) -> p g s", g=POOL_G),
                                           row.to_broadcast([P, POOL_G, SEQ]), ALU.mult, after=[done, pads, self.row_ready])
                self.after_units(1, window_sums)
                return [got["pool"]]

            n_n = Q_LORA + KV_LORA

            def tables():
                for tag, rot, at, out in (("m", ROPE, ROW_QM, tq), ("m", ROPE, ROW_KM, tk), ("g", HD, ROW_QG, tgq),
                                          ("g", HD, ROW_KG, tgk)):
                    self.rope_tables(tag, rot, rows[:, at[0]:at[1]], out, [rows_loaded])

            self.after_units(4, tables)

            def compressed_norm():
                sq = self.scr[:, 0:TT * n_n].rearrange("p (t n) -> p t n", t=TT)
                t1 = self.dve.run(v.tensor_tensor, sq, c[:, :, 0:n_n], c[:, :, 0:n_n], ALU.mult,
                                  after=[got["c"], self.dve.last()])
                st, rr = self.stat[:, 300:304], self.stat[:, 304:308]
                self.dve.run(v.tensor_reduce, st[:, 0:2], sq[:, :, 0:Q_LORA], AXIS_X, ALU.add, after=[t1])
                t2 = self.dve.run(v.tensor_reduce, st[:, 2:4], sq[:, :, Q_LORA:n_n], AXIS_X, ALU.add, after=[t1])
                self.pool.run(g.tensor_scalar, st[:, 0:2], st[:, 0:2], 1.0 / Q_LORA, EPS, ALU.mult, ALU.add, after=[t2])
                t3 = self.pool.run(g.tensor_scalar, st[:, 2:4], st[:, 2:4], 1.0 / KV_LORA, EPS, ALU.mult, ALU.add)
                t4 = self.pool.run(g.tensor_tensor, rr, st, self.half[:, 0:4], ALU.pow, after=[t3])
                yield
                for i, (c0, c1) in enumerate(((0, Q_LORA), (Q_LORA, n_n))):
                    rb = rr[:, 2 * i:2 * i + 2].rearrange("p (t o) -> p t o", o=1).to_broadcast([P, TT, c1 - c0])
                    t5 = self.dve.run(v.tensor_tensor, c[:, :, c0:c1], c[:, :, c0:c1], rb, ALU.mult, after=[t4])
                got["c_norm"] = t5

            def compressed_features():
                a, b = FIRST_COLS["q_lora_g"][0], FIRST_COLS["kv_lora_g"][1]
                gain = self.cols[:, l * N_FIRST_COLS + a:l * N_FIRST_COLS + b]
                got["lora"] = self.to_features(c, [0, 1, 2], [got["c_norm"]], gqa_h, gqa_l, gain, (6, 7))

            def window_sums():
                tmp = [tok[:, 512 + i * POOL_G * pw:512 + (i + 1) * POOL_G * pw].rearrange("p (g n) -> p g n", g=POOL_G)
                       for i in range(2)]
                t = self.pool.run(g.tensor_tensor, tmp[0][:, :, 1:pw], pp[:, :, 0:pw - 1], pp[:, :, 1:pw], ALU.add,
                                  after=[got["pool"]])
                sums = [tmp[0]]
                for n in range(1, POOL_G):
                    d = 2 ** (n - 1)
                    lo, hi = 2 * d, pw - 2 * d + 1
                    t = self.pool.run(g.tensor_tensor, tmp[n % 2][:, n:, lo:hi], sums[-1][:, n:, lo - d:hi - d],
                                      sums[-1][:, n:, lo + d:hi + d], ALU.add, after=[t])
                    sums.append(tmp[n % 2])
                edge = self.const("pool_edge").rearrange("p (g n) -> p g n", g=POOL_G)
                for n in range(POOL_G):
                    for at, c0 in ((POOL_PAD, 0), (SEQ, POOL_PAD)):
                        part = sums[n][:, n, at:at + POOL_PAD]
                        t = self.pool.run(g.tensor_tensor, part, part, edge[:, n, c0:c0 + POOL_PAD], ALU.mult, after=[t])
                for n, w in enumerate(POOL_WINDOWS):
                    part = pp[:, n, POOL_PAD:POOL_PAD + SEQ]
                    t1 = self.pool.run(g.tensor_scalar, sums[n][:, n, POOL_PAD:POOL_PAD + SEQ],
                                       sums[n][:, n, POOL_PAD:POOL_PAD + SEQ], 1.0 / w, None, ALU.mult, after=[t])
                    t = self.pool.run(g.tensor_tensor, part, sums[n][:, n, POOL_PAD:POOL_PAD + SEQ], part, ALU.subtract,
                                      after=[t1])
                got["mixed"] = t

            def grouped_heads():
                scale = self.head_scale(gqk, GQA_H + GQA_KV, HD, [got["gqa"], got["gq"]])
                next(scale)
                yield
                t = next(scale)
                yield
                kd = tok[:, 0:2 * TT * GQA_KV * HD].rearrange("p (t g u d) -> p t g u d", t=TT, g=GQA_KV, u=2)
                tk_ready = self.rotate(gqk[:, :, GQA_H:, :], GQA_KV, 0, HD, tgk, [t],
                                       outs=[kd[:, :, :, u, :] for u in range(2)])
                yield
                tq_ready = self.rotate(gqk[:, :, 0:GQA_H, :], GQA_H, 0, HD, tgq, [t])
                flat = gqk.rearrange("p t h d -> p t (h d)")
                yield
                b = self.transpose_pairs(lambda n, t: kd[:, t, n, :, :], GQA_KV, P, gh[:, 4:6, :], [tk_ready], banks=(4,))
                yield
                a = self.transpose_pairs(lambda n, t: flat[:, t, n * P:(n + 1) * P], GQA_H // 2, P, gh[:, 0:4, :],
                                         [tq_ready], banks=(4, 5))
                got["gqa_turned"] = [a, b]

            run_all(self.linear("proj", l, self.xh, self.xl, ready, lambda p: p == 3, take, (0, 1, 2)))

            def take_gates(first):
                def take(panel, acc, w, done):
                    part = gates[:, 4 * (panel + first):4 * (panel + first) + 4, :]
                    got["gates"] = self.dve.run(v.tensor_tensor, part, self.kt_view(acc), row.to_broadcast([P, 4, SEQ]),
                                                ALU.mult, after=[done, self.row_ready])
                    return [got["gates"]]
                return take

            run_all(self.linear("gates_early", l, self.xh, self.xl, ready, True, take_gates(0), (1,)))
            got["tokens_free"] = [self.pe.last(), got["mixed"]]

            mq_flat = mq.rearrange("p t h d -> p t (h d)")

            def take_q(panel, acc, w, done):
                a = acc.rearrange("p (t n) -> p t n", t=TT)[:, :, 0:w]
                got["mq"] = self.act.run(s.activation, mq_flat[:, :, panel * PANEL:panel * PANEL + w], a, ACT.Copy,
                                         after=[done, got["tokens_free"]])
                return [got["mq"]]

            def take_kv(panel, acc, w, done):
                hp = w // (NOPE + MLA_V)
                a = acc.rearrange("p (t h d) -> p t h d", t=TT, d=NOPE + MLA_V)
                hs = slice(panel * hp, (panel + 1) * hp)
                got["mk"] = self.act.run(s.activation, mk[:, :, hs, 0:NOPE], a[:, :, :, 0:NOPE], ACT.Copy,
                                         after=[done, got["tokens_free"]])
                got["mv"] = self.act.run(s.activation, mv[:, :, hs, :], a[:, :, :, NOPE:], ACT.Copy)
                return [got["mv"]]

            lora = got["lora"]
            run_all(self.linear("up_q", l, gqa_h, gqa_l, lora, False, take_q, (0, 1)))
            run_all(self.linear("up_kv", l, gqa_h[:, 2:3, :], gqa_l[:, 2:3, :], lora[2:], False, take_kv, (0, 1)))

            def mla_heads():
                kr = c[:, :, Q_LORA + KV_LORA:].rearrange("p t (o d) -> p t o d", o=1).to_broadcast([P, TT, MLA_H, ROPE])
                t = self.pool.run(g.tensor_copy, mk[:, :, :, NOPE:], kr, after=[got["tokens_free"]])
                scale_k = self.head_scale(mk, MLA_H, MLA_QK, [t, got["mk"]], 0, True)
                next(scale_k)
                yield
                scale_q = self.head_scale(mq, MLA_H, MLA_QK, [got["mq"]], 1, True)
                k_scaled = next(scale_k)
                next(scale_q)
                yield
                yield
                tk_ready = self.rotate(mk, MLA_H, NOPE, ROPE, tk, [k_scaled])
                q_scaled = next(scale_q)
                yield
                yield
                tq_ready = self.rotate(mq, MLA_H, NOPE, ROPE, tq, [q_scaled])
                a = self.transpose_pairs(lambda h, t: mk[:, t, h, :], MLA_H, MLA_QK, qk[:, MLA_H:, :], [tk_ready],
                                         cols("k_head_g"))
                yield
                b = self.transpose_pairs(lambda h, t: mq[:, t, h, :], MLA_H, MLA_QK, qk[:, 0:MLA_H, :], [tq_ready],
                                         cols("q_head_g"))
                got["mla_turned"] = [a, b]

            gqa_tokens, mla_tokens = [], []
            prepare = mla_heads()

            def heads():
                rep = GQA_H // GQA_KV
                for h in range(GQA_H):
                    half = slice(HD * (h % 2), HD * (h % 2) + HD)
                    yield self.head_attention(h, h, gh[half, h // 2, :], gh[half, 4 + h // rep, :],
                                              lambda kt, h=h: gv[:, kt, HD * (h // rep):HD * (h // rep) + HD],
                                              HD ** -0.5, gqa_h, gqa_l, work, [got["gqa_turned"], got["gqa"]], gqa_tokens)
                run_all(prepare)
                for h in range(MLA_H):
                    yield self.head_attention(GQA_H + h, h, qk[0:MLA_QK, h, :], qk[0:MLA_QK, MLA_H + h, :],
                                              lambda kt, h=h: mv[:, kt, h, :], MLA_QK ** -0.5, mla_h, mla_l, work,
                                              [got["mla_turned"], got["mv"]], mla_tokens)

            def rounds():
                for _ in pipelined(heads()):
                    advance(prepare)
                    yield

            interleave(rounds(), self.linear("gates", l, self.xh, self.xl, ready, True, take_gates(1), (0, 1)), 1)
            for b in (1, 0, 2):
                for i in range(2):
                    part = gates[:, b * DK + 4 * i:b * DK + 4 * i + 4, :]
                    got["gate", b, i] = self.act.run(s.activation, part, part, ACT.Sigmoid, after=[got["gates"]])

            merged, out_ready = {}, []

            def gated(b):
                def take(panel, acc, w, done):
                    for bank in range(2):
                        at = 4 * panel + 2 * bank
                        part, total = gates[:, b * DK + at:b * DK + at + 2, :], gates[:, DK + at:DK + at + 2, :]
                        read = self.dve.run(v.tensor_tensor, part, part, self.kt_view(acc)[:, 2 * bank:2 * bank + 2, :],
                                            ALU.mult, after=[done, got["gate", b, panel]])
                        t = read
                        if b != 1:
                            t = self.dve.run(v.tensor_tensor, total, total, part, ALU.add, after=[read, merged[at]])
                        merged[at] = t
                    if b == 0:
                        for at in (4 * panel, 4 * panel + 2):
                            kk, total = slice(at, at + 2), gates[:, DK + at:DK + at + 2, :]
                            a = self.act.run(s.activation, mixh[:, kk, :], total, ACT.Copy, after=[merged[at], self.pe.last()])
                            d = self.dve.run(v.tensor_tensor, mixl[:, kk, :], total, mixh[:, kk, :], ALU.subtract, after=[a])
                            out_ready.extend([d] * 2)
                    return [read]
                return take

            pool_h, pool_l, pool_ready = self.xh[:, 0:POOL_G, :], self.xl[:, 0:POOL_G, :], []
            for n in range(POOL_G):
                b = 4 + n
                done = self.pe.run(self.t.matmul, self.bank[b][:, 0:SEQ], pool_w[:, n, :],
                                   pp[:, n, POOL_PAD:POOL_PAD + SEQ], start=True, stop=True,
                                   after=[got["mixed"], pool_w_loaded, self.free.get(b)])
                self.free[b] = self.split_out(self.bank[b][:, 0:SEQ], n, pool_h, pool_l, done, cols("pool_scale")[:, n:n + 1])
                pool_ready.append(self.free[b][1])
            run_all(self.linear("branch_gqa", l, gqa_h, gqa_l, gqa_tokens, True, gated(1), (0, 1)))
            run_all(self.linear("branch_pool", l, pool_h, pool_l, pool_ready, True, gated(2), (2, 3)))
            run_all(self.linear("branch_mla", l, mla_h, mla_l, mla_tokens, True, gated(0), (0, 1)))
            ready = out_ready
            run_all(self.linear("out", l, mixh, mixl, ready, False, self.residual_add(cols("ffn_g"), scaled=True), (0, 1)))

    def first_ffn(self, l):
        v, s = self.v, self.s
        cols = lambda name: self.first_col(l, name)
        ready = self.features
        with ExitStack() as ctx:
            ah = self.kt_view(self.sb(f"ffn_high_{l}", FT * SEQ, F32R, ctx))
            al = self.kt_view(self.sb(f"ffn_low_{l}", FT * SEQ, F32R, ctx))
            self.fence()
            conv_w, conv_b = cols("conv_w"), cols("conv_b")
            acts, got = [], {}

            def take(panel, acc, w, done):
                pair, value = panel // 2, panel % 2
                buf = self.scr[:, (pair % 2) * 2 * UNIT:(pair % 2 + 1) * 2 * UNIT]
                o = self.kt_view(buf[:, value * UNIT:value * UNIT + w * TT])
                u = self.kt_view(acc)
                readers = []
                def tap(i, f):
                    ft = i * 2 * FT + value * FT + pair * (PANEL // P) + f
                    return conv_w[:, ft:ft + 1]
                for bank in range(w // (2 * P)):
                    fs = (2 * bank, 2 * bank + 1)
                    for f in fs:
                        ft = value * FT + pair * (PANEL // P) + f
                        a = self.act.run(s.activation, o[:, f, :], u[:, f, :], ACT.Identity, scale=tap(1, f),
                                         bias=conv_b[:, ft:ft + 1], after=[done, self.free.get(("conv", pair % 2))])
                    for f in fs:
                        d = self.dve.run(v.scalar_tensor_tensor, o[:, f, 1:], u[:, f, 0:SEQ - 1], tap(0, f),
                                         o[:, f, 1:], ALU.mult, ALU.add, after=[done, a])
                    for f in fs:
                        d = self.dve.run(v.scalar_tensor_tensor, o[:, f, 0:SEQ - 1], u[:, f, 1:], tap(2, f),
                                         o[:, f, 0:SEQ - 1], ALU.mult, ALU.add, after=[d])
                    readers += [a, d]
                n = w * TT
                gate, val = buf[:, 0:n], buf[:, UNIT:UNIT + n]

                def multiply():
                    a = self.act.run(s.activation, gate, gate, ACT.Silu, after=[d])
                    got[pair] = self.dve.run(v.tensor_tensor, gate, gate, val, ALU.mult, after=[a])

                def split():
                    ks = slice(pair * 4, pair * 4 + w // P)
                    a = self.act.run(s.activation, ah[:, ks, :], self.kt_view(gate), ACT.Copy, after=[got[pair]])
                    e = self.dve.run(v.tensor_tensor, al[:, ks, :], self.kt_view(gate), ah[:, ks, :], ALU.subtract, after=[a])
                    self.free[("conv", pair % 2)] = e
                    acts.extend([e] * (w // P))

                if value:
                    self.after_units(1, multiply)
                    self.after_units(2, split)
                return readers

            run_all(self.linear("ffn_up", l, self.xh, self.xl, ready, True, take, (0, 1, 2, 3)))
            gain = self.first_col(l + 1, "attn_g") if l + 1 < DEPTH else self.second_col(0, "mix_g")
            run_all(self.linear("ffn_down", l, ah, al, acts, False, self.residual_add(gain), (0, 1)))

    def post_norm(self, gain, banks):
        sums, r = self.stat[:, 8:12], self.stat[:, 12:14]
        held, squared = [], []

        def take(panel, acc, w, done):
            held.append(acc.rearrange("p (t n) -> p t n", t=TT))
            for t in range(TT):
                squared.append(self.act.run(self.s.activation, self.junk[t], held[-1][:, t, 0:w], ACT.Square,
                                            accum_out=sums[:, 2 * panel + t:2 * panel + t + 1],
                                            after=[done, self.free.get(("junk", t))]))
                self.free["junk", t] = squared[-1]
            return [squared[-1]]

        def finish(slots):
            ready = self.token_rstd(sums, r, squared)
            self.start_features()
            features = self.features
            y = self.scr[:, 0:TT * D].rearrange("p (t n) -> p t n", t=TT)

            def add(half, c0, c1):
                for t in range(TT):
                    d = self.dve.run(self.v.scalar_tensor_tensor, y[:, t, c0:c1],
                                     held[half][:, t, c0 - half * PANEL:c1 - half * PANEL], r[:, t:t + 1],
                                     self.rows[:, c0:c1], ALU.mult, ALU.mult, after=[ready, self.rows_ready, before])
                self.free[2 * slots[half]] = self.free[2 * slots[half] + 1] = [d]
                for t in range(TT):
                    d = self.dve.run(self.v.tensor_tensor, self.x[:, t, c0:c1], self.x[:, t, c0:c1], y[:, t, c0:c1],
                                     ALU.add, after=[d])
                return d

            high, low = self.xh, self.xl
            turn = lambda kts, d: features.extend(self.to_features(self.x, kts, [d], high, low, gain, banks))
            before = [self.dve.last(), self.act.last()]
            first = add(0, 0, 2 * P)
            second = add(0, 2 * P, PANEL)
            third = add(1, PANEL, D)
            yield
            turn([0, 1], first)
            turn([2, 3], second)
            self.after_units(2, lambda: turn([4, 5, 6, 7], third))
            self.act.wait([third])
            sums_x = self.stat[:, 0:4]
            squares = self.squares(self.x, 0, sums_x) + self.squares(self.x, 1, sums_x)
            self.r_ready = self.token_rstd(sums_x, self.stat[:, 4:6], squares)
            self.x_ready = third
        return take, finish

    def stick_breaking(self, l):
        v, s = self.v, self.s
        ready = self.features
        with ExitStack() as ctx:
            sb = lambda name, floats, dt=F32: self.sb(f"{name}_{l}", floats, dt, ctx)
            q, k = self.kt_view(sb("sb_q", DK * SEQ)), self.kt_view(sb("sb_k", DK * SEQ))
            val = sb("sb_v", TT * D).rearrange("p (t n) -> p t n", t=TT)
            oh, ol = self.kt_view(sb("sb_out_high", DK * SEQ, F32R)), self.kt_view(sb("sb_out_low", DK * SEQ, F32R))
            NZ = 3 * P
            masks = sb("sb_masks", 2 * NZ)
            weights = [sb(f"sb_weights{i}", 2 * NZ).rearrange("p (j n) -> p j n", j=2) for i in range(2)]
            part = lambda i: self.scr[:, i * 2 * NZ:(i + 1) * 2 * NZ].rearrange("p (j n) -> p j n", j=2)
            softs, fails = [part(i) for i in range(3)], [part(i) for i in range(3, 5)]
            self.fence()
            self.rows_ready = self.small_load(f"mix_gain_loaded_{l}", self.rows,
                                              self.dram["second_rows"][l, 0].partition_broadcast(P))
            at = CONSTS["sb_neg"][0]
            masks_loaded = self.small_load("sb_masks_loaded", masks, self.dram["consts"][:, at:at + 2 * NZ])
            row = self.scale_row([self.r_ready])
            r = [self.stat[:, 4 + t:5 + t] for t in range(TT)]
            got = {}

            def take(panel, acc, w, done):
                part = slice(4 * (panel % 2), 4 * (panel % 2) + 4)
                got["qk"] = self.dve.run(v.scalar_tensor_tensor, (q if panel < 2 else k)[:, part, :], self.kt_view(acc),
                                         HD ** -0.5 if panel < 2 else 1.0, row.to_broadcast([P, 4, SEQ]), ALU.mult,
                                         ALU.mult, after=[done, self.row_ready])
                return [got["qk"]]

            def take_v(panel, acc, w, done):
                c = panel * PANEL
                a = acc.rearrange("p (t n) -> p t n", t=TT)
                for t in range(TT):
                    got["v"] = self.act.run(s.activation, val[:, t, c:c + w], a[:, t], ACT.Copy, scale=r[t],
                                            after=[done, self.r_ready])
                return [got["v"]]

            run_all(self.linear("sb_in", l, self.xh, self.xl, ready, True, take, (0, 1, 2)))
            values = self.linear("sb_values", l, self.xh, self.xl, ready, False, take_v, (2,))
            self.act.run(s.preload_act_table_set, "natural_log_exp_and_others", signal=False)
            neg, add = (masks[:, i * NZ:(i + 1) * NZ].rearrange("p (o n) -> p o n", o=1).to_broadcast([P, 2, NZ])
                        for i in range(2))
            not_below, ones = self.const("not_below"), self.const("ones")
            tokens = []

            def pair(j):
                b, c = j % 2, j % 2
                for _ in range(2 if j < 2 else 1):
                    advance(values)
                z = self.slot[b].rearrange("p (j n) -> p j n", j=2)
                zs = z[:, :, 0:NZ]
                soft, fail, w = softs[b], fails[c], weights[c]
                self.pe.wait([self.free.get(2 * b), self.free.get(2 * b + 1)])
                for i in range(2):
                    rows = slice(HD * i, HD * i + HD)
                    self.pe.run(self.t.matmul, z[:, i, 0:SEQ], k[rows, j, 0:P], q[rows, j, :], start=True, stop=True,
                                after=[got["qk"]], signal=False, skip_group_check=True)
                    done = self.pe.run(self.t.matmul, z[:, i, SEQ:NZ], k[rows, j, P:SEQ], q[rows, j, P:SEQ],
                                       start=False, stop=True, skip_group_check=True)
                a = self.act.run(s.activation, soft, zs, ACT.Abs, after=[done, self.free.get(("soft", b))])
                a = self.act.run(s.activation, soft, soft, ACT.Exp, scale=-1.0, after=[a])
                a = self.act.run(s.activation, soft, soft, ACT.Ln, bias=1.0, after=[a])
                yield
                d = self.dve.run(v.scalar_tensor_tensor, fail, zs, 0.0, soft, ALU.max, ALU.add,
                                 after=[a, self.free.get(("fail", c))])
                d = self.dve.run(v.tensor_tensor, fail, fail, neg, ALU.mult, after=[d, masks_loaded])
                yield
                for i in range(2):
                    for o, m, r in ((z[:, i, 0:SEQ], not_below, fail[:, i, 0:SEQ]),
                                    (z[:, i, P:SEQ], ones, fail[:, i, SEQ:NZ]),
                                    (z[:, i, SEQ:NZ], not_below, fail[:, i, SEQ:NZ])):
                        done = self.pe.run(self.t.matmul, o, m, r, start=False, stop=True, after=[d],
                                           skip_group_check=True)
                self.free[("fail", c)] = done
                d = self.dve.run(v.scalar_tensor_tensor, soft, zs, 0.0, add, ALU.min, ALU.add, after=[done])
                a = self.act.run(s.activation, w, soft, ACT.Exp, after=[d, self.free.get(("weights", c))])
                self.free[2 * b] = self.free[2 * b + 1] = [d]
                self.free[("soft", b)] = a
                yield
                o_bank = self.bank[6 + c]
                self.pe.wait([self.free.get(6 + c)])
                for i in range(2):
                    h = 2 * j + i
                    o = o_bank[HD * i:HD * i + HD, :]
                    self.pe.run(self.t.matmul, o[:, 0:SEQ], val[:, 0, HD * h:HD * h + HD], w[:, i, 0:SEQ], start=True,
                                stop=True, after=[a, got["v"]], signal=False, skip_group_check=True)
                    done = self.pe.run(self.t.matmul, o[:, P:SEQ], val[:, 1, HD * h:HD * h + HD], w[:, i, SEQ:NZ],
                                       start=False, stop=True, skip_group_check=True)
                self.free[("weights", c)] = done
                self.free[6 + c] = self.split_out(o_bank[:, 0:SEQ], j, oh, ol, done)
                tokens.append(self.free[6 + c][1])

            run_all(pipelined(pair(j) for j in range(SB_H // 2)))
            take_y, finish = self.post_norm(self.second_col(l, "ffn_g"), (4, 5, 6, 7))
            run_all(self.linear("sb_out", l, oh, ol, tokens, False, take_y, (0, 1)))
            run_all(finish((0, 1)))

    def position_tables(self, pos, loaded, ang, out):
        v = self.v
        n = DIL_ROT // 2
        parts, rest = [], 2 * np.pi
        for bits in (8, 8, 8):
            e = 2.0 ** (bits - 1 - np.floor(np.log2(rest)))
            parts.append(float(np.floor(rest * e) / e))
            rest -= parts[-1]
        parts.append(float(np.float32(rest)))
        a0, turns, a1 = (ang[:, i * TT * n:(i + 1) * TT * n] for i in range(3))
        t3 = lambda ap: ap.rearrange("p (t n) -> p t n", t=TT)
        magic = 1.5 * 2.0 ** 23
        posf = ang[:, 3 * TT * n:3 * TT * n + TT]
        t = self.dve.run(v.tensor_copy, posf, pos, after=[loaded])
        t = self.dve.run(v.tensor_tensor, t3(a0), posf.rearrange("p (t o) -> p t o", o=1).to_broadcast([P, TT, n]),
                         self.const("inv_freq").rearrange("p (o n) -> p o n", o=1).to_broadcast([P, TT, n]),
                         ALU.mult, after=[t])
        t = self.dve.run(v.tensor_scalar, turns, a0, 1.0 / (2 * np.pi), magic, ALU.mult, ALU.add, after=[t])
        t = self.dve.run(v.tensor_scalar, turns, turns, magic, None, ALU.subtract, after=[t])
        for part in parts:
            t = self.dve.run(v.scalar_tensor_tensor, a0, turns, -part, a0, ALU.mult, ALU.add, after=[t])
        t = self.dve.run(v.tensor_scalar, a1, a0, np.pi / 2, None, ALU.add, after=[t])
        t = self.dve.run(v.tensor_scalar, turns, a1, np.pi, -2 * np.pi, ALU.is_gt, ALU.mult, after=[t])
        t = self.dve.run(v.tensor_tensor, a1, a1, turns, ALU.add, after=[t])
        for a in (a0, a1):
            t = self.dve.run(v.tensor_scalar, a, a, 3.1415925, -3.1415925, ALU.min, ALU.max, after=[t])
        c, sn = out[:, 0:TT * n], out[:, TT * n:2 * TT * n]
        a = self.act.run(self.s.activation, c, a1, ACT.Sin, after=[t])
        b = self.act.run(self.s.activation, sn, a0, ACT.Sin)
        self.dve.run(v.tensor_copy, out[:, 2 * TT * n:3 * TT * n], sn, after=[a, b])
        self.dil_tables_ready = self.dve.run(v.tensor_copy, out[:, 3 * TT * n:], c)

    def dilated(self, l):
        v, s = self.v, self.s
        ready = self.features
        G = len(DIL)
        with ExitStack() as ctx:
            sb = lambda name, floats, dt=F32: self.sb(f"{name}_{l}", floats, dt, ctx)
            tok = [sb(f"dil_tokens{i}", TT * DIL_W).rearrange("p (t h d) -> p t h d", t=TT, d=HD) for i in range(2)]
            qt = [self.kt_view(sb(f"dil_q{i}", 4 * SEQ)) for i in range(G)]
            kt_ = [self.kt_view(sb(f"dil_k{i}", 4 * SEQ)) for i in range(G)]
            val = [sb(f"dil_v{i}", TT * DIL_W).rearrange("p (t n) -> p t n", t=TT) for i in range(G)]
            oh, ol = self.kt_view(sb("dil_out_high", 4 * SEQ, F32R)), self.kt_view(sb("dil_out_low", 4 * SEQ, F32R))
            mask = sb("dil_masks", 9 * P)
            self.fence()
            self.rows_ready = self.small_load(f"mix_gain_loaded_{l}", self.rows,
                                              self.dram["second_rows"][l, 0].partition_broadcast(P))
            at = CONSTS["dil_add"][0]
            mask_loaded = self.small_load("dil_masks_loaded", mask, self.dram["consts"][:, at:at + 9 * P])
            r_ready = self.pool.run(self.g.tensor_scalar, self.stat[:, 6:8], self.stat[:, 4:6], HD ** -0.5, None,
                                    ALU.mult, after=[self.r_ready])
            tab, tables = self.dil_tables, self.dil_tables_ready
            got, late = {}, []

            def scaled(out, part, at, after):
                for t in range(TT):
                    e = self.act.run(s.activation, out[:, t], part[:, t], ACT.Copy,
                                     scale=self.stat[:, at + t:at + t + 1], after=[r_ready, after])
                return e

            def turn_late():
                if late:
                    n, out, t = late.pop()
                    flat = tok[n].rearrange("p t h d -> p t (h d)")
                    got["turned"] = self.transpose_pairs(lambda i, t: flat[:, t, i * P:(i + 1) * P], 4, P, out, [t],
                                                         banks=(6, 7))
                    self.free[("tok", n)] = self.pe.last()

            def take(panel, acc, w, done):
                g, what = panel // 3, panel % 3
                a = acc.rearrange("p (t n) -> p t n", t=TT)
                if what == 2:
                    got["v"] = scaled(val[g], a, 4, [done])
                    turn_late()
                    return [got["v"]]
                c = scaled(tok[what], a.rearrange("p t (h d) -> p t h d", d=HD), 4 if what else 6,
                           [done, self.free.get(("tok", what))])
                t = self.rotate(tok[what], DIL_H, 0, DIL_ROT, tab, [c, tables])
                turn_late()
                late.append((what, (qt, kt_)[what][g], t))
                return [c]

            run_all(self.linear("dil_in", 0, self.xh, self.xl, ready, False, take, (0, 1, 2)))
            turn_late()
            turned = [got["turned"], self.act.last(), self.dve.last(), mask_loaded]
            tokens = []
            wide = G * SEQ
            buffer = lambda i: self.scr[:, i * wide:(i + 1) * wide]

            def unit(m):
                h, t = m // TT, m % TT
                keys = (t + 1) * P
                n = G * keys
                b, c = m % 3, m % 2
                banks = (2 * (h % 2), 2 * (h % 2) + 1) if t else (4,)
                s_ps = (self.slot[h % 2] if t else self.bank[4])[:, 0:n]
                base = (0 if t == 0 else G * P)
                st = self.stat[:, 128 + 16 * b:136 + 16 * b]
                prob, probt = buffer(b)[:, 0:n], buffer(3 + c)[:, 0:n]
                half = slice(HD * (h % 2), HD * (h % 2) + HD)
                self.pe.wait([self.free.get(i) for i in banks])
                for g in range(G):
                    done = self.pe.run(self.t.matmul, s_ps[:, g * keys:(g + 1) * keys], qt[g][half, h // 2, t * P:(t + 1) * P],
                                       kt_[g][half, h // 2, 0:keys], start=True, stop=True, after=[turned],
                                       signal=g == G - 1)
                a = self.dve.run(v.tensor_tensor_reduce, prob, s_ps, mask[:, base:base + n], 1.0, MASKED, ALU.add,
                                 ALU.max, st[:, 0:1], after=[done, self.free.get(("prob", b)), self.free.get(("stat", b))])
                for i in banks:
                    self.free[i] = [a]
                a = self.dve.run(v.tensor_scalar, st[:, 1:2], st[:, 0:1], -1.0, None, ALU.mult, after=[a])
                e = self.act.run(s.activation, prob, prob, ACT.Exp, bias=st[:, 1:2], accum_out=st[:, 2:3], after=[a])
                yield
                a = self.dve.run(v.reciprocal, st[:, 3:4], st[:, 2:3], after=[e])
                p_ready = self.dve.run(v.tensor_scalar, prob, prob, st[:, 3:4], None, ALU.mult, after=[a])
                self.free[("stat", b)] = p_ready
                yield
                for i in range(n // P):
                    bank = 5 + i // 4
                    done = self.pe.run(self.t.transpose, self.bank[bank][:, (i % 4) * P:(i % 4 + 1) * P],
                                       prob[:, i * P:(i + 1) * P], self.const("ident"),
                                       after=[p_ready, self.free.get(bank)])
                self.free[("prob", b)] = done
                c1 = min(n, PANEL)
                e = self.act.run(s.activation, probt[:, 0:c1], self.bank[5][:, 0:c1], ACT.Copy,
                                 after=[done, self.free.get(("probt", c))])
                self.free[5] = [e]
                d = None
                if n > PANEL:
                    d = self.dve.run(v.tensor_copy, probt[:, c1:n], self.bank[6][:, 0:n - c1],
                                     after=[done, self.free.get(("probt", c))])
                    self.free[6] = [d]
                yield
                o = self.bank[7][half, t * P:(t + 1) * P]
                blocks = [(g, kt) for g in range(G) for kt in range(t + 1)]
                for i, (g, kt) in enumerate(blocks):
                    done = self.pe.run(self.t.matmul, o, val[g][:, kt, HD * h:HD * h + HD], probt[:, i * P:(i + 1) * P],
                                       start=i == 0, stop=i == len(blocks) - 1,
                                       after=[e, d, got["v"], self.free.get(7)], skip_group_check=True)
                self.free[("probt", c)] = done
                if t == TT - 1 and h % 2:
                    self.free[7] = self.split_out(self.bank[7][:, 0:SEQ], h // 2, oh, ol, done)
                    tokens.append(self.free[7][1])

            run_all(pipelined(unit(m) for m in range(DIL_H * TT)))
            take_y, finish = self.post_norm(self.second_col(l, "ffn_g"), (4, 5, 6, 7))
            run_all(self.linear("dil_out", 0, oh, ol, tokens, False, take_y, (0, 1)))
            run_all(finish((0, 1)))

    def second_ffn(self, l):
        v, s = self.v, self.s
        ready = self.features
        with ExitStack() as ctx:
            sb = lambda name, floats, dt=F32: self.sb(f"{name}_{l}", floats, dt, ctx)
            n_f = D_FF_2 // P
            ah, al = self.kt_view(sb("ff_high", n_f * SEQ, F32R)), self.kt_view(sb("ff_low", n_f * SEQ, F32R))
            emb = sb("ple_tokens", TT * PLE).rearrange("p (t n) -> p t n", t=TT)
            eh, el = self.kt_view(sb("ple_high", 2 * SEQ, F32R)), self.kt_view(sb("ple_low", 2 * SEQ, F32R))
            up = sb("ple_up", TT * D).rearrange("p (t n) -> p t n", t=TT)
            self.fence()
            self.rows_ready = self.small_load(f"ffn_gain_loaded_{l}", self.rows,
                                              self.dram["second_rows"][l, 1].partition_broadcast(P))
            emb_loaded = self.small_load(f"ple_loaded_{l}", emb, self.dram["ple"][l].rearrange("(t p) n -> p t n", p=P))
            row = self.scale_row([self.r_ready]).to_broadcast([P, 4, SEQ])
            acts = []

            def take(panel, acc, w, done):
                i = panel % 2
                a, sq = (self.scr[:, (2 * i + j) * UNIT:(2 * i + j + 1) * UNIT] for j in range(2))
                relu = self.dve.run(v.scalar_tensor_tensor, self.kt_view(a), self.kt_view(acc), 0.0, row, ALU.max,
                                    ALU.mult, after=[done, self.row_ready, self.free.get(("act", i))])
                t = self.act.run(s.activation, sq, a, ACT.Square, after=[relu, self.free.get(("act", i))])
                self.free[("act", i)] = t
                ks = slice(4 * panel, 4 * panel + 4)
                t = self.act.run(s.activation, ah[:, ks, :], self.kt_view(sq), ACT.Copy, after=[t])
                e = self.dve.run(v.tensor_tensor, al[:, ks, :], self.kt_view(sq), ah[:, ks, :], ALU.subtract, after=[t])
                self.free[("act", i)] = e
                acts.extend([e] * 4)
                return [relu]

            run_all(self.linear("ff_in", l, self.xh, self.xl, ready, True, take, (0, 1, 2, 3)))
            emb_ready = self.to_features(emb, [0, 1], [emb_loaded], eh, el)
            take_y, finish = self.post_norm(self.second_col(l, "ple_g"), (4, 5, 6, 7))
            run_all(self.linear("ff_out", l, ah, al, acts, False, take_y, (0, 1)))

            def take_up(panel, acc, w, done):
                t = self.act.run(s.activation, up[:, :, panel * PANEL:panel * PANEL + w],
                                 acc.rearrange("p (t n) -> p t n", t=TT), ACT.Copy, after=[done])
                return [t]

            steps = finish((0, 1))
            next(steps)
            run_all(self.linear("ple_up", l, eh, el, emb_ready, False, take_up, (2, 3)))
            run_all(steps)

            ready, high, low = self.features, self.xh, self.xl
            self.xh, self.xl, self.xh_next, self.xl_next = self.xh_next, self.xl_next, self.xh, self.xl
            r = [self.stat[:, 14 + t:15 + t] for t in range(TT)]
            r_kept = self.pool.run(self.g.tensor_copy, self.stat[:, 14:16], self.stat[:, 4:6], after=[self.r_ready, self.act.last()])
            self.start_features()

            def take_gate(panel, acc, w, done):
                c = slice(panel * PANEL, panel * PANEL + w)
                a = acc.rearrange("p (t n) -> p t n", t=TT)
                gate = self.scr[:, panel * UNIT:(panel + 1) * UNIT].rearrange("p (t n) -> p t n", t=TT)
                for t in range(TT):
                    e = self.act.run(s.activation, gate[:, t, :], a[:, t, :], ACT.Sigmoid, scale=r[t],
                                     after=[done, r_kept, self.dve.last()])
                    d = self.dve.run(v.tensor_tensor, gate[:, t, :], gate[:, t, :], up[:, t, c], ALU.mult, after=[e])
                    d = self.dve.run(v.tensor_tensor, self.x[:, t, c], self.x[:, t, c], gate[:, t, :], ALU.add, after=[d])
                self.x_ready = d
                if l + 1 < DEPTH:
                    step = lambda: self.half_done(panel, d, self.second_col(l + 1, "mix_g"), False, (4, 5, 6, 7))
                    if panel:
                        step()
                    else:
                        self.after_units(2, step)
                return [e]

            run_all(self.linear("ple_gate", l, high, low, ready, False, take_gate, (0, 1)))

    def build(self, stages=8):
        self.pool.run(self.g.memset, self.half, -0.5)
        src = self.dram["x"].rearrange("(t p) n -> p t n", p=P)
        x_load = lambda i: self.small_load(f"x_loaded{i}", self.x[:, :, i * PANEL:(i + 1) * PANEL],
                                           src[:, :, i * PANEL:(i + 1) * PANEL])
        n1, n2 = N_FIRST_COLS, DEPTH * N_FIRST_COLS
        on_act = lambda name, out, in_: self.act.load(self.nc.scalar.dma_start, out, in_, self.sem(name), 16)
        first = [on_act("first_cols_loaded0", self.cols[:, 0:n1], self.dram["first_cols"][0]),
                 on_act("consts_loaded", self.consts, self.dram["consts"][:, 0:N_HELD])]
        x_loaded = [x_load(0)]
        self.load_weights(0)
        x_loaded.append(x_load(1))
        self.n_loaded = 1
        for e in (self.pe, self.act, self.dve, self.pool):
            e.wait(first)
        self.start_features()
        for i in range(2):
            self.half_done(i, x_loaded[i], self.first_col(0, "attn_g"), False, (4, 5, 6, 7))
        self.x_ready = x_loaded
        rest = []

        def load_rest():
            for i in range(1, DEPTH):
                rest.append(self.small_load(f"first_cols_loaded{i}", self.cols[:, i * n1:(i + 1) * n1],
                                            self.dram["first_cols"][i]))
            rest.append(self.small_load("second_cols_loaded",
                                        self.cols[:, n2:].rearrange("p (l n) -> p l n", n=N_SECOND_COLS),
                                        self.dram["second_cols"].rearrange("l p n -> p l n")))

        self.after_units(20, load_rest)
        steps = [lambda: self.first_mixing(0), lambda: self.first_ffn(0), lambda: self.first_mixing(1),
                 lambda: self.first_ffn(1), lambda: self.stick_breaking(0), lambda: self.second_ffn(0),
                 lambda: self.dilated(1), lambda: self.second_ffn(1)]
        for n, step in enumerate(steps[:stages]):
            if n == 1:
                for e in (self.act, self.dve, self.pool):
                    e.wait(rest)
            if n == 2 * DEPTH:
                self.xh_next = self.kt_view(self.sb("x_high_next", DK * SEQ, F32R))
                self.xl_next = self.kt_view(self.sb("x_low_next", DK * SEQ, F32R))
                positions, angles = self.sb("positions", TT, I32), self.sb("angles", 64)
                self.dil_tables = self.sb("dil_tables", 4 * TT * DIL_ROT // 2)
                self.fence()
                loaded = self.small_load("positions_loaded", positions, self.dram["positions"])
                self.after_units(6, lambda: self.position_tables(positions, loaded, angles, self.dil_tables))
            step()
        stored = self.small_load("out_stored", self.out.rearrange("(t p) n -> p t n", p=P), self.x, after=[self.x_ready])
        self.sp.wait([stored])

        with self.nc.Block() as block:
            @block.sync
            def _(eng):
                self.sp.play(eng)

            @block.tensor
            def _(eng):
                self.pe.play(eng)

            @block.scalar
            def _(eng):
                self.act.play(eng)

            @block.vector
            def _(eng):
                self.dve.play(eng)

            @block.gpsimd
            def _(eng):
                self.pool.play(eng)


def run_all(gen):
    for _ in gen:
        pass


def pipelined(gens):
    active = []
    for gen in gens:
        active = [g for g in active if advance(g)]
        next(gen)
        active.append(gen)
        yield
    while active:
        active = [g for g in active if advance(g)]
        yield


def advance(gen):
    for _ in gen:
        return True
    return False


def interleave(front, back, per):
    for _ in front:
        for _ in range(per):
            advance(back)
    run_all(back)


KTS = {p[0]: p[3] // P for p in weight_plan()}



def pack(inputs):
    f = {k: np.asarray(v) for k, v in inputs.items()}
    units, loads, total = weight_units()
    flat = np.empty(total, np.float32)
    by_load = {}
    for u in units:
        by_load.setdefault(u["load"], []).append(u)
    for n, (at, size) in enumerate(loads):
        parts = []
        for u in by_load[n]:
            w = f[u["source"]][u["layer"]][u["k0"] * P:(u["k0"] + u["nk"]) * P, u["c0"]:u["c0"] + u["w"]]
            parts.append(w.reshape(u["nk"], P, u["w"]).transpose(1, 0, 2).reshape(P, -1))
        flat[at:at + P * size] = np.concatenate(parts, 1).reshape(-1)

    def col(a):
        return a.reshape(-1, P).T

    def head_col(g):
        return np.concatenate([g[:NOPE], np.ones(P - NOPE, np.float32)])[:, None]

    first_cols = np.stack([np.concatenate(
        [col(f["attn_norm_g"][l]), col(f["mla_q_norm_g"][l]), col(f["mla_kv_norm_g"][l]),
         head_col(f["mla_q_head_g"][l]), head_col(f["mla_k_head_g"][l]), col(f["pool_scale"][l]),
         col(f["ffn_norm_g"][l])] + [col(f["ffn_conv_w"][l, i]) for i in range(3)] + [col(f["ffn_conv_b"][l])], 1)
        for l in range(DEPTH)])
    first_rows = np.stack([np.concatenate(
        [f["mla_q_head_g"][l, NOPE:], f["mla_k_head_g"][l, NOPE:], f["gqa_q_head_g"][l], f["gqa_k_head_g"][l]])
        for l in range(DEPTH)])
    second_cols = np.stack([np.concatenate([col(f[n][l]) for n in ("g_mix_pre_2", "g_ffn_pre_2", "g_ple_2")], 1)
                            for l in range(DEPTH)])
    second_rows = np.stack([np.stack([f["g_mix_post_2"][l], f["g_ffn_post_2"][l]]) for l in range(DEPTH)])
    arrays = {
        "weights": flat, "x": f["x"][0], "first_cols": first_cols, "first_rows": first_rows,
        "pool_w": f["pool_w"].transpose(0, 2, 1, 3).reshape(DEPTH, P, POOL_G * P), "second_cols": second_cols,
        "second_rows": second_rows, "ple": f["p_2"][:, 0], "positions": f["positions_2"].reshape(TT, P).T,
        "consts": constants(),
    }
    return {k: np.ascontiguousarray(v) for k, v in arrays.items()}


def kernel(**inputs):
    import concourse.bacc as bacc
    from concourse.bass_utils import run_bass_kernel_spmd

    nc = bacc.Bacc("TRN2", target_bir_lowering=False, num_devices=1, dynamic_dma_scratch_size=1024)
    arrays = pack(inputs)
    dram = {n: nc.dram_tensor("in_" + n, a.shape, mybir.dt.from_np(a.dtype), kind="ExternalInput").ap()
            for n, a in arrays.items()}
    out = nc.dram_tensor("out", (SEQ, D), F32, kind="ExternalOutput").ap()
    with ExitStack() as ctx:
        Program(nc, ctx, dram, out).build()
    got = run_bass_kernel_spmd(nc, [{"in_" + n: a for n, a in arrays.items()}], core_ids=[0]).results[0]["out"]
    return np.asarray(got).reshape(1, SEQ, D)
```
